# Optimizing a Trainium2 kernel written in Bass

```python
import math
import jax, jax.numpy as jnp
from jax import lax
import numpy as np

D_MODEL = 1024
BATCH = 1
SEQ = 512
DEPTH = 1

SSM_CH = 16
D_SSM = 512
SSM_GROUPS = D_SSM // SSM_CH
SSM_STATE = 64
N_HEADS = 8
HEAD_DIM = 64
D_ATTN = N_HEADS * HEAD_DIM
D_MIX = D_SSM + D_ATTN
IDX_HEADS = 8
IDX_DIM = 64
TOPK_MAX = 256
Q_BLOCK = 128
D_FF = 2816
CONV_W = 3
ROPE_THETA = 10000.0
EPS = 1e-6
D_IN_PROJ = D_SSM + 3 * D_ATTN + IDX_HEADS * IDX_DIM + IDX_DIM + IDX_HEADS

kernel_name = "hymba_s5_dsa_convffn_adaln"

def _rmsnorm(x, g):
    xf = x.astype(jnp.float32)
    return xf * lax.rsqrt(jnp.mean(xf * xf, axis=-1, keepdims=True) + EPS) * g.astype(jnp.float32)

def _modulate(xn, shift, scale):
    return xn * (1.0 + scale[:, None, :].astype(jnp.float32)) + shift[:, None, :].astype(jnp.float32)

def _rope(x, pos):
    d = x.shape[-1]
    inv = ROPE_THETA ** (-jnp.arange(0, d, 2, dtype=jnp.float32) / d)
    ang = pos.astype(jnp.float32)[..., None] * inv
    cos = jnp.cos(ang)[:, :, None, :]
    sin = jnp.sin(ang)[:, :, None, :]
    xf = x.astype(jnp.float32)
    x1, x2 = xf[..., : d // 2], xf[..., d // 2:]
    return jnp.concatenate([x1 * cos - x2 * sin, x1 * sin + x2 * cos], axis=-1)

def _s5_mixer(u, log_dt, a_re, a_im, b_re, b_im, c_re, c_im, d_skip, w_glu, b_glu):
    bsz, L, _ = u.shape
    uf = u.astype(jnp.float32).reshape(bsz, L, SSM_GROUPS, SSM_CH)
    dt = jnp.exp(log_dt.astype(jnp.float32))[:, None]
    lr = a_re.astype(jnp.float32)
    li = a_im.astype(jnp.float32)
    mag = jnp.exp(lr * dt)
    lb_re = mag * jnp.cos(li * dt)
    lb_im = mag * jnp.sin(li * dt)
    den = lr * lr + li * li
    nr, ni = lb_re - 1.0, lb_im
    coef_re = (nr * lr + ni * li) / den
    coef_im = (ni * lr - nr * li) / den
    br = b_re.astype(jnp.float32)
    bi = b_im.astype(jnp.float32)
    bb_re = coef_re[..., None] * br - coef_im[..., None] * bi
    bb_im = coef_re[..., None] * bi + coef_im[..., None] * br
    bu_re = jnp.einsum('blgc,gpc->blgp', uf, bb_re)
    bu_im = jnp.einsum('blgc,gpc->blgp', uf, bb_im)
    a_re_t = jnp.broadcast_to(lb_re, bu_re.shape)
    a_im_t = jnp.broadcast_to(lb_im, bu_im.shape)

    def combine(e1, e2):
        a1r, a1i, b1r, b1i = e1
        a2r, a2i, b2r, b2i = e2
        return (a2r * a1r - a2i * a1i,
                a2r * a1i + a2i * a1r,
                a2r * b1r - a2i * b1i + b2r,
                a2r * b1i + a2i * b1r + b2i)

    _, _, xr, xi = lax.associative_scan(combine, (a_re_t, a_im_t, bu_re, bu_im), axis=1)
    y = (jnp.einsum('blgp,gcp->blgc', xr, c_re.astype(jnp.float32))
         - jnp.einsum('blgp,gcp->blgc', xi, c_im.astype(jnp.float32))
         + d_skip.astype(jnp.float32).reshape(SSM_GROUPS, SSM_CH) * uf)
    y = jax.nn.gelu(y.reshape(bsz, L, D_SSM))
    return y * jax.nn.sigmoid(y @ w_glu.astype(jnp.float32) + b_glu.astype(jnp.float32))

def _dsa_mixer(q, k, v, qi, ki, wi):
    bsz, L = q.shape[0], q.shape[1]
    topk = min(TOPK_MAX, L // 4)
    nblk = L // Q_BLOCK
    scale = 1.0 / math.sqrt(HEAD_DIM)
    key_pos = jnp.arange(L, dtype=jnp.int32)

    def to_blocks(t):
        t = t.reshape((bsz, nblk, Q_BLOCK) + t.shape[2:])
        return jnp.moveaxis(t, 1, 0)

    def one_block(args):
        qb, qib, wib, start = args
        qpos = start + jnp.arange(Q_BLOCK, dtype=jnp.int32)
        s_h = jnp.einsum('bthd,bsd->bths', qib, ki)
        s_idx = jnp.einsum('bths,bth->bts', jax.nn.relu(s_h), wib)
        causal = key_pos[None, :] <= qpos[:, None]
        s_idx = jnp.where(causal[None], s_idx, -jnp.inf)
        _, sel = lax.top_k(s_idx, topk)
        valid = sel <= qpos[None, :, None]
        kg = jax.vmap(lambda kk, ii: kk[ii])(k, sel)
        vg = jax.vmap(lambda vv, ii: vv[ii])(v, sel)
        logits = jnp.einsum('bthd,btkhd->bhtk', qb, kg) * scale
        logits = jnp.where(valid[:, None], logits, -jnp.inf)
        p = jax.nn.softmax(logits, axis=-1)
        return jnp.einsum('bhtk,btkhd->bthd', p, vg.astype(jnp.float32))

    starts = jnp.arange(nblk, dtype=jnp.int32) * Q_BLOCK
    out = lax.map(one_block, (to_blocks(q), to_blocks(qi), to_blocks(wi), starts))
    out = jnp.moveaxis(out, 0, 1)
    return out.reshape(bsz, L, D_ATTN)

def _causal_dwconv(h, w, b):
    L = h.shape[1]
    hp = jnp.pad(h, ((0, 0), (CONV_W - 1, 0), (0, 0)))
    out = b.astype(jnp.float32)
    for j in range(CONV_W):
        out = out + w[j].astype(jnp.float32) * hp[:, j:j + L, :]
    return out

def setup_inputs(seed: int = 0) -> dict:
    key = jax.random.key(seed)
    ks = jax.random.split(key, 32)
    f32 = jnp.float32
    nrm = lambda k, shape, s: (jax.random.normal(k, shape, f32) * s)
    Dp = DEPTH
    x = jax.random.normal(ks[0], (BATCH, SEQ, D_MODEL), f32)
    c = jax.random.normal(ks[1], (BATCH, D_MODEL), f32)
    positions = jnp.broadcast_to(jnp.arange(SEQ, dtype=jnp.int32), (BATCH, SEQ))
    w_ada = nrm(ks[2], (Dp, D_MODEL, 6 * D_MODEL), 0.5 * D_MODEL ** -0.5)
    b_ada = nrm(ks[3], (Dp, 6 * D_MODEL), 0.02)
    norm_mix = 1.0 + nrm(ks[4], (Dp, D_MODEL), 0.02)
    w_in = nrm(ks[5], (Dp, D_MODEL, D_IN_PROJ), D_MODEL ** -0.5)
    ssm_log_dt = jax.random.uniform(ks[6], (Dp, SSM_GROUPS), f32, math.log(1e-3), math.log(1e-1))
    ssm_a_re = -0.5 + nrm(ks[7], (Dp, SSM_GROUPS, SSM_STATE), 0.01)
    ssm_a_im = (math.pi * jnp.arange(SSM_STATE, dtype=f32))[None, None, :] + nrm(ks[8], (Dp, SSM_GROUPS, SSM_STATE), 0.01)
    ssm_b_re = nrm(ks[9], (Dp, SSM_GROUPS, SSM_STATE, SSM_CH), (2 * SSM_CH) ** -0.5)
    ssm_b_im = nrm(ks[10], (Dp, SSM_GROUPS, SSM_STATE, SSM_CH), (2 * SSM_CH) ** -0.5)
    ssm_c_re = nrm(ks[11], (Dp, SSM_GROUPS, SSM_CH, SSM_STATE), (2 * SSM_STATE) ** -0.5)
    ssm_c_im = nrm(ks[12], (Dp, SSM_GROUPS, SSM_CH, SSM_STATE), (2 * SSM_STATE) ** -0.5)
    ssm_d = nrm(ks[13], (Dp, D_SSM), 1.0)
    ssm_w_glu = nrm(ks[14], (Dp, D_SSM, D_SSM), D_SSM ** -0.5)
    ssm_b_glu = nrm(ks[15], (Dp, D_SSM), 0.01)
    q_norm = 1.0 + nrm(ks[16], (Dp, HEAD_DIM), 0.02)
    k_norm = 1.0 + nrm(ks[17], (Dp, HEAD_DIM), 0.02)
    out_norm_ssm = 1.0 + nrm(ks[18], (Dp, D_SSM), 0.02)
    out_norm_attn = 1.0 + nrm(ks[19], (Dp, D_ATTN), 0.02)
    w_out = nrm(ks[20], (Dp, D_MIX, D_MODEL), D_MIX ** -0.5)
    norm_ffn = 1.0 + nrm(ks[21], (Dp, D_MODEL), 0.02)
    w_up = nrm(ks[22], (Dp, D_MODEL, 2 * D_FF), D_MODEL ** -0.5)
    conv_w = nrm(ks[23], (Dp, CONV_W, 2 * D_FF), CONV_W ** -0.5)
    conv_b = nrm(ks[24], (Dp, 2 * D_FF), 0.01)
    w_down = nrm(ks[25], (Dp, D_FF, D_MODEL), D_FF ** -0.5)
    return {"x": x, "c": c, "positions": positions, "w_ada": w_ada, "b_ada": b_ada,
            "norm_mix": norm_mix, "w_in": w_in, "ssm_log_dt": ssm_log_dt,
            "ssm_a_re": ssm_a_re, "ssm_a_im": ssm_a_im, "ssm_b_re": ssm_b_re,
            "ssm_b_im": ssm_b_im, "ssm_c_re": ssm_c_re, "ssm_c_im": ssm_c_im,
            "ssm_d": ssm_d, "ssm_w_glu": ssm_w_glu, "ssm_b_glu": ssm_b_glu,
            "q_norm": q_norm, "k_norm": k_norm, "out_norm_ssm": out_norm_ssm,
            "out_norm_attn": out_norm_attn, "w_out": w_out, "norm_ffn": norm_ffn,
            "w_up": w_up, "conv_w": conv_w, "conv_b": conv_b, "w_down": w_down}

def reference(x, c, positions, w_ada, b_ada, norm_mix, w_in, ssm_log_dt, ssm_a_re, ssm_a_im,
              ssm_b_re, ssm_b_im, ssm_c_re, ssm_c_im, ssm_d, ssm_w_glu, ssm_b_glu,
              q_norm, k_norm, out_norm_ssm, out_norm_attn, w_out, norm_ffn, w_up,
              conv_w, conv_b, w_down):
    bsz, L, _ = x.shape
    h = x.astype(jnp.float32)
    cs = jax.nn.silu(c.astype(jnp.float32))
    for l in range(DEPTH):
        mod = cs @ w_ada[l].astype(jnp.float32) + b_ada[l].astype(jnp.float32)
        sh1, sc1, g1, sh2, sc2, g2 = jnp.split(mod, 6, axis=-1)

        hn = _modulate(_rmsnorm(h, norm_mix[l]), sh1, sc1)
        proj = hn @ w_in[l].astype(jnp.float32)
        o = 0
        u = proj[..., o:o + D_SSM]; o += D_SSM
        q = proj[..., o:o + D_ATTN].reshape(bsz, L, N_HEADS, HEAD_DIM); o += D_ATTN
        k = proj[..., o:o + D_ATTN].reshape(bsz, L, N_HEADS, HEAD_DIM); o += D_ATTN
        v = proj[..., o:o + D_ATTN].reshape(bsz, L, N_HEADS, HEAD_DIM); o += D_ATTN
        qi = proj[..., o:o + IDX_HEADS * IDX_DIM].reshape(bsz, L, IDX_HEADS, IDX_DIM); o += IDX_HEADS * IDX_DIM
        ki = proj[..., o:o + IDX_DIM]; o += IDX_DIM
        wi = proj[..., o:o + IDX_HEADS] * (IDX_HEADS ** -0.5 * IDX_DIM ** -0.5)

        y_ssm = _s5_mixer(u, ssm_log_dt[l], ssm_a_re[l], ssm_a_im[l], ssm_b_re[l], ssm_b_im[l],
                          ssm_c_re[l], ssm_c_im[l], ssm_d[l], ssm_w_glu[l], ssm_b_glu[l])

        qr = _rope(_rmsnorm(q, q_norm[l]), positions)
        kr = _rope(_rmsnorm(k, k_norm[l]), positions)
        qir = _rope(qi, positions)
        kir = _rope(ki[:, :, None, :], positions)[:, :, 0, :]
        y_attn = _dsa_mixer(qr, kr, v, qir, kir, wi)

        y_mix = jnp.concatenate([_rmsnorm(y_ssm, out_norm_ssm[l]),
                                 _rmsnorm(y_attn, out_norm_attn[l])], axis=-1)
        h = h + g1[:, None, :] * (y_mix @ w_out[l].astype(jnp.float32))

        hn2 = _modulate(_rmsnorm(h, norm_ffn[l]), sh2, sc2)
        up = _causal_dwconv(hn2 @ w_up[l].astype(jnp.float32), conv_w[l], conv_b[l])
        gate, val = up[..., :D_FF], up[..., D_FF:]
        h = h + g2[:, None, :] * ((jax.nn.gelu(gate) * val) @ w_down[l].astype(jnp.float32))
    return h.astype(x.dtype)


_drawn_inputs = setup_inputs


def setup_inputs(seed=0):
    import zlib

    import numpy as np

    out = dict(_drawn_inputs(seed))
    spreads = {}
    factors = {'norm_mix': 4.404,
     'ssm_log_dt': 34.856,
     'ssm_a_re': 64.0,
     'ssm_a_im': 28.48,
     'ssm_b_re': 45.456,
     'ssm_b_im': 41.576,
     'ssm_c_re': 43.912,
     'ssm_c_im': 40.712,
     'ssm_b_glu': 26.691,
     'q_norm': 8.0,
     'k_norm': 8.0,
     'out_norm_ssm': 25.488,
     'out_norm_attn': 25.868,
     'norm_ffn': 8.0,
     'conv_b': 32.126}
    for name, (base, spread) in spreads.items():
        noise = np.random.default_rng([zlib.crc32(name.encode()), seed]).standard_normal(out[name].shape)
        drawn = base * np.exp(spread * noise) if base else spread * noise
        out[name] = __import__('jax').numpy.asarray(drawn.astype(out[name].dtype))
    for name, factor in factors.items():
        out[name] = (out[name] * factor).astype(out[name].dtype)
    return out
```

```python
import math
from contextlib import ExitStack

import numpy as np
import concourse.bass as bass
from concourse import mybir

F32 = mybir.dt.float32
F32R = mybir.dt.float32r
I32 = mybir.dt.int32
ALU = mybir.AluOpType
ACT = mybir.ActivationFunctionType
AX = mybir.AxisListType.X

P = 128
SEQ, D_MODEL = 512, 1024
TT, KD = SEQ // P, D_MODEL // P
HEADS, HD = 8, 64
HALF = HD // 2
CH, GROUPS, STATE = 16, 32, 64
GP = GROUPS // 2
GH = GP // 2
NG = 2 * GH
CHUNK = 8
NCH = SEQ // CHUNK
TOPK = min(256, SEQ // 4)
D_FF, CONV_W = 2816, 3
FT = D_FF // P
UPS = FT // 2
EPS = 1e-6
ARENA = 26024
UNIT = 2048
TAIL = HD + HEADS
ATT_SCALE = 1.0 / math.sqrt(HD)
WI_SCALE = HEADS ** -0.5 * HD ** -0.5
MAGIC = 12582912.0
RSQRT_GUESS = 1597463007.0
TAKEN = -3.4028234663852886e38
FUTURE = -3.0e38
MASK = -1.0e30


def parts(x, bits, n):
    out = []
    for _ in range(n - 1):
        e = math.frexp(x)[1] - bits
        out.append(math.ldexp(float(round(math.ldexp(x, -e))), e))
        x -= out[-1]
    return out + [float(np.float32(x))]


TWO_PI = parts(2 * math.pi, 8, 4)
LN2 = parts(math.log(2.0), 12, 2)

U_TAIL, U_QI, U_U, U_K, U_Q, U_V, U_GLU, U_OUT = 0, 1, 3, 5, 7, 9, 11, 12
U_UP = U_OUT + 4
U_DOWN = U_UP + 2 * UPS
UNITS = U_DOWN + FT // 2
COLS = {U_U: 0, U_Q: 512, U_K: 1024, U_V: 1536, U_QI: 2048}


def layer(nc, x, c, positions, w_ada, b_ada, norm_mix, w_in, ssm_log_dt, ssm_a_re, ssm_a_im, ssm_b_re,
          ssm_b_im, ssm_c_re, ssm_c_im, ssm_d, ssm_w_glu, ssm_b_glu, q_norm, k_norm, out_norm_ssm,
          out_norm_attn, w_out, norm_ffn, w_up, conv_w, conv_b, w_down, inv_freq, out):
    u_dram = nc.dram_tensor("u_dram", (SEQ, 512), F32, kind="Internal").ap()
    y_dram = nc.dram_tensor("y_dram", (SEQ, 512), F32, kind="Internal").ap()
    lag_dram = nc.dram_tensor("lag_dram", (CH, GROUPS, 2 * CHUNK - 1, CH), F32, kind="Internal").ap()

    with ExitStack() as ctx:
        def sb(name, shape, dt=F32, stack=ctx):
            return stack.enter_context(nc.sbuf_tensor(name, shape, dt))

        def sem(name):
            return ctx.enter_context(nc.semaphore(name))

        bank = [ctx.enter_context(nc.psum_tensor(f"bank{i}", [P, 512], F32)) for i in range(8)]

        xh = sb("xh", [P, TT, D_MODEL])
        w_raw = sb("w_raw", [P, 2, UNIT])
        w_hi = sb("w_hi", [P, 2, UNIT], F32R)
        w_lo = sb("w_lo", [P, 2, UNIT], F32R)
        ident = sb("ident", [P, P])
        ones = sb("ones", [P, P])
        vec_cols = sb("vec_cols", [P, 296])
        c_col = sb("c_col", [P, 3, KD])
        mod_cols = sb("mod_cols", [P, 6, KD])
        silu_c = c_col[:, 1, :]
        scale1, shift1, scale2, shift2, gate2 = (mod_cols[:, i, :] for i in range(5))
        wi = sb("wi", [P, TT, HEADS])
        stat = sb("stat", [P, 640])
        up32 = sb("up32", [P, 2, 512])

        act_in = ExitStack()
        act_hi = sb("act_hi", [P, KD, SEQ], F32R, act_in)
        act_lo = sb("act_lo", [P, KD, SEQ], F32R, act_in)
        act_in.close()
        s5_mem = sb("s5_mem", [P, 8192])

        mixer = ExitStack()
        arena = sb("arena", [P, ARENA], stack=mixer)

        def cut(a, *shape):
            n = math.prod(shape)
            assert a + n <= ARENA
            v = arena[:, a:a + n]
            names = "abcd"[:len(shape)]
            if len(shape) == 1:
                return v
            return v.rearrange(f"p ({' '.join(names)}) -> p {' '.join(names)}",
                               **{k: s for k, s in zip(names, shape)})

        KEYS = [P * (t + 1) for t in range(TT)]
        KEYS_AT = [sum(KEYS[:t]) for t in range(TT)]
        q_t, k_t = cut(0, 4, SEQ), cut(2048, 4, SEQ)
        v_tok = cut(4096, TT, 512)
        y_attn, y_ssm = cut(6144, TT, 512), cut(8192, TT, 512)
        qi_t, ki_t = cut(10240, 4, SEQ), cut(12288, SEQ)
        pre, rot = cut(12800, TT, 512), cut(14848, TT, 512)
        tmp = cut(16896, 512)
        relu = cut(17408, 2, 512)
        ada_acc = cut(18432, 1024)
        score = [cut(19880 + KEYS_AT[t], KEYS[t]) for t in range(TT)]
        bias = [cut(21160 + KEYS_AT[t], KEYS[t]) for t in range(TT)]
        rope = cut(22440, 6, TT, HD)
        g1_row = cut(23976, D_MODEL)
        vec_rows = cut(18432, 4, P)
        ki_w = cut(19456, TT, TAIL)
        b_g1_row = cut(0, D_MODEL)[0:1]
        d_bc = cut(25000, 512)[0:CH]
        b_glu_row = cut(25512, 512)[0:1]
        square_at = [up32[:].rearrange("p a n -> p (a n)"), cut(18944, D_MODEL)]
        ada_first = cut(0, 4, KD, 512)
        ada_first_acc = cut(16384, 2048)
        ada_next = [cut(6144, KD, 256), cut(8192, KD, 256)]
        logit = cut(10240, 8, 512)
        prob, prob_t = cut(14336, 2, 512), cut(15360, 2, 512)
        lag_w = cut(16384, 2, GH, CHUNK + 1, CH)
        turn = cut(18688, 2, GH, NCH)
        s5_b, s5_c = cut(19712, 2, GP, CH), cut(20224, 2, GP, CH)
        power = cut(20736, 2, CHUNK + 1, GP)
        s5_bb = cut(22440, 2, GP, CH)
        s5_p = cut(22952, 24, GP)
        scan_r = cut(23336, GH, NCH)
        s5_v = s5_mem[:, 0:2048].rearrange("p (g r n) -> p g r n", g=GH, r=2)
        s5_vt = s5_mem[:, 2048:4096].rearrange("p (r g j h) -> p r g j h", r=2, g=GH, j=CHUNK)
        s5_m = s5_mem[:, 2048:4096].rearrange("p (g n) -> p g n", g=NG)
        s5_u = s5_mem[:, 4096:5120].rearrange("p (g n) -> p g n", g=NG)
        s5_z = s5_mem[:, 5120:6144].rearrange("p (r n) -> p r n", r=2)
        lags = s5_mem[0:CH, 4096:6144].rearrange("p (g l h) -> p g l h", g=NG, l=CHUNK)
        def lags_of(i):
            return lags.rearrange("p (b c q) l h -> p b q c l h", b=2, q=2)[:, i // 2, i % 2]
        c_rows = s5_mem[:, 4096:5120].rearrange("p (r a q n) -> p r a q n", r=2, a=4, q=2)
        s5_x = s5_mem[:, 6144:7168].rearrange("p (r g n) -> p r g n", r=2, g=GH)
        s5_t = s5_mem[:, 7168:8192].rearrange("p (r n) -> p r n", r=2)
        chunk_rows = xh[0:NCH, :, :].rearrange("c a n -> c (a n)")
        chunk_in = chunk_rows.rearrange("c (i n) -> c i n", i=CHUNK)
        group_in = xh[NCH:2 * NCH, :, :].rearrange("c a n -> c (a n)").rearrange("c (g m) -> c g m", g=GROUPS)
        hn_tok = cut(0, TT, D_MODEL)
        mixer.close()

        ff_hi = sb("ff_hi", [P, FT, SEQ], F32R)
        ff_lo = sb("ff_lo", [P, FT, SEQ], F32R)
        conv = sb("conv", [P, 4, SEQ])

        ss_x, rstd_x = stat[:, 0:4], stat[:, 4:8]
        ss_qk, rstd_qk = stat[:, 8:72], stat[:, 72:136]
        top8 = stat[:, 136:144]
        neg_max = stat[:, 144:176]
        psum_p = stat[:, 176:208]
        q_scale = stat[:, 208:240]
        ss_y, rstd_y = stat[:, 240:248], stat[:, 248:256]
        work = stat[:, 256:384]
        ss_h, rstd_h = stat[:, 384:388], stat[:, 388:392]
        rinv = stat[:, 392:424]
        pos_f = stat[:, 424:428]
        pos_i = stat[:, 428:432].bitcast(I32)
        inv_bc = stat[:, 432:464]
        gq_bc, gk_bc = stat[:, 464:528], stat[:, 528:592]
        dt_rows = stat[:, 592:594]

        C_BADA, C_NMIX, C_NFFN, C_NSSM, C_NATT, C_W0, C_W1, C_W2, C_CB, C_ARE, C_AIM, C_LDT = (
            0, 48, 56, 64, 68, 72, 116, 160, 204, 248, 264, 280)

        S = {n: sem(n) for n in (
            "ident_ready", "ones_ready", "rows_loaded", "dt_spread", "vec_t", "c_loaded", "pos_loaded",
            "bc_loaded", "x_loaded", "ss_x_ready", "rstd_x_ready", "xn_ready", "tanh_c", "angle_ready", "sin_ready",
            "ada_first_loaded0", "ada_first_loaded1", "ada_first_loaded2", "ada_first_loaded3",
            "ada_acc_ready", "mod_ready", "mod1_ready", "x_t_ready", "x_t_read", "act_in_ready",
            "raw_loaded0", "raw_loaded1", "hi_ready", "lo_ready", "weights_used",
            "proj_ready", "proj_read", "rot_ready", "turned_ready", "turned_read", "u_stored",
            "ada_next_loaded0", "ada_next_loaded1", "ada_used", "ada_sum_ready", "ada_sum_read",
            "ss_qk_ready", "sq_used", "score_mm", "relu_ready", "relu_used", "future_set",
            "bias_ready", "logit_mm", "logit_ready", "prob_ready", "prob_turned", "prob_t_ready", "pv_done",
            "pv_read", "y_attn_ready", "u_loaded", "u_grouped", "s5_loaded", "c_t", "c_t_read", "s5_angle", "s5_sin",
            "vt_ready", "v_t", "v_ready", "lag_mm", "lags_ready", "lags_stored", "zeros_stored", "m_loaded",
            "zero_ready", "lag_d_added", "u_t", "u_t_read", "state_mm", "state_read", "s5_state", "y_mm", "y_read", "y_stored",
            "y_loaded", "gelu_ready", "g_t", "g_t_read", "glu_in", "glu_mm", "tanh_z", "glu_read", "y_ssm_ready",
            "ss_y_ready", "yn_ready", "mix_t", "mix_t_read", "mix_in", "out_mm", "h_ready", "ss_h_ready",
            "hn_ready", "h_t", "h_t_read", "mlp_in", "up_mm", "tap_ready", "conv_read", "conv_ready",
            "gelu_up", "ff32_ready", "ff_hi_ready", "ff_lo_ready", "down_mm", "down_scaled", "down_t",
            "sum_ready", "stored", "dve_chain", "act_chain", "pool_chain", "d_loaded", "x_again", "b_rows_loaded",
        )}

        def unit_view(buf, n, *shape):
            k, m = shape
            return buf[:, n % 2, 0:k * m].rearrange("p (k m) -> p k m", k=k)

        block = ctx.enter_context(nc.Block())

        @block.sync
        def _(sp):
            def load(dst, src, s):
                sp.dma_start(dst, src).then_inc(S[s], 16)

            def unit(n, dst, src):
                if n >= 2:
                    sp.wait_ge(S["lo_ready"], n - 1)
                sp.dma_start(dst, src).then_inc(S[f"raw_loaded{n % 2}"], 16)

            load(c_col[:, 0, :], c.rearrange("a (p k) -> p (a k)", p=P), "c_loaded")
            for t in range(TT):
                load(xh[:, t, :], x[0, t * P:(t + 1) * P, :], "x_loaded")
            sp.dma_start(pos_i, positions[0].rearrange("(a p) -> p a", p=P), allow_slow_non_contiguous=True
                         ).then_inc(S["pos_loaded"], 16)
            load(inv_bc, inv_freq[0].partition_broadcast(P), "bc_loaded")
            load(gq_bc, q_norm[0].partition_broadcast(P), "bc_loaded")
            load(gk_bc, k_norm[0].partition_broadcast(P), "bc_loaded")
            rows = lambda v, n: v.rearrange("(a p) -> a p", a=n)
            load(vec_rows[0:48, 0, :], rows(b_ada[0], 48), "rows_loaded")
            load(vec_rows[48:56, 0, :], rows(norm_mix[0], KD), "rows_loaded")
            load(vec_rows[56:64, 0, :], rows(norm_ffn[0], KD), "rows_loaded")
            load(vec_rows[64:68, 0, :], rows(out_norm_ssm[0], 4), "rows_loaded")
            load(vec_rows[68:72, 0, :], rows(out_norm_attn[0], 4), "rows_loaded")
            load(vec_rows[0:88, 1, :], conv_w[0, 0:2, :].rearrange("j (a p) -> (j a) p", p=P), "rows_loaded")
            load(vec_rows[0:44, 2, :], rows(conv_w[0, 2, :], 44), "rows_loaded")
            load(vec_rows[44:88, 2, :], rows(conv_b[0], 44), "rows_loaded")
            load(vec_rows[0:GP, 3, :], ssm_a_re[0].rearrange("(g q) p -> g (q p)", q=2), "rows_loaded")
            load(vec_rows[GP:2 * GP, 3, :], ssm_a_im[0].rearrange("(g q) p -> g (q p)", q=2), "rows_loaded")
            load(dt_rows[32:32 + GP, :], ssm_log_dt[0].rearrange("(g q) -> g q", q=2), "rows_loaded")
            load(b_glu_row, ssm_b_glu, "b_rows_loaded")
            load(d_bc, ssm_d[0].partition_broadcast(CH), "d_loaded")
            wa = w_ada[0].rearrange("(p k) n -> p k n", k=KD)
            for i in range(4):
                load(ada_first[:, i], wa[:, :, i * 512:(i + 1) * 512], f"ada_first_loaded{i}")

            w_in_k = w_in[0].rearrange("(k p) n -> p k n", p=P)
            unit(U_TAIL, unit_view(w_raw, U_TAIL, KD, TAIL), w_in_k[:, :, 2560:2560 + TAIL])
            sp.wait_ge(S["ada_acc_ready"], 4)
            load(b_g1_row, b_ada[:, 2 * D_MODEL:3 * D_MODEL], "b_rows_loaded")
            nth_ada = [0]

            def later_ada(pieces):
                for _ in range(pieces):
                    n = nth_ada[0]
                    if n < 2:
                        sp.wait_ge(S["ada_acc_ready"], 4)
                    else:
                        sp.wait_ge(S["ada_used"], n - 1)
                    a = 2048 + 256 * n
                    load(ada_next[n % 2], wa[:, :, a:a + 256], f"ada_next_loaded{n % 2}")
                    nth_ada[0] += 1

            for n0 in (U_QI, U_U, U_K, U_Q, U_V):
                for kh in range(2):
                    unit(n0 + kh, unit_view(w_raw, n0 + kh, 4, 512),
                         w_in_k[:, 4 * kh:4 * kh + 4, COLS[n0]:COLS[n0] + 512])
                    if n0 + kh in (U_K + 1, U_Q, U_V):
                        later_ada(2)
                if n0 == U_K:
                    for t in range(TT):
                        sp.wait_ge(S["proj_read"], 4 * 2 + t + 1)
                        sp.dma_start(u_dram[t * P:(t + 1) * P, :], v_tok[:, t, :]).then_inc(S["u_stored"], 16)
            unit(U_GLU, unit_view(w_raw, U_GLU, 4, 512), ssm_w_glu[0].rearrange("(k p) n -> p k n", p=P))
            later_ada(10)
            w_out_k = w_out[0].rearrange("(k p) n -> p k n", p=P)
            unit(U_OUT, unit_view(w_raw, U_OUT, 4, 512), w_out_k[:, 0:4, 0:512])

            sp.wait_ge(S["x_t_ready"], KD)
            sp.wait_ge(S["u_stored"], 16 * TT)
            load(chunk_rows, u_dram.rearrange("(c i) n -> c (i n)", i=CHUNK), "u_loaded")
            sp.wait_ge(S["weights_used"], U_V + 2)
            sp.wait_ge(S["rot_ready"], 1 + 3 * TT)
            sp.wait_ge(S["bias_ready"], TT - 1)
            for r, (bsrc, csrc) in enumerate(((ssm_b_re, ssm_c_re), (ssm_b_im, ssm_c_im))):
                load(s5_b[:, r], bsrc[0].rearrange("(g q) p h -> (q p) g h", q=2), "s5_loaded")
                for q in range(2):
                    load(c_rows[:, r, :, q, :], csrc[0].rearrange("(a g) h p -> (g h) a p", a=4), "s5_loaded")
            sp.wait_ge(S["zero_ready"], 1)
            for i in range(2):
                sp.dma_start(lag_dram[:, NG * i:NG * (i + 1), 0:CHUNK - 1, :],
                             s5_mem[0:CH, 0:NG * (CHUNK - 1) * CH].rearrange("p (g l h) -> p g l h", g=NG, l=CHUNK - 1)
                             ).then_inc(S["zeros_stored"], 16)
            sp.wait_ge(S["zeros_stored"], 32)
            for half in range(2):
                sp.wait_ge(S["lag_d_added"], 4 * half + 4)
                gs = slice(NG * half, NG * (half + 1))
                sp.dma_start(lag_dram[:, gs, CHUNK - 1:, :], lags).then_inc(S["lags_stored"], 16)
                sp.wait_ge(S["lags_stored"], 16 * (half + 1))
                sp.wait_ge(S["v_ready"], 4 * half + 4)
                for j in range(CHUNK):
                    load(s5_m[CH * j:CH * (j + 1)].rearrange("p g (l h) -> p g l h", l=CHUNK),
                         lag_dram[:, gs, CHUNK - 1 - j:2 * CHUNK - 1 - j, :], "m_loaded")
            sp.wait_ge(S["y_read"], 8)
            sp.dma_start(y_dram.rearrange("(c i) n -> c (i n)", i=CHUNK), chunk_rows).then_inc(S["y_stored"], 16)
            sp.wait_ge(S["y_stored"], 16)
            load(y_ssm, y_dram.rearrange("(a p) n -> p a n", p=P), "y_loaded")
            for t in range(TT):
                load(xh[:, t, :], x[0, t * P:(t + 1) * P, :], "x_again")

            for n in range(2):
                for kh in range(2):
                    i = U_OUT + 2 * n + kh
                    if i > U_OUT:
                        unit(i, unit_view(w_raw, i, 4, 512), w_out_k[:, 4 * kh:4 * kh + 4, 512 * n:512 * n + 512])

            w_up_k = w_up[0].rearrange("(k p) (s n) -> p k s n", p=P, s=2)
            with sp.Fori(0, UPS) as j:
                for kh in range(2):
                    sp.wait_ge(S["lo_ready"], j * 2 + (U_UP + kh - 1))
                    for s in range(2):
                        sp.dma_start(w_raw[:, (U_UP + kh) % 2, :].rearrange("p (k s n) -> p k s n", k=4, s=2)[:, :, s, :],
                                     w_up_k[:, 4 * kh:4 * kh + 4, s, bass.ds(j * 256, 256)]
                                     ).then_inc(S[f"raw_loaded{(U_UP + kh) % 2}"], 16)
            with sp.Fori(0, FT // 2 - 1, 2) as j:
                for i in range(2):
                    sp.wait_ge(S["lo_ready"], j + (U_DOWN + i - 1))
                    for k in range(2):
                        sp.dma_start(w_raw[:, (U_DOWN + i) % 2, 1024 * k:1024 * k + 1024],
                                     w_down[0][bass.ds(j * 256 + (256 * i + P * k), P), :]
                                     ).then_inc(S[f"raw_loaded{(U_DOWN + i) % 2}"], 16)
            sp.wait_ge(S["lo_ready"], UNITS - 2)
            for k in range(2):
                sp.dma_start(w_raw[:, (UNITS - 1) % 2, 1024 * k:1024 * k + 1024],
                             w_down[0, (FT - 2 + k) * P:(FT - 1 + k) * P, :]
                             ).then_inc(S[f"raw_loaded{(UNITS - 1) % 2}"], 16)
            for n in range(4):
                sp.wait_ge(S["sum_ready"], 2 * n + 2)
                sp.dma_start(out[0].rearrange("(a p) n -> p a n", p=P)[:, :, 256 * n:256 * n + 256],
                             xh[:, :, 256 * n:256 * n + 256]).then_inc(S["stored"], 16)
            sp.wait_ge(S["stored"], 64)

        def raw_count(n):
            total = 0
            for i in range(n % 2, n + 1, 2):
                total += 2 if i >= U_UP else 1
            return 16 * total

        @block.gpsimd
        def _(pool):
            chain = [0]

            def link(ins):
                chain[0] += 1
                ins.then_inc(S["pool_chain"], 1)
                pool.wait_ge(S["pool_chain"], chain[0])

            def lo(slot, width=UNIT):
                nc.gpsimd.tensor_tensor(w_lo[:, slot, 0:width], w_raw[:, slot, 0:width],
                                        w_hi[:, slot, 0:width].bitcast(F32), ALU.subtract).then_inc(S["lo_ready"], 1)

            link(nc.gpsimd.memset(ident[:], 0.0))
            nc.gpsimd.affine_select(out=ident[:], in_=ident[:], compare_op=ALU.not_equal, fill=1.0, base=0,
                                    pattern=[[-1, P]], channel_multiplier=1).then_inc(S["ident_ready"], 1)
            nc.gpsimd.memset(ones[:], 1.0).then_inc(S["ones_ready"], 1)
            link(nc.gpsimd.memset(bias[0], 0.0))
            link(nc.gpsimd.affine_select(out=bias[0], in_=bias[0], compare_op=ALU.is_ge, fill=MASK, base=0,
                                         pattern=[[-1, P]], channel_multiplier=1))

            def future(t):
                pool.wait_ge(S["relu_used"], HEADS * t)
                diag = score[t][:, t * P:(t + 1) * P]
                nc.gpsimd.affine_select(out=diag, in_=diag, compare_op=ALU.is_ge, fill=FUTURE, base=0,
                                        pattern=[[-1, P]], channel_multiplier=1).then_inc(S["future_set"], 1)

            for n in range(U_UP):
                pool.wait_ge(S["hi_ready"], n + 1)
                lo(n % 2, KD * TAIL if n == U_TAIL else UNIT)
                if n == U_K:
                    for t in range(1, TT):
                        future(t)
                if n == U_V + 1:
                    pool.wait_ge(S["weights_used"], U_V + 2)
                    nc.gpsimd.memset(s5_mem[:, 0:2048], 0.0).then_inc(S["zero_ready"], 1)
            with pool.Fori(0, 2 * UPS + 10, 2) as j:
                for i in range(2):
                    pool.wait_ge(S["hi_ready"], j + (U_UP + i + 1))
                    lo((U_UP + i) % 2)
            pool.wait_ge(S["hi_ready"], UNITS)
            lo((UNITS - 1) % 2)

        @block.scalar
        def _(act):
            chain = [0]

            def link(ins):
                chain[0] += 1
                ins.then_inc(S["act_chain"], 1)
                act.wait_ge(S["act_chain"], chain[0])

            def hi(n, width=UNIT):
                act.wait_ge(S[f"raw_loaded{n % 2}"], raw_count(n))
                if n >= 2:
                    act.wait_ge(S["weights_used"], n - 1)
                nc.scalar.activation(w_hi[:, n % 2, 0:width], w_raw[:, n % 2, 0:width], ACT.Copy
                                     ).then_inc(S["hi_ready"], 1)

            act.wait_ge(S["c_loaded"], 16)
            nc.scalar.activation(c_col[:, 2, :], c_col[:, 0, :], ACT.Tanh, scale=0.5).then_inc(S["tanh_c"], 1)
            act.wait_ge(S["x_loaded"], 16 * TT)
            for t in range(TT):
                if t >= 2:
                    act.wait_ge(S["ss_x_ready"], t - 1)
                nc.scalar.activation(square_at[t % 2], xh[:, t, :], ACT.Square,
                                     accum_out=ss_x[:, t:t + 1]).then_inc(S["ss_x_ready"], 1)
            act.wait_ge(S["angle_ready"], 1)
            nc.scalar.activation(rope[:, 1], rope[:, 3], ACT.Sin).then_inc(S["sin_ready"], 1)
            nc.scalar.activation(rope[:, 0], rope[:, 2], ACT.Sin).then_inc(S["sin_ready"], 1)
            act.wait_ge(S["rstd_x_ready"], 1)
            for t in range(TT):
                nc.scalar.activation(xh[:, t, :], xh[:, t, :], ACT.Copy, scale=rstd_x[:, t:t + 1]
                                     ).then_inc(S["xn_ready"], 1)
            act.wait_ge(S["mod1_ready"], 1)
            for k in range(KD):
                act.wait_ge(S["x_t_ready"], k + 1)
                if k >= 2:
                    act.wait_ge(S["act_in_ready"], k - 1)
                nc.scalar.activation(up32[:, k % 2, :], bank[k % 4][:], ACT.Identity, scale=scale1[:, k:k + 1],
                                     bias=shift1[:, k:k + 1]).then_inc(S["x_t_read"], 1)
            hi(U_TAIL, KD * TAIL)
            hi(U_QI)

            def results(nth, n_last, dst, width=512, before=None):
                for t in range(TT):
                    if t < TT - 1:
                        act.wait_ge(S["proj_ready"], 3 * nth + t + 1)
                    else:
                        act.wait_ge(S["weights_used"], n_last + 1)
                    if before is not None:
                        before(t)
                    nc.scalar.activation(dst[:, t, 0:width], bank[t][:, 0:width], ACT.Copy).then_inc(S["proj_read"], 1)

            turned = [0]

            def turned_read(dst):
                for t in range(TT):
                    act.wait_ge(S["turned_ready"], turned[0] + 1)
                    nc.scalar.activation(dst[:, :, t * P:(t + 1) * P],
                                         bank[4 + turned[0] % 2][:].rearrange("p (g t) -> p g t", g=4), ACT.Copy
                                         ).then_inc(S["turned_read"], 1)
                    turned[0] += 1

            def squares(which):
                for t in range(TT):
                    n = 4 * which + t
                    act.wait_ge(S["proj_read"], 4 * (3 + which) + t + 1)
                    if n >= 2:
                        act.wait_ge(S["sq_used"], n - 1)
                    nc.scalar.activation(up32[:, n % 2, :], pre[:, t, :], ACT.Square).then_inc(S["ss_qk_ready"], 1)

            results(0, U_TAIL, ki_w, TAIL)
            hi(U_QI + 1)
            hi(U_U)
            results(1, U_QI + 1, pre)
            hi(U_U + 1)
            hi(U_K)
            results(2, U_U + 1, v_tok)
            hi(U_K + 1)
            act.wait_ge(S["turned_ready"], 1)
            nc.scalar.activation(ki_t, bank[4][:], ACT.Copy).then_inc(S["turned_read"], 1)
            turned[0] = 1
            turned_read(qi_t)
            for i in range((TT - 1) * HEADS):
                t = 1 + i // HEADS
                act.wait_ge(S["score_mm"], i + 1)
                if i >= 2:
                    act.wait_ge(S["relu_used"], i - 1)
                nc.scalar.activation(relu[:, i % 2, 0:KEYS[t]], bank[6 + i % 2][:, 0:KEYS[t]], ACT.Relu
                                     ).then_inc(S["relu_ready"], 1)
            hi(U_Q)
            results(3, U_K + 1, pre, before=lambda t: act.wait_ge(S["rot_ready"], 1 + t + 1))
            squares(0)
            hi(U_Q + 1)
            hi(U_V)
            results(4, U_Q + 1, pre, before=lambda t: act.wait_ge(S["rot_ready"], 5 + t + 1))
            turned_read(k_t)
            squares(1)
            hi(U_V + 1)
            hi(U_GLU)
            results(5, U_V + 1, v_tok, before=lambda t: act.wait_ge(S["u_stored"], 16 * TT))
            turned_read(q_t)
            hi(U_OUT)

            for i in range(TT * HEADS):
                t = i // HEADS
                act.wait_ge(S["logit_ready"], i + 1)
                if i >= 2:
                    act.wait_ge(S["prob_turned"], i - 1)
                nc.scalar.activation(prob[:, i % 2, 0:KEYS[t]], logit[:, i % 8, 0:KEYS[t]], ACT.Exp, scale=-1.0,
                                     bias=neg_max[:, i:i + 1], accum_out=psum_p[:, i:i + 1]
                                     ).then_inc(S["prob_ready"], 1)

            act.wait_ge(S["u_loaded"], 16)
            for i in range(2):
                gs = slice(NG * i, NG * (i + 1))
                nc.scalar.activation(
                    group_in[:, gs, :].rearrange("c g (i h) -> c g i h", i=CHUNK),
                    chunk_in.rearrange("c i (g h) -> c g i h", g=GROUPS)[:, gs], ACT.Copy).then_inc(S["u_grouped"], 1)
            act.wait_ge(S["c_t"], 1)
            for r in range(2):
                for q in range(2):
                    hp = slice(64 * q, 64 * q + 64)
                    ins = nc.scalar.activation(s5_c[hp, r],
                                               bank[r][hp, :].rearrange("p (g q h) -> p g q h", g=GP, q=2)[:, :, q, :],
                                               ACT.Copy)
            ins.then_inc(S["c_t_read"], 1)
            act.wait_ge(S["s5_angle"], 1)
            nc.scalar.activation(s5_p[:, 8:10], s5_p[:, 6:8], ACT.Sin).then_inc(S["s5_sin"], 1)
            for half in range(2):
                for i in range(4):
                    act.wait_ge(S["v_t"], 4 * half + i + 1)
                    nc.scalar.activation(s5_v[:, 2 * i:2 * i + 2], bank[i][:].rearrange("p (g r n) -> p g r n", g=2, r=2),
                                         ACT.Copy).then_inc(S["v_ready"], 1)
                for i in range(4):
                    act.wait_ge(S["lag_mm"], 4 * half + i + 1)
                    if i == 0 and half:
                        act.wait_ge(S["y_mm"], 4)
                    nc.scalar.activation(lags_of(i), bank[4 + (i % 2) * 2 + i // 2][0:CH, :].rearrange(
                        "p (g l h) -> p g l h", g=4, l=CHUNK), ACT.Copy).then_inc(S["lags_ready"], 1)
                for i in range(2):
                    act.wait_ge(S["u_t"], 2 * half + i + 1)
                    if i == 0:
                        act.wait_ge(S["lags_stored"], 16 * (half + 1))
                    nc.scalar.activation(s5_u[:, 8 * i:8 * i + 8], bank[i][:].rearrange("p (g n) -> p g n", g=8),
                                         ACT.Copy).then_inc(S["u_t_read"], 1)
                for i in range(4):
                    act.wait_ge(S["y_mm"], 4 * half + i + 1)
                    for c in range(4):
                        g = NG * half + 8 * (i // 2) + 2 * c + i % 2
                        ins = nc.scalar.activation(
                            chunk_in[:, :, g * CH:(g + 1) * CH],
                            bank[4 + (i % 2) * 2 + i // 2][0:NCH, c * P:(c + 1) * P].rearrange(
                                "c (i h) -> c i h", i=CHUNK), ACT.Copy)
                    ins.then_inc(S["y_read"], 1)

            act.wait_ge(S["y_loaded"], 16)
            for t in range(TT):
                nc.scalar.activation(y_ssm[:, t, :], y_ssm[:, t, :], ACT.Gelu_apprx_tanh).then_inc(S["gelu_ready"], 1)
            for k in range(4):
                act.wait_ge(S["g_t"], k + 1)
                if k >= 2:
                    act.wait_ge(S["glu_in"], k - 1)
                nc.scalar.activation(up32[:, k % 2, :], bank[k][:], ACT.Copy).then_inc(S["g_t_read"], 1)
            for t in range(TT):
                act.wait_ge(S["glu_mm"], t + 1)
                if t >= 2:
                    act.wait_ge(S["glu_read"], t - 1)
                if t == 0:
                    act.wait_ge(S["glu_in"], 4)
                nc.scalar.activation(up32[:, t % 2, :], bank[4 + t][:], ACT.Tanh, scale=0.5).then_inc(S["tanh_z"], 1)
            hi(U_OUT + 1)
            for w, y in ((1, y_attn), (0, y_ssm)):
                for t in range(TT):
                    if w:
                        act.wait_ge(S["y_attn_ready"], TT)
                    else:
                        act.wait_ge(S["glu_read"], TT)
                    nc.scalar.activation(logit[:, 4 * w + t, :], y[:, t, :], ACT.Square,
                                         accum_out=ss_y[:, 4 * w + t:4 * w + t + 1]).then_inc(S["ss_y_ready"], 1)
            for k in range(KD):
                act.wait_ge(S["mix_t"], k + 1)
                if k >= 2:
                    act.wait_ge(S["mix_in"], k - 1)
                nc.scalar.activation(up32[:, k % 2, :], bank[k % 4][:], ACT.Copy,
                                     scale=vec_cols[:, C_NSSM + k:C_NSSM + k + 1]).then_inc(S["mix_t_read"], 1)
            hi(U_OUT + 2)
            hi(U_OUT + 3)
            for t in range(TT):
                act.wait_ge(S["h_ready"], TT + t + 1)
                if t == 0:
                    act.wait_ge(S["mix_in"], KD)
                if t >= 2:
                    act.wait_ge(S["ss_h_ready"], t - 1)
                nc.scalar.activation(square_at[t % 2], xh[:, t, :], ACT.Square,
                                     accum_out=ss_h[:, t:t + 1]).then_inc(S["ss_h_ready"], 1)
            hi(U_UP)
            hi(U_UP + 1)
            for k in range(KD):
                act.wait_ge(S["h_t"], k + 1)
                if k >= 2:
                    act.wait_ge(S["mlp_in"], k - 1)
                nc.scalar.activation(up32[:, k % 2, :], bank[k % 4][:], ACT.Identity, scale=scale2[:, k:k + 1],
                                     bias=shift2[:, k:k + 1]).then_inc(S["h_t_read"], 1)
            act.wait_ge(S["mlp_in"], KD)

            def hi_ahead(j, kh):
                act.wait_ge(S[f"raw_loaded{kh}"], j * 32 + (raw_count(U_UP + kh) + 32))
                act.wait_ge(S["weights_used"], j * 2 + (U_UP + kh + 1))
                nc.scalar.activation(w_hi[:, kh, :], w_raw[:, kh, :], ACT.Copy).then_inc(S["hi_ready"], 1)

            with act.Fori(0, UPS) as j:
                hi_ahead(j, 0)
                for q in range(4):
                    f = (0, 1, FT, FT + 1)[q]
                    if q < 3:
                        act.wait_ge(S["up_mm"], j * 3 + (q + 1))
                    else:
                        act.wait_ge(S["weights_used"], j * 2 + (U_UP + 2))
                    nc.scalar.activation(conv[:, q, :], bank[q][:], ACT.Identity,
                                         scale=vec_cols[:, bass.ds(j * 2 + (C_W2 + f), 1)],
                                         bias=vec_cols[:, bass.ds(j * 2 + (C_CB + f), 1)]
                                         ).then_inc(S["tap_ready"], 1)
                hi_ahead(j, 1)
                for q in range(2):
                    act.wait_ge(S["conv_ready"], j * 4 + (q + 1))
                    nc.scalar.activation(conv[:, q, :], conv[:, q, :], ACT.Gelu_apprx_tanh
                                         ).then_inc(S["gelu_up"], 1)
                for q in range(2):
                    act.wait_ge(S["ff32_ready"], j * 2 + (q + 1))
                    nc.scalar.activation(ff_hi[:, bass.ds(j * 2 + q, 1), :].rearrange("p a t -> p (a t)"),
                                         up32[:, q, :], ACT.Copy).then_inc(S["ff_hi_ready"], 1)
            for n in range(U_DOWN + 2, UNITS):
                hi(n)
            for n in range(KD):
                act.wait_ge(S["down_mm"], n + 1)
                if n >= 2:
                    act.wait_ge(S["down_t"], n - 1)
                nc.scalar.activation(up32[:, n % 2, :], bank[n][:], ACT.Copy, scale=gate2[:, n:n + 1]
                                     ).then_inc(S["down_scaled"], 1)

        @block.vector
        def _(dve):
            V = nc.vector
            count = {}

            def link(ins, s="dve_chain"):
                count[s] = count.get(s, 0) + 1
                ins.then_inc(S[s], 1)
                dve.wait_ge(S[s], count[s])

            def signal(ins, s):
                count[s] = count.get(s, 0) + 1
                ins.then_inc(S[s], 1)

            def rsqrt(y, v, t, s="dve_chain"):
                link(V.tensor_scalar(y.bitcast(I32), v.bitcast(I32), 1, None, ALU.logical_shift_right))
                link(V.tensor_scalar(y.bitcast(I32), y.bitcast(I32), -1.0, RSQRT_GUESS, ALU.mult, ALU.add))
                for n in range(4):
                    link(V.scalar_tensor_tensor(t, y, 1.0, y, ALU.mult, ALU.mult))
                    link(V.scalar_tensor_tensor(t, t, -0.5, v, ALU.mult, ALU.mult))
                    link(V.scalar_tensor_tensor(y, t, 1.5, y, ALU.add, ALU.mult), s if n == 3 else "dve_chain")

            def reduce_angle(r, k):
                link(V.tensor_scalar(k, r, 1 / (2 * math.pi), MAGIC, ALU.mult, ALU.add))
                link(V.tensor_scalar(k, k, -MAGIC, None, ALU.add))
                for part in TWO_PI:
                    link(V.scalar_tensor_tensor(r, k, -part, r, ALU.mult, ALU.add))
                pi = float(np.nextafter(np.float32(math.pi), np.float32(0)))
                link(V.tensor_scalar(r, r, pi, -pi, ALU.min, ALU.max))

            def cos_angle(out, r, s):
                link(V.scalar_tensor_tensor(out, r, -1.0, r, ALU.mult, ALU.min))
                link(V.tensor_scalar(out, out, math.pi / 2, None, ALU.add), s)

            def exp(y, x, k, k1, r):
                link(V.tensor_scalar(r, x, -174.0, 178.0, ALU.max, ALU.min))
                link(V.tensor_scalar(k, r, 1 / math.log(2.0), MAGIC, ALU.mult, ALU.add))
                link(V.tensor_scalar(k, k, -MAGIC, None, ALU.add))
                for part in LN2:
                    link(V.scalar_tensor_tensor(r, k, -part, r, ALU.mult, ALU.add))
                link(V.tensor_scalar(y, r, 1 / 5040, 1 / 720, ALU.mult, ALU.add))
                for i in (5, 4, 3, 2, 1, 0):
                    link(V.tensor_tensor(y, y, r, ALU.mult))
                    link(V.tensor_scalar(y, y, 1 / math.factorial(i), None, ALU.add))
                link(V.tensor_scalar(k1, k, 0.5, MAGIC, ALU.mult, ALU.add))
                link(V.tensor_scalar(k1, k1, -MAGIC, None, ALU.add))
                link(V.tensor_tensor(k, k, k1, ALU.subtract))
                for e in (k1, k):
                    link(V.tensor_scalar(r.bitcast(I32), e, 127.0, 8388608.0, ALU.add, ALU.mult))
                    link(V.tensor_tensor(y, y, r, ALU.mult))

            dve.wait_ge(S["rows_loaded"], 16 * 11)
            V.tensor_copy(vec_rows[32:32 + GP, 3, :].rearrange("g (q p) -> g q p", q=2),
                          dt_rows[32:32 + GP, :].unsqueeze(2).broadcast_to([GP, 2, 64])).then_inc(S["dt_spread"], 1)
            dve.wait_ge(S["tanh_c"], 1)
            link(V.scalar_tensor_tensor(silu_c, c_col[:, 2, :], 1.0, c_col[:, 0, :], ALU.add, ALU.mult))
            link(V.tensor_scalar(silu_c, silu_c, 0.5, None, ALU.mult))
            dve.wait_ge(S["pos_loaded"], 16)
            dve.wait_ge(S["bc_loaded"], 48)
            link(V.tensor_copy(pos_f, pos_i))
            ang = rope[:, 3]
            for i in range(2):
                link(V.tensor_tensor(ang[:, :, HALF * i:HALF * (i + 1)], pos_f.unsqueeze(2).broadcast_to([P, TT, HALF]),
                                     inv_bc.unsqueeze(1).broadcast_to([P, TT, HALF]), ALU.mult))
            reduce_angle(ang, rope[:, 4])
            cos_angle(rope[:, 2], ang, "angle_ready")

            dve.wait_ge(S["ss_x_ready"], TT)
            link(V.tensor_scalar(ss_x, ss_x, 1 / D_MODEL, EPS, ALU.mult, ALU.add))
            rsqrt(rstd_x, ss_x, work[:, 0:4], "rstd_x_ready")

            dve.wait_ge(S["sin_ready"], 2)
            link(V.tensor_scalar(rope[:, 1, :, 0:HALF], rope[:, 1, :, 0:HALF], -1.0, None, ALU.mult))
            for i, g in ((2, gq_bc), (4, gk_bc)):
                link(V.tensor_tensor(rope[:, i], rope[:, 0], g.unsqueeze(1).broadcast_to([P, TT, HD]), ALU.mult))
                for a in range(2):
                    link(V.tensor_tensor(rope[:, i + 1, :, HALF * a:HALF * (a + 1)], rope[:, 1, :, HALF * a:HALF * (a + 1)],
                                         g[:, HALF * (1 - a):HALF * (2 - a)].unsqueeze(1).broadcast_to([P, TT, HALF]),
                                         ALU.mult))

            def ada(dst, src, s):
                link(V.tensor_scalar(dst, src[:, 0, :], silu_c[:, 0:1], None, ALU.mult))
                for k in range(1, KD):
                    ins = V.scalar_tensor_tensor(dst, src[:, k, :], silu_c[:, k:k + 1], dst, ALU.mult, ALU.add)
                    link(ins, s if k == KD - 1 else "dve_chain")

            for i in range(4):
                dve.wait_ge(S[f"ada_first_loaded{i}"], 16)
                ada(ada_first_acc[:, 512 * i:512 * i + 512], ada_first[:, i], "ada_acc_ready")
            dve.wait_ge(S["vec_t"], 1)
            link(V.tensor_copy(vec_cols[:], bank[4][:, 0:296]))
            dve.wait_ge(S["mod_ready"], 1)
            link(V.tensor_tensor(shift1, bank[5][:, 0:KD], vec_cols[:, C_BADA:C_BADA + KD], ALU.add))
            link(V.tensor_tensor(scale1, bank[5][:, KD:2 * KD], vec_cols[:, C_BADA + KD:C_BADA + 2 * KD], ALU.add))
            link(V.scalar_tensor_tensor(scale1, scale1, 1.0, vec_cols[:, C_NMIX:C_NMIX + KD], ALU.add, ALU.mult),
                 "mod1_ready")

            def split(k, s, ready):
                dve.wait_ge(S[s], k + 1)
                link(V.tensor_copy(act_hi[:, k, :], up32[:, k % 2, :]))
                signal(V.tensor_tensor(act_lo[:, k, :], up32[:, k % 2, :], act_hi[:, k, :].bitcast(F32), ALU.subtract),
                       ready)

            for k in range(KD):
                split(k, "x_t_read", "act_in_ready")

            def rotate(src, dst, tab, t, heads, s):
                cos, sin = rope[:, tab, t, :], rope[:, tab + 1, t, :]
                sh = src.rearrange("p (h d) -> p h d", h=heads)
                dh = dst.rearrange("p (h d) -> p h d", h=heads)
                th = tmp[:, 0:heads * HD].rearrange("p (h d) -> p h d", h=heads)
                V.tensor_tensor(dh, sh, cos.unsqueeze(1).broadcast_to([P, heads, HD]), ALU.mult)
                for a in range(2):
                    o = slice(HALF * a, HALF * (a + 1))
                    w = slice(HALF * (1 - a), HALF * (2 - a))
                    ins = V.tensor_tensor(th[:, :, o], sh[:, :, w],
                                          sin[:, o].unsqueeze(1).broadcast_to([P, heads, HALF]), ALU.mult)
                link(ins)
                link(V.tensor_tensor(dst, dst, tmp[:, 0:heads * HD], ALU.add), s)

            dve.wait_ge(S["proj_read"], 4)
            link(V.tensor_scalar(wi[:], ki_w[:, :, HD:TAIL], WI_SCALE, None, ALU.mult))
            for t in range(TT):
                rotate(ki_w[:, t, 0:HD], rot[:, 0, P * t:P * t + HD], 0, t, 1, "dve_chain")
            signal(V.tensor_copy(rot[:, 0, :].rearrange("p (t a d) -> p t a d", t=TT, a=2)[:, :, 1, :],
                                 rot[:, 0, :].rearrange("p (t a d) -> p t a d", t=TT, a=2)[:, :, 0, :]), "rot_ready")
            for t in range(TT):
                dve.wait_ge(S["proj_read"], 4 + t + 1)
                if t == 0:
                    dve.wait_ge(S["turned_ready"], 1)
                rotate(pre[:, t, :], rot[:, t, :], 0, t, HEADS, "rot_ready")

            def scores(t):
                for h in range(HEADS):
                    i = (t - 1) * HEADS + h
                    dve.wait_ge(S["relu_ready"], i + 1)
                    if h == 0:
                        link(V.tensor_scalar(score[t], relu[:, i % 2, 0:KEYS[t]], wi[:, t, h:h + 1], None, ALU.mult),
                             "relu_used")
                    else:
                        link(V.scalar_tensor_tensor(score[t], relu[:, i % 2, 0:KEYS[t]], wi[:, t, h:h + 1], score[t],
                                                    ALU.mult, ALU.add), "relu_used")

            def top_k(t):
                dve.wait_ge(S["future_set"], t)
                for _ in range(TOPK // 8):
                    link(V.max(top8, score[t]))
                    link(V.match_replace(score[t], top8, score[t], TAKEN))
                signal(V.tensor_scalar(bias[t], score[t], TAKEN, MASK, ALU.not_equal, ALU.mult), "bias_ready")

            def later_ada(n):
                dve.wait_ge(S[f"ada_next_loaded{n % 2}"], 16 * (n // 2 + 1))
                ada(ada_acc[:, 256 * (n % 4):256 * (n % 4) + 256], ada_next[n % 2], "ada_used")
                if n % 4 < 3:
                    return
                v = n // 4
                dve.wait_ge(S["ada_sum_ready"], v + 1)
                b = vec_cols[:, C_BADA + 8 * (2 + v):C_BADA + 8 * (3 + v)]
                if v == 0:
                    for i in range(2):
                        ins = V.tensor_copy(g1_row[:, 512 * i:512 * i + 512], bank[6 + i][:])
                    link(ins, "ada_sum_read")
                elif v == 2:
                    link(V.tensor_tensor(scale2, bank[6][:, 0:KD], b, ALU.add))
                    link(V.scalar_tensor_tensor(scale2, scale2, 1.0, vec_cols[:, C_NFFN:C_NFFN + KD], ALU.add, ALU.mult),
                         "ada_sum_read")
                else:
                    link(V.tensor_tensor(shift2 if v == 1 else gate2, bank[6][:, 0:KD], b, ALU.add), "ada_sum_read")

            def head_sums(which):
                for t in range(TT):
                    n = 4 * which + t
                    dve.wait_ge(S["ss_qk_ready"], n + 1)
                    link(V.tensor_reduce(ss_qk[:, 32 * which + 8 * t:32 * which + 8 * t + 8],
                                         up32[:, n % 2, :].rearrange("p (h d) -> p h d", h=HEADS), AX, ALU.add), "sq_used")
                w = slice(32 * which, 32 * which + 32)
                link(V.tensor_scalar(ss_qk[:, w], ss_qk[:, w], 1 / HD, EPS, ALU.mult, ALU.add))
                rsqrt(rstd_qk[:, w], ss_qk[:, w], work[:, 0:32])

            def norm_rotate(which, t):
                dve.wait_ge(S["turned_ready"], 1 + 4 + (4 if which else 0))
                rotate(pre[:, t, :], rot[:, t, :], 2 if which else 4, t, HEADS, "rot_ready" if which else "dve_chain")
                if not which:
                    rs = rstd_qk[:, 8 * t:8 * t + 8].unsqueeze(2).broadcast_to([P, HEADS, HD])
                    r3 = rot[:, t, :].rearrange("p (h d) -> p h d", h=HEADS)
                    link(V.tensor_tensor(r3, r3, rs, ALU.mult), "rot_ready")

            for t in range(1, TT):
                scores(t)
            for n in range(4):
                later_ada(n)
            head_sums(0)
            for t in range(TT):
                norm_rotate(0, t)
            top_k(1)
            head_sums(1)
            for n in range(4, 8):
                later_ada(n)
            for t in range(TT):
                norm_rotate(1, t)
            top_k(2)
            for n in range(8, 16):
                later_ada(n)
            top_k(3)
            link(V.tensor_scalar(q_scale, rstd_qk[:, 32:64], -ATT_SCALE, None, ALU.mult))

            def logits(i):
                t = i // HEADS
                dve.wait_ge(S["logit_mm"], i + 1)
                if i >= 8:
                    dve.wait_ge(S["prob_ready"], i - 7)
                signal(V.tensor_tensor_reduce(out=logit[:, i % 8, 0:KEYS[t]], in0=bank[i % 2][:, 0:KEYS[t]], in1=bias[t],
                                              scale=q_scale[:, i:i + 1], scalar=3.0e38, op0=ALU.add, op1=ALU.min,
                                              accum_out=neg_max[:, i:i + 1]), "logit_ready")

            def turned_probs(i):
                t = i // HEADS
                dve.wait_ge(S["prob_turned"], i + 1)
                if i >= 2:
                    dve.wait_ge(S["pv_done"], i - 1)
                signal(V.tensor_copy(prob_t[:, i % 2, 0:KEYS[t]], bank[2 + i % 2][:, 0:KEYS[t]]), "prob_t_ready")

            def heads_out(t):
                dve.wait_ge(S["pv_done"], HEADS * (t + 1))
                w = slice(HEADS * t, HEADS * (t + 1))
                link(V.reciprocal(rinv[:, w], psum_p[:, w]))
                signal(V.tensor_tensor(y_attn[:, t, :].rearrange("p (h d) -> p h d", h=HEADS),
                                       bank[4 + t % 2][:].rearrange("p (h d) -> p h d", h=HEADS),
                                       rinv[:, w].unsqueeze(2).broadcast_to([P, HEADS, HD]), ALU.mult), "y_attn_ready")

            N = TT * HEADS
            for i in range(N + 1):
                if i < N:
                    logits(i)
                if i >= 1:
                    turned_probs(i - 1)
                    if i % HEADS == 0 and i // HEADS >= 2:
                        heads_out(i // HEADS - 2)
            heads_out(TT - 1)

            lr, li, ldt = (vec_cols[:, a:a + GP] for a in (C_ARE, C_AIM, C_LDT))
            dt_, mag, th, cth, kk, k1, tc, ts, snt, cst = (s5_p[:, i] for i in range(10))
            ang_s, ang_c = s5_p[:, 6], s5_p[:, 7]
            sin_t, cos_t = s5_p[:, 8], s5_p[:, 9]
            lb_r, lb_i, cf_r, cf_i, den, n1, n2, ur, ui, r8, w1, w2, w3, w4 = (s5_p[:, i] for i in range(10, 24))
            exp(dt_, ldt, kk, k1, w1)
            link(V.tensor_tensor(w2, lr, dt_, ALU.mult))
            exp(mag, w2, kk, k1, w1)
            link(V.tensor_tensor(ang_s, li, dt_, ALU.mult))
            reduce_angle(ang_s, kk)
            cos_angle(ang_c, ang_s, "s5_angle")
            dve.wait_ge(S["s5_sin"], 1)
            link(V.tensor_tensor(lb_r, mag, cos_t, ALU.mult))
            link(V.tensor_tensor(lb_i, mag, sin_t, ALU.mult))
            link(V.tensor_tensor(den, lr, lr, ALU.mult))
            link(V.tensor_tensor(w1, li, li, ALU.mult))
            link(V.tensor_tensor(den, den, w1, ALU.add))
            link(V.reciprocal(den, den))
            link(V.tensor_scalar(n1, lb_r, -1.0, None, ALU.add))
            link(V.tensor_tensor(cf_r, n1, lr, ALU.mult))
            link(V.tensor_tensor(w1, lb_i, li, ALU.mult))
            link(V.tensor_tensor(cf_r, cf_r, w1, ALU.add))
            link(V.tensor_tensor(cf_r, cf_r, den, ALU.mult))
            link(V.tensor_tensor(cf_i, lb_i, lr, ALU.mult))
            link(V.tensor_tensor(w1, n1, li, ALU.mult))
            link(V.tensor_tensor(cf_i, cf_i, w1, ALU.subtract))
            link(V.tensor_tensor(cf_i, cf_i, den, ALU.mult))

            def cmul(o_r, o_i, a_r, a_i, b_r, b_i, t1, t2, s="dve_chain"):
                V.tensor_tensor(o_r, a_r, b_r, ALU.mult)
                V.tensor_tensor(t1, a_i, b_i, ALU.mult)
                V.tensor_tensor(o_i, a_r, b_i, ALU.mult)
                link(V.tensor_tensor(t2, a_i, b_r, ALU.mult))
                V.tensor_tensor(o_r, o_r, t1, ALU.subtract)
                link(V.tensor_tensor(o_i, o_i, t2, ALU.add), s)

            link(V.memset(power[:, 0, 0, :], 1.0))
            link(V.memset(power[:, 1, 0, :], 0.0))
            link(V.tensor_copy(power[:, 0, 1, :], lb_r))
            link(V.tensor_copy(power[:, 1, 1, :], lb_i))
            for n in range(2, CHUNK + 1):
                a, b = n // 2, n - n // 2
                cmul(power[:, 0, n, :], power[:, 1, n, :], power[:, 0, a, :], power[:, 1, a, :], power[:, 0, b, :],
                     power[:, 1, b, :], w1, w2)
            cmul(ur, ui, cos_t, sin_t, cos_t, sin_t, w1, w2)
            cmul(w3, w4, ur, ui, ur, ui, w1, w2)
            cmul(ur, ui, w3, w4, w3, w4, w1, w2)
            link(V.tensor_tensor(r8, mag, mag, ALU.mult))
            link(V.tensor_tensor(r8, r8, r8, ALU.mult))
            link(V.tensor_tensor(r8, r8, r8, ALU.mult))
            dve.wait_ge(S["s5_loaded"], 96)
            def by_channel(v, n=GP):
                return v.unsqueeze(2).broadcast_to([P, n, CH])
            t1, t2 = (s5_t[:, i, 0:GP * CH].rearrange("p (g h) -> p g h", g=GP) for i in range(2))
            dve.wait_ge(S["weights_used"], U_V + 2)
            cmul(s5_bb[:, 0], s5_bb[:, 1], s5_b[:, 0], s5_b[:, 1], by_channel(cf_r), by_channel(cf_i), t1, t2)

            d_eye = d_bc.rearrange("p (g h) -> p g h", g=GROUPS)
            dve.wait_ge(S["d_loaded"], 16)
            dve.wait_ge(S["ident_ready"], 1)
            link(V.tensor_tensor(d_eye, d_eye, ident[0:CH, 0:CH].unsqueeze(1).broadcast_to([CH, GROUPS, CH]), ALU.mult))

            dve.wait_ge(S["c_t_read"], 1)
            for half in range(2):
                gs = slice(GH * half, GH * (half + 1))
                t1, t2 = (s5_t[:, i, 0:GH * CH].rearrange("p (g h) -> p g h", g=GH) for i in range(2))
                if half:
                    dve.wait_ge(S["y_mm"], 4)
                for n in range(CHUNK + 1):
                    cmul(lag_w[:, 0, :, n, :], lag_w[:, 1, :, n, :], s5_c[:, 0, gs], s5_c[:, 1, gs],
                         by_channel(power[:, 0, n, gs], GH), by_channel(power[:, 1, n, gs], GH), t1, t2)
                link(V.tensor_scalar(lag_w[:, 1], lag_w[:, 1], -1.0, None, ALU.mult))
                for j in range(CHUNK):
                    if j == 0 and half == 0:
                        dve.wait_ge(S["zeros_stored"], 32)
                    cmul(s5_vt[:, 0, :, j, :], s5_vt[:, 1, :, j, :], s5_bb[:, 0, gs], s5_bb[:, 1, gs],
                         by_channel(power[:, 0, CHUNK - 1 - j, gs], GH), by_channel(power[:, 1, CHUNK - 1 - j, gs], GH),
                         t1, t2, "vt_ready" if j == CHUNK - 1 else "dve_chain")
                link(V.memset(turn[:, 0, :, 0:1], 1.0))
                link(V.memset(turn[:, 1, :, 0:1], 0.0))
                link(V.tensor_copy(w3[:, gs], ur[:, gs]))
                link(V.tensor_copy(w4[:, gs], ui[:, gs]))
                n = 1
                while n < NCH:
                    f = lambda v: v[:, gs].unsqueeze(2).broadcast_to([P, GH, n])
                    tt = [s5_t[:, i, 0:GH * n].rearrange("p (g c) -> p g c", g=GH) for i in range(2)]
                    cmul(turn[:, 0, :, n:2 * n], turn[:, 1, :, n:2 * n], turn[:, 0, :, 0:n], turn[:, 1, :, 0:n],
                         f(w3), f(w4), *tt)
                    cmul(w1[:, gs], w2[:, gs], w3[:, gs], w4[:, gs], w3[:, gs], w4[:, gs], kk[:, gs], k1[:, gs])
                    link(V.tensor_copy(w3[:, gs], w1[:, gs]))
                    link(V.tensor_copy(w4[:, gs], w2[:, gs]))
                    n *= 2
                link(V.tensor_copy(scan_r, r8[:, gs].unsqueeze(2).broadcast_to([P, GH, NCH])))
                link(V.memset(scan_r[:, :, 0:1], 0.0))
                for i in range(4):
                    dve.wait_ge(S["lags_ready"], 4 * half + i + 1)
                    d = d_eye[:, NG * half:NG * (half + 1), :].rearrange("p (b c q) h -> p b q c h", b=2, q=2)
                    link(V.tensor_tensor(lags_of(i)[:, :, 0, :], lags_of(i)[:, :, 0, :], d[:, i // 2, i % 2],
                                         ALU.add), "lag_d_added")
                flat = lambda v: v.rearrange("p g c -> p (g c)")
                er, ei = flat(turn[:, 0]), flat(turn[:, 1])
                dve.wait_ge(S["state_mm"], half + 1)
                sr, si = bank[2][:], bank[3][:]
                zr, zi = s5_z[:, 0, :], s5_z[:, 1, :]
                t1, t2 = s5_t[:, 0, :], s5_t[:, 1, :]
                V.tensor_tensor(zr, sr, er, ALU.mult)
                V.tensor_tensor(t1, si, ei, ALU.mult)
                V.tensor_tensor(zi, si, er, ALU.mult)
                link(V.tensor_tensor(t2, sr, ei, ALU.mult), "state_read")
                V.tensor_tensor(zr, zr, t1, ALU.add)
                link(V.tensor_tensor(zi, zi, t2, ALU.subtract))
                fr = flat(scan_r)
                V.tensor_tensor_scan(t1, fr, zr, 0.0, ALU.mult, ALU.add)
                link(V.tensor_tensor_scan(t2, fr, zi, 0.0, ALU.mult, ALU.add))
                a, b = (v.rearrange("p (g c) -> p g c", g=GH)[:, :, 0:NCH - 1] for v in (t1, t2))
                e1, e2 = turn[:, 0, :, 0:NCH - 1], turn[:, 1, :, 0:NCH - 1]
                z1, z2 = (v.rearrange("p (g c) -> p g c", g=GH)[:, :, 0:NCH - 1] for v in (zr, zi))
                V.memset(s5_x[:, :, :, 0:1], 0.0)
                V.tensor_tensor(s5_x[:, 0, :, 1:NCH], a, e1, ALU.mult)
                V.tensor_tensor(z1, b, e2, ALU.mult)
                V.tensor_tensor(s5_x[:, 1, :, 1:NCH], a, e2, ALU.mult)
                link(V.tensor_tensor(z2, b, e1, ALU.mult))
                V.tensor_tensor(s5_x[:, 0, :, 1:NCH], s5_x[:, 0, :, 1:NCH], z1, ALU.subtract)
                link(V.tensor_tensor(s5_x[:, 1, :, 1:NCH], s5_x[:, 1, :, 1:NCH], z2, ALU.add), "s5_state")

            for k in range(4):
                dve.wait_ge(S["g_t_read"], k + 1)
                link(V.tensor_copy(act_hi[:, k, :], up32[:, k % 2, :]))
                signal(V.tensor_tensor(act_lo[:, k, :], up32[:, k % 2, :], act_hi[:, k, :].bitcast(F32), ALU.subtract),
                       "glu_in")
            for t in range(TT):
                dve.wait_ge(S["tanh_z"], t + 1)
                signal(V.scalar_tensor_tensor(y_ssm[:, t, :], up32[:, t % 2, :], 1.0, y_ssm[:, t, :], ALU.add, ALU.mult),
                       "glu_read")
            dve.wait_ge(S["ss_y_ready"], 8)
            link(V.tensor_scalar(ss_y[:, 0:4], ss_y[:, 0:4], 0.25 / 512, EPS, ALU.mult, ALU.add))
            link(V.tensor_scalar(ss_y[:, 4:8], ss_y[:, 4:8], 1.0 / 512, EPS, ALU.mult, ALU.add))
            rsqrt(rstd_y, ss_y, work[:, 0:8])
            link(V.tensor_scalar(rstd_y[:, 0:4], rstd_y[:, 0:4], 0.5, None, ALU.mult))
            for w, y in ((0, y_ssm), (1, y_attn)):
                for t in range(TT):
                    signal(V.tensor_scalar(y[:, t, :], y[:, t, :], rstd_y[:, 4 * w + t:4 * w + t + 1], None, ALU.mult),
                           "yn_ready")
            dve.wait_ge(S["weights_used"], U_GLU + 1)
            for k in range(KD):
                split(k, "mix_t_read", "mix_in")
            dve.wait_ge(S["x_again"], 16 * TT)
            for n in range(2):
                for t in range(TT):
                    if t < TT - 1:
                        dve.wait_ge(S["out_mm"], 3 * n + t + 1)
                    else:
                        dve.wait_ge(S["weights_used"], U_OUT + 2 * n + 2)
                    o = xh[:, t, 512 * n:512 * n + 512]
                    tb = logit[:, t % 2, :]
                    link(V.tensor_tensor(tb, bank[4 * n + t][:], g1_row[:, 512 * n:512 * n + 512], ALU.mult))
                    signal(V.tensor_tensor(o, o, tb, ALU.add), "h_ready")
            dve.wait_ge(S["ss_h_ready"], TT)
            link(V.tensor_scalar(ss_h, ss_h, 1 / D_MODEL, EPS, ALU.mult, ALU.add))
            rsqrt(rstd_h, ss_h, work[:, 64:68])
            for t in range(TT):
                signal(V.tensor_scalar(hn_tok[:, t, :], xh[:, t, :], rstd_h[:, t:t + 1], None, ALU.mult), "hn_ready")
            dve.wait_ge(S["weights_used"], U_OUT + 4)
            for k in range(KD):
                split(k, "h_t_read", "mlp_in")

            with dve.Fori(0, UPS) as j:
                for q in range(4):
                    f = (0, 1, FT, FT + 1)[q]
                    dve.wait_ge(S["tap_ready"], j * 4 + (q + 1))
                    V.scalar_tensor_tensor(conv[:, q, 1:], bank[q][:, 0:SEQ - 1],
                                           vec_cols[:, bass.ds(j * 2 + (C_W1 + f), 1)], conv[:, q, 1:],
                                           ALU.mult, ALU.add).then_inc(S["conv_read"], 1)
                    dve.wait_ge(S["conv_read"], j * 4 + (q + 1))
                    V.scalar_tensor_tensor(conv[:, q, 2:], bank[q][:, 0:SEQ - 2],
                                           vec_cols[:, bass.ds(j * 2 + (C_W0 + f), 1)], conv[:, q, 2:],
                                           ALU.mult, ALU.add).then_inc(S["conv_ready"], 1)
                for q in range(2):
                    dve.wait_ge(S["gelu_up"], j * 2 + (q + 1))
                    dve.wait_ge(S["conv_ready"], j * 4 + 4)
                    V.tensor_tensor(up32[:, q, :], conv[:, q, :], conv[:, 2 + q, :], ALU.mult
                                    ).then_inc(S["ff32_ready"], 1)
                for q in range(2):
                    dve.wait_ge(S["ff_hi_ready"], j * 2 + (q + 1))
                    V.tensor_tensor(ff_lo[:, bass.ds(j * 2 + q, 1), :].rearrange("p a t -> p (a t)"), up32[:, q, :],
                                    ff_hi[:, bass.ds(j * 2 + q, 1), :].rearrange("p a t -> p (a t)").bitcast(F32),
                                    ALU.subtract).then_inc(S["ff_lo_ready"], 1)
            for n in range(KD):
                dve.wait_ge(S["down_t"], n + 1)
                o = xh[:, :, n * P:(n + 1) * P]
                signal(V.tensor_tensor(o, o, bank[n][:].rearrange("p (t d) -> p t d", t=TT), ALU.add), "sum_ready")

        @block.tensor
        def _(pe):
            T = nc.tensor

            def mm3(dst, lhs_hi, lhs_lo, rhs_hi, rhs_lo, start, stop):
                T.matmul(dst, lhs_hi, rhs_hi, start=start, stop=False)
                T.matmul(dst, lhs_hi, rhs_lo, start=False, stop=False)
                return T.matmul(dst, lhs_lo, rhs_hi, start=False, stop=stop)

            def flip(dst, src, n=P, at=0):
                return T.matmul(dst, src, ident[at:at + n, at:at + n], is_transpose=True, start=True, stop=True)

            pe.wait_ge(S["ident_ready"], 1)
            pe.wait_ge(S["rows_loaded"], 16 * 11)
            pe.wait_ge(S["dt_spread"], 1)
            at = 0
            for i, n in enumerate((72, 88, 88, 48)):
                ins = flip(bank[4][:, at:at + n], vec_rows[0:n, i, :], n)
                at += n
            ins.then_inc(S["vec_t"], 1)
            pe.wait_ge(S["xn_ready"], TT)
            for k in range(KD):
                if k >= 4:
                    pe.wait_ge(S["x_t_read"], k - 3)
                for t in range(TT):
                    ins = flip(bank[k % 4][:, t * P:(t + 1) * P], xh[:, t, k * P:(k + 1) * P])
                ins.then_inc(S["x_t_ready"], 1)
                if k == 3:
                    pe.wait_ge(S["ones_ready"], 1)
                    pe.wait_ge(S["ada_acc_ready"], 4)
                    for i in range(16):
                        ins = T.matmul(bank[5][:, i:i + 1], ada_first_acc[:, i * P:(i + 1) * P], ones[:, 0:1],
                                       start=True, stop=True)
                    ins.then_inc(S["mod_ready"], 1)

            def tail():
                n = U_TAIL
                pe.wait_ge(S["lo_ready"], n + 1)
                pe.wait_ge(S["act_in_ready"], KD)
                pe.wait_ge(S["x_t_read"], KD)
                wh, wl = unit_view(w_hi, n, KD, TAIL), unit_view(w_lo, n, KD, TAIL)
                for t in range(TT):
                    ts = slice(t * P, (t + 1) * P)
                    for k in range(KD):
                        ins = mm3(bank[t][:, 0:TAIL], act_hi[:, k, ts], act_lo[:, k, ts], wh[:, k, :], wl[:, k, :],
                                  k == 0, k == KD - 1)
                    ins.then_inc(S["proj_ready" if t < TT - 1 else "weights_used"], 1)

            def project(n0, nth, banks=0, out_sem="proj_ready", free=None):
                for kh in range(2):
                    n = n0 + kh
                    pe.wait_ge(S["lo_ready"], n + 1)
                    wh, wl = unit_view(w_hi, n, 4, 512), unit_view(w_lo, n, 4, 512)
                    for t in range(TT):
                        ts = slice(t * P, (t + 1) * P)
                        if kh == 0 and free is not None:
                            pe.wait_ge(S[free], 4 * nth + t + 1)
                        for i in range(4):
                            k = 4 * kh + i
                            ins = mm3(bank[banks + t][:], act_hi[:, k, ts], act_lo[:, k, ts], wh[:, i, :], wl[:, i, :],
                                      k == 0, k == KD - 1)
                        if t == TT - 1:
                            ins.then_inc(S["weights_used"], 1)
                        elif kh == 1:
                            ins.then_inc(S[out_sem], 1)

            turned = [0]

            def turn_heads(rot_before):
                for t in range(TT):
                    pe.wait_ge(S["rot_ready"], rot_before + t + 1)
                    pe.wait_ge(S["turned_read"], max(turned[0] - 1, 1))
                    for g in range(4):
                        ins = flip(bank[4 + turned[0] % 2][:, g * P:(g + 1) * P], rot[:, t, g * P:(g + 1) * P])
                    ins.then_inc(S["turned_ready"], 1)
                    turned[0] += 1

            tail()
            project(U_QI, 0, free="proj_read")
            pe.wait_ge(S["rot_ready"], 1)
            pe.wait_ge(S["mod1_ready"], 1)
            for t in range(TT):
                ins = flip(bank[4][:, t * P:(t + 1) * P], rot[:, 0, t * P:(t + 1) * P])
            ins.then_inc(S["turned_ready"], 1)
            turned[0] = 1
            project(U_U, 1, free="proj_read")
            turn_heads(1)
            pe.wait_ge(S["turned_read"], 5)
            for i in range((TT - 1) * HEADS):
                t, h = 1 + i // HEADS, i % HEADS
                if i >= 2:
                    pe.wait_ge(S["relu_ready"], i - 1)
                hp = slice(64 * (h % 2), 64 * (h % 2) + 64)
                T.matmul(bank[6 + i % 2][:, 0:KEYS[t]], qi_t[hp, h // 2, t * P:(t + 1) * P], ki_t[hp, 0:KEYS[t]],
                         start=True, stop=True).then_inc(S["score_mm"], 1)

            def ada_sums(v):
                pe.wait_ge(S["ada_used"], 4 * (v + 1))
                if v:
                    pe.wait_ge(S["ada_sum_read"], v)
                else:
                    pe.wait_ge(S["relu_ready"], (TT - 1) * HEADS)
                    pe.wait_ge(S["b_rows_loaded"], 32)
                if v == 0:
                    for i in range(2):
                        T.matmul(bank[6 + i][:], ones[:], ada_acc[:, 512 * i:512 * i + 512], start=True, stop=False)
                        ins = T.matmul(bank[6 + i][:], ones[0:1, :], b_g1_row[:, 512 * i:512 * i + 512],
                                       start=False, stop=True)
                else:
                    for i in range(KD):
                        ins = T.matmul(bank[6][:, i:i + 1], ada_acc[:, i * P:(i + 1) * P], ones[:, 0:1],
                                       start=True, stop=True)
                ins.then_inc(S["ada_sum_ready"], 1)

            project(U_K, 2, free="proj_read")
            ada_sums(0)
            project(U_Q, 3, free="proj_read")
            turn_heads(5)
            project(U_V, 4, free="proj_read")
            ada_sums(1)
            turn_heads(9)
            ada_sums(2)
            ada_sums(3)

            pe.wait_ge(S["proj_read"], 24)
            pe.wait_ge(S["turned_read"], 13)
            pe.wait_ge(S["ada_sum_read"], 4)

            def logits(i):
                t, h = i // HEADS, i % HEADS
                hp = slice(64 * (h % 2), 64 * (h % 2) + 64)
                if i >= 2:
                    pe.wait_ge(S["logit_ready"], i - 1)
                T.matmul(bank[i % 2][:, 0:KEYS[t]], q_t[hp, h // 2, t * P:(t + 1) * P], k_t[hp, h // 2, 0:KEYS[t]],
                         start=True, stop=True).then_inc(S["logit_mm"], 1)

            def turn_probs(i):
                t = i // HEADS
                pe.wait_ge(S["prob_ready"], i + 1)
                if i >= 2:
                    pe.wait_ge(S["prob_t_ready"], i - 1)
                for s in range(t + 1):
                    ins = flip(bank[2 + i % 2][:, s * P:(s + 1) * P], prob[:, i % 2, s * P:(s + 1) * P])
                ins.then_inc(S["prob_turned"], 1)

            def values(i):
                t, h = i // HEADS, i % HEADS
                pe.wait_ge(S["prob_t_ready"], i + 1)
                if h == 0 and t >= 2:
                    pe.wait_ge(S["y_attn_ready"], t - 1)
                for s in range(t + 1):
                    ins = T.matmul(bank[4 + t % 2][:, h * HD:(h + 1) * HD], prob_t[:, i % 2, s * P:(s + 1) * P],
                                   v_tok[:, s, h * HD:(h + 1) * HD], start=(s == 0), stop=(s == t))
                ins.then_inc(S["pv_done"], 1)

            N = TT * HEADS
            for i in range(N + 2):
                if i < N:
                    logits(i)
                if 1 <= i <= N:
                    turn_probs(i - 1)
                if i >= 2:
                    values(i - 2)

            def group_bank(g, n):
                return bank[4 + (g % 2) * 2 + g // 8][0:n, (g % 8 // 2) * P:(g % 8 // 2 + 1) * P]

            pe.wait_ge(S["s5_loaded"], 96)
            pe.wait_ge(S["logit_ready"], N)
            for r in range(2):
                for a in range(4):
                    ins = flip(bank[r][:, P * a:P * (a + 1)], c_rows[:, r, a].rearrange("p q n -> p (q n)"))
            ins.then_inc(S["c_t"], 1)
            pe.wait_ge(S["u_grouped"], 2)
            pe.wait_ge(S["prob_t_ready"], N)
            pe.wait_ge(S["y_attn_ready"], TT)
            pe.wait_ge(S["c_t_read"], 1)
            for half in range(2):
                pe.wait_ge(S["vt_ready"], half + 1)
                if half:
                    pe.wait_ge(S["state_read"], half)
                for g in range(GH):
                    for r in range(2):
                        ins = flip(bank[g // 2][:, ((g % 2) * 2 + r) * P:((g % 2) * 2 + r + 1) * P],
                                   s5_vt[:, r, g].rearrange("p j h -> p (j h)"))
                    if g % 2:
                        ins.then_inc(S["v_t"], 1)
                if half:
                    pe.wait_ge(S["y_read"], 4)
                for g in range(NG):
                    hp = slice(64 * (g % 2), 64 * (g % 2) + 64)
                    o = group_bank(g, CH)
                    for r in range(2):
                        ins = T.matmul(o, s5_bb[hp, r, GH * half + g // 2, :],
                                       lag_w[hp, r, g // 2, 0:CHUNK, :].rearrange("p l h -> p (l h)"),
                                       start=(r == 0), stop=(r == 1))
                    if g % 8 >= 6:
                        ins.then_inc(S["lag_mm"], 1)
                pe.wait_ge(S["v_ready"], 4 * half + 4)
                for g in range(NG):
                    gg = NG * half + g
                    ins = flip(bank[g // 8][:, (g % 8) * NCH:(g % 8 + 1) * NCH], group_in[:, gg, :], NCH, NCH)
                    if g % 8 == 7:
                        ins.then_inc(S["u_t"], 1)
                pe.wait_ge(S["u_t_read"], 2 * half + 2)
                for g in range(NG):
                    hp = slice(64 * (g % 2), 64 * (g % 2) + 64)
                    for r in range(2):
                        ins = T.matmul(bank[2 + r][hp, (g // 2) * NCH:(g // 2 + 1) * NCH], s5_v[:, g // 2, r, hp],
                                       s5_u[:, g, :], start=True, stop=True)
                ins.then_inc(S["state_mm"], 1)
                pe.wait_ge(S["m_loaded"], 16 * CHUNK * (half + 1))
                pe.wait_ge(S["s5_state"], half + 1)
                pe.wait_ge(S["lags_ready"], 4 * half + 4)
                for g in range(NG):
                    hp = slice(64 * (g % 2), 64 * (g % 2) + 64)
                    o = group_bank(g, NCH)
                    T.matmul(o, s5_u[:, g, :], s5_m[:, g, :], start=True, stop=False)
                    for r in range(2):
                        ins = T.matmul(o, s5_x[hp, r, g // 2, :],
                                       lag_w[hp, r, g // 2, 1:, :].rearrange("p l h -> p (l h)"),
                                       start=False, stop=(r == 1))
                    if g % 8 >= 6:
                        ins.then_inc(S["y_mm"], 1)

            pe.wait_ge(S["gelu_ready"], TT)
            for k in range(4):
                for t in range(TT):
                    ins = flip(bank[k][:, t * P:(t + 1) * P], y_ssm[:, t, k * P:(k + 1) * P])
                ins.then_inc(S["g_t"], 1)
            pe.wait_ge(S["lo_ready"], U_GLU + 1)
            pe.wait_ge(S["glu_in"], 4)
            pe.wait_ge(S["y_read"], 8)
            pe.wait_ge(S["b_rows_loaded"], 32)
            wh, wl = unit_view(w_hi, U_GLU, 4, 512), unit_view(w_lo, U_GLU, 4, 512)
            for t in range(TT):
                ts = slice(t * P, (t + 1) * P)
                T.matmul(bank[4 + t][:], ones[0:1, :], b_glu_row, start=True, stop=False)
                for k in range(4):
                    ins = mm3(bank[4 + t][:], act_hi[:, k, ts], act_lo[:, k, ts], wh[:, k, :], wl[:, k, :],
                              False, k == 3)
                ins.then_inc(S["glu_mm"], 1)
            pe.wait_ge(S["g_t_read"], 4)
            flip(bank[0][:, 0:P], ident[:]).then_inc(S["weights_used"], 1)

            for k in range(KD):
                pe.wait_ge(S["yn_ready"], 4 * (k // 4) + 4)
                if k >= 4:
                    pe.wait_ge(S["mix_t_read"], k - 3)
                y = y_ssm if k < 4 else y_attn
                for t in range(TT):
                    ins = flip(bank[k % 4][:, t * P:(t + 1) * P], y[:, t, (k % 4) * P:(k % 4 + 1) * P])
                ins.then_inc(S["mix_t"], 1)
            pe.wait_ge(S["mix_t_read"], KD)
            pe.wait_ge(S["mix_in"], KD)
            pe.wait_ge(S["tanh_z"], TT)
            project(U_OUT, 0, 0, "out_mm")
            project(U_OUT + 2, 0, 4, "out_mm")
            pe.wait_ge(S["hn_ready"], TT)
            for k in range(KD):
                if k >= 4:
                    pe.wait_ge(S["h_t_read"], k - 3)
                for t in range(TT):
                    ins = flip(bank[k % 4][:, t * P:(t + 1) * P], hn_tok[:, t, k * P:(k + 1) * P])
                ins.then_inc(S["h_t"], 1)
            pe.wait_ge(S["h_t_read"], KD)
            pe.wait_ge(S["mlp_in"], KD)

            def up(j, first):
                for kh in range(2):
                    pe.wait_ge(S["lo_ready"], j * 2 + (U_UP + kh + 1))
                    wh, wl = unit_view(w_hi, U_UP + kh, 4, 512), unit_view(w_lo, U_UP + kh, 4, 512)
                    for q in range(4):
                        if kh == 0 and not first:
                            pe.wait_ge(S["conv_ready"], j * 4 + (q - 3))
                        for i in range(4):
                            k = 4 * kh + i
                            qs = slice(q * P, (q + 1) * P)
                            ins = mm3(bank[q][:], wh[:, i, qs], wl[:, i, qs], act_hi[:, k, :], act_lo[:, k, :],
                                      k == 0, k == KD - 1)
                        if q == 3:
                            ins.then_inc(S["weights_used"], 1)
                        elif kh == 1:
                            ins.then_inc(S["up_mm"], 1)

            up(0, True)
            with pe.Fori(1, UPS) as j:
                up(j, False)

            def down(slot, k0, first, last, dyn):
                wh = w_hi[:, slot, :].rearrange("p (k n) -> p k n", k=2)
                wl = w_lo[:, slot, :].rearrange("p (k n) -> p k n", k=2)
                for i in range(2):
                    if dyn:
                        fh = ff_hi[:, bass.ds(k0 + i, 1), :].rearrange("p a t -> p (a t)")
                        fl = ff_lo[:, bass.ds(k0 + i, 1), :].rearrange("p a t -> p (a t)")
                    else:
                        fh, fl = ff_hi[:, k0 + i, :], ff_lo[:, k0 + i, :]
                    for n in range(KD):
                        ns = slice(n * P, (n + 1) * P)
                        ins = mm3(bank[n][:], wh[:, i, ns], wl[:, i, ns], fh, fl, first and i == 0, last and i == 1)
                        if last and i == 1:
                            ins.then_inc(S["down_mm"], 1)
                if not last:
                    ins.then_inc(S["weights_used"], 1)

            pe.wait_ge(S["ff_lo_ready"], FT)
            pe.wait_ge(S["lo_ready"], U_DOWN + 1)
            down(U_DOWN % 2, 0, True, False, False)
            with pe.Fori(0, FT // 2 - 3, 2) as j:
                for i in range(2):
                    pe.wait_ge(S["lo_ready"], j + (U_DOWN + 2 + i))
                    down((U_DOWN + 1 + i) % 2, j * 2 + (2 + 2 * i), False, False, True)
            pe.wait_ge(S["lo_ready"], UNITS - 1)
            down((UNITS - 2) % 2, FT - 4, False, False, False)
            pe.wait_ge(S["lo_ready"], UNITS)
            down((UNITS - 1) % 2, FT - 2, False, True, False)
            for n in range(KD):
                pe.wait_ge(S["down_scaled"], n + 1)
                for t in range(TT):
                    ins = flip(bank[n][:, t * P:(t + 1) * P], up32[:, n % 2, t * P:(t + 1) * P])
                ins.then_inc(S["down_t"], 1)


INPUTS = ["x", "c", "positions", "w_ada", "b_ada", "norm_mix", "w_in", "ssm_log_dt", "ssm_a_re", "ssm_a_im",
          "ssm_b_re", "ssm_b_im", "ssm_c_re", "ssm_c_im", "ssm_d", "ssm_w_glu", "ssm_b_glu", "q_norm", "k_norm",
          "out_norm_ssm", "out_norm_attn", "w_out", "norm_ffn", "w_up", "conv_w", "conv_b", "w_down"]


def kernel(**inputs):
    import concourse.bacc as bacc
    from concourse.bass_utils import run_bass_kernel_spmd

    nc = bacc.Bacc("TRN2", target_bir_lowering=False, num_devices=1)
    arrays, args = {}, []
    given = [(n, inputs[n]) for n in INPUTS]
    given.append(("inv_freq", (10000.0 ** (-np.arange(0, HD, 2, dtype=np.float64) / HD)).astype(np.float32)[None]))
    for name, a in given:
        a = np.ascontiguousarray(a)
        arrays[f"in_{name}"] = a
        args.append(nc.dram_tensor(f"in_{name}", a.shape, mybir.dt.from_np(a.dtype), kind="ExternalInput").ap())
    out = nc.dram_tensor("out", (1, SEQ, D_MODEL), F32, kind="ExternalOutput").ap()
    layer(nc, *args, out)
    result = run_bass_kernel_spmd(nc, [arrays], core_ids=[0])
    return result.results[0]["out"]
```

```python
import math
from contextlib import ExitStack

import numpy as np
import concourse.bass as bass
from concourse import mybir

F32 = mybir.dt.float32
F32R = mybir.dt.float32r
I32 = mybir.dt.int32
ALU = mybir.AluOpType
ACT = mybir.ActivationFunctionType
AX = mybir.AxisListType.X

P = 128
SEQ, D_MODEL = 512, 1024
TT, KD = SEQ // P, D_MODEL // P
HEADS, HD = 8, 64
HALF = HD // 2
CH, GROUPS, STATE = 16, 32, 64
GP = GROUPS // 2
GH = GP // 2
NG = 2 * GH
CHUNK = 8
NCH = SEQ // CHUNK
TOPK = min(256, SEQ // 4)
D_FF, CONV_W = 2816, 3
FT = D_FF // P
UPS = FT // 2
EPS = 1e-6
ARENA = 26024
UNIT = 2048
TAIL = HD + HEADS
ATT_SCALE = 1.0 / math.sqrt(HD)
WI_SCALE = HEADS ** -0.5 * HD ** -0.5
MAGIC = 12582912.0
RSQRT_GUESS = 1597463007.0
TAKEN = -3.4028234663852886e38
FUTURE = -3.0e38
MASK = -1.0e30


def parts(x, bits, n):
    out = []
    for _ in range(n - 1):
        e = math.frexp(x)[1] - bits
        out.append(math.ldexp(float(round(math.ldexp(x, -e))), e))
        x -= out[-1]
    return out + [float(np.float32(x))]


TWO_PI = parts(2 * math.pi, 8, 4)
LN2 = parts(math.log(2.0), 12, 2)

U_TAIL, U_QI, U_U, U_K, U_Q, U_V, U_GLU, U_OUT = 0, 1, 3, 5, 7, 9, 11, 12
U_UP = U_OUT + 4
U_DOWN = U_UP + 2 * UPS
UNITS = U_DOWN + FT // 2
COLS = {U_U: 0, U_Q: 512, U_K: 1024, U_V: 1536, U_QI: 2048}


ATT_UNITS = TT * HEADS
S5_AT = {2: ("V", 0, 0), 3: ("V", 0, 1), 5: ("lags", 0, 0), 6: ("lags", 0, 1), 7: ("u", 0, 0), 8: ("states", 0, 0),
         12: ("y", 0, 0), 13: ("y", 0, 1), 14: ("V", 1, 0), 15: ("V", 1, 1), 16: ("lags", 1, 0), 17: ("lags", 1, 1),
         18: ("u", 1, 0), 19: ("states", 1, 0), 23: ("y", 1, 0), 24: ("y", 1, 1)}
MIX_ORDER = (4, 5, 6, 7, 0, 1, 2, 3)
LOGITS = 3


def layer(nc, x, c, positions, w_ada, b_ada, norm_mix, w_in, ssm_log_dt, ssm_a_re, ssm_a_im, ssm_b_re,
          ssm_b_im, ssm_c_re, ssm_c_im, ssm_d, ssm_w_glu, ssm_b_glu, q_norm, k_norm, out_norm_ssm,
          out_norm_attn, w_out, norm_ffn, w_up, conv_w, conv_b, w_down, inv_freq, out):
    u_dram = nc.dram_tensor("u_dram", (SEQ, 512), F32, kind="Internal").ap()
    y_dram = nc.dram_tensor("y_dram", (SEQ, 512), F32, kind="Internal").ap()
    lag_dram = nc.dram_tensor("lag_dram", (CH, GROUPS, 2 * CHUNK - 1, CH), F32, kind="Internal").ap()

    with ExitStack() as ctx:
        def sb(name, shape, dt=F32, stack=ctx):
            return stack.enter_context(nc.sbuf_tensor(name, shape, dt))

        def sem(name):
            return ctx.enter_context(nc.semaphore(name))

        bank = [ctx.enter_context(nc.psum_tensor(f"bank{i}", [P, 512], F32)) for i in range(8)]

        xh = sb("xh", [P, TT, D_MODEL])
        w_raw = sb("w_raw", [P, 2, UNIT])
        w_hi = sb("w_hi", [P, 2, UNIT], F32R)
        w_lo = sb("w_lo", [P, 2, UNIT], F32R)
        ident = sb("ident", [P, P])
        ones = sb("ones", [P, P])
        vec_cols = sb("vec_cols", [P, 296])
        c_col = sb("c_col", [P, 3, KD])
        mod_cols = sb("mod_cols", [P, 6, KD])
        silu_c = c_col[:, 1, :]
        scale1, shift1, gate1, shift2, scale2, gate2 = (mod_cols[:, i, :] for i in range(6))
        wi = sb("wi", [P, TT, HEADS])
        stat = sb("stat", [P, 640])
        up32 = sb("up32", [P, 2, 512])

        act_in = ExitStack()
        act_hi = sb("act_hi", [P, KD, SEQ], F32R, act_in)
        act_lo = sb("act_lo", [P, KD, SEQ], F32R, act_in)
        act_in.close()
        s5_mem = sb("s5_mem", [P, 8192])

        mixer = ExitStack()
        arena = sb("arena", [P, ARENA], stack=mixer)

        def cut(a, *shape):
            n = math.prod(shape)
            assert a + n <= ARENA
            v = arena[:, a:a + n]
            names = "abcd"[:len(shape)]
            if len(shape) == 1:
                return v
            return v.rearrange(f"p ({' '.join(names)}) -> p {' '.join(names)}",
                               **{k: s for k, s in zip(names, shape)})

        KEYS = [P * (t + 1) for t in range(TT)]
        KEYS_AT = [sum(KEYS[:t]) for t in range(TT)]
        q_t, k_t = cut(0, 4, SEQ), cut(2048, 4, SEQ)
        v_tok = cut(4096, TT, 512)
        y_attn, y_ssm = cut(6144, TT, 512), cut(8192, TT, 512)
        qi_t, ki_t = cut(10240, 4, SEQ), cut(12288, SEQ)
        pre, rot = cut(12800, TT, 512), cut(14848, TT, 512)
        tmp = cut(16896, 512)
        relu = cut(17408, 2, 512)
        diag = cut(17408, KD, P)
        score = [cut(19880 + KEYS_AT[t], KEYS[t]) for t in range(TT)]
        bias = [cut(21160, P)] + score[1:]
        rope = cut(22440, 6, TT, HD)
        g1_row = cut(23976, D_MODEL)
        vec_rows = cut(18432, 4, P)
        ki_w = cut(19616, TT, TAIL)
        b_g1_row = cut(0, D_MODEL)[0:1]
        d_bc = cut(25000, 512)[0:CH]
        b_glu_row = cut(25512, 512)[0:1]
        square_at = [up32[:].rearrange("p a n -> p (a n)"), cut(18944, D_MODEL)]
        ada_first = cut(0, 4, KD, 512)
        ada_first_acc = cut(16384, 4, 512)
        ada_next = [cut(0, KD, 512), cut(6144, KD, 512)]
        ada_next_acc = cut(23976, 2, 512)
        logit = cut(10240, LOGITS, 512)
        prob, prob_t = cut(14336, 2, 512), cut(15360, 2, 512)
        lag_w = [cut(16384, 2, GH, CHUNK + 1, CH), cut(12032, 2, GH, CHUNK + 1, CH)]
        turn = cut(8192, 2, GP, NCH)
        s5_b, s5_c = cut(21288, 2, GP, CH), cut(21800, 2, GP, CH)
        power = cut(19072, 2, CHUNK + 1, GP)
        power_back = cut(19360, 2, CHUNK, GP)
        s5_bb = cut(22440, 2, GP, CH)
        s5_p = cut(18688, 24, GP)
        scan_r = cut(23336, GH, NCH)
        s5_v = [s5_mem[:, a:a + 2048].rearrange("p (g r n) -> p g r n", g=GH, r=2) for a in (0, 2048)]
        s5_vt = [s5_mem[:, a:a + 2048].rearrange("p (r g j h) -> p r g j h", r=2, g=GH, j=CHUNK) for a in (2048, 0)]
        s5_m = [s5_mem[:, a:a + 2048].rearrange("p (g n) -> p g n", g=NG) for a in (2048, 0)]
        s5_u = s5_mem[:, 4096:5120].rearrange("p (g n) -> p g n", g=NG)
        s5_z = s5_mem[:, 5120:6144].rearrange("p (r n) -> p r n", r=2)
        lags = s5_mem[0:CH, 4096:6144].rearrange("p (g l h) -> p g l h", g=NG, l=CHUNK)
        def lags_of(i):
            return lags.rearrange("p (b c q) l h -> p b q c l h", b=2, q=2)[:, i // 2, i % 2]
        c_rows = xh[:, 0:2, :].rearrange("p t n -> p (t n)")[:, 0:1024].rearrange(
            "p (r a q n) -> p r a q n", r=2, a=4, q=2)
        s5_x = s5_mem[:, 6144:7168].rearrange("p (r g n) -> p r g n", r=2, g=GH)
        s5_t = s5_mem[:, 7168:8192].rearrange("p (r n) -> p r n", r=2)
        square_to = [logit[:, i] for i in range(2)]
        chunk_rows = xh[0:NCH, :, :].rearrange("c a n -> c (a n)")
        chunk_in = chunk_rows.rearrange("c (i n) -> c i n", i=CHUNK)
        group_in = xh[NCH:2 * NCH, :, :].rearrange("c a n -> c (a n)").rearrange("c (g m) -> c g m", g=GROUPS)
        hn_tok = cut(0, TT, D_MODEL)
        mixer.close()

        ff_hi = sb("ff_hi", [P, FT, SEQ], F32R)
        ff_lo = sb("ff_lo", [P, FT, SEQ], F32R)
        conv = sb("conv", [P, 4, SEQ])

        ss_x, rstd_x = stat[:, 0:4], stat[:, 4:8]
        ss_qk, rstd_qk = stat[:, 8:72], stat[:, 72:136]
        top8 = stat[:, 136:144]
        neg_max = stat[:, 144:176]
        psum_p = stat[:, 176:208]
        q_scale = stat[:, 208:240]
        ss_y, rstd_y = stat[:, 240:248], stat[:, 248:256]
        work = stat[:, 256:384]
        ss_h, rstd_h = stat[:, 384:388], stat[:, 388:392]
        rinv = stat[:, 392:424]
        pos_f = stat[:, 424:428]
        pos_i = stat[:, 428:432].bitcast(I32)
        inv_bc = stat[:, 432:464]
        gq_bc, gk_bc = stat[:, 464:528], stat[:, 528:592]
        dt_rows = stat[:, 592:594]

        C_BADA, C_NMIX, C_NFFN, C_NSSM, C_NATT, C_W0, C_W1, C_W2, C_CB, C_ARE, C_AIM, C_LDT = (
            0, 48, 56, 64, 68, 72, 116, 160, 204, 248, 264, 280)

        S = {n: sem(n) for n in (
            "ident_ready", "ones_ready", "rows_loaded", "dt_spread", "vec_t", "c_loaded", "pos_loaded",
            "bc_loaded", "x_loaded", "ss_x_ready", "rstd_x_ready", "xn_ready", "tanh_c", "silu_ready", "angle_ready", "sin_ready",
            "ada_first_loaded0", "ada_first_loaded1", "ada_first_loaded2", "ada_first_loaded3",
            "ada_acc_ready", "mod_ready", "mod1_ready", "x_t_ready", "x_t_read", "act_in_ready",
            "raw_loaded0", "raw_loaded1", "hi_ready", "lo_ready", "weights_used",
            "proj_ready", "proj_read", "rot_ready", "turned_ready", "turned_read", "u_stored",
            "ada_next_loaded0", "ada_next_loaded1", "ada_used", "ada_sum_ready", "ada_sum_read",
            "ss_qk_ready", "sq_used", "score_mm", "relu_ready", "relu_used", "future_set",
            "bias_ready", "logit_mm", "logit_ready", "prob_ready", "prob_turned", "prob_t_ready", "pv_done",
            "pv_read", "y_attn_ready", "u_loaded", "u_grouped", "s5_loaded", "c_rows_loaded", "lag_w_ready", "turn_ready", "diag_ready", "ada_sums_read", "g1_spread", "g1_read", "c_t", "c_t_read", "s5_angle", "s5_sin", "s5_params",
            "vt_ready", "v_t", "v_ready", "lag_mm", "lags_ready", "lags_stored", "zeros_stored", "m_loaded",
            "zero_ready", "lag_d_added", "u_t", "u_t_read", "state_mm", "state_read", "s5_state", "y_mm", "y_read", "y_stored",
            "y_loaded", "gelu_ready", "g_t", "g_t_read", "glu_in", "glu_mm", "tanh_z", "glu_read", "y_ssm_ready",
            "ss_y_ready", "yn_ready", "mix_t", "mix_t_read", "mix_in", "out_mm", "h_ready", "ss_h_ready",
            "hn_ready", "h_t", "h_t_read", "mlp_in", "up_mm", "tap_ready", "conv_read", "conv_ready",
            "gelu_up", "ff32_ready", "ff_hi_ready", "ff_lo_ready", "down_mm", "down_scaled", "down_t",
            "sum_ready", "stored", "dve_chain", "act_chain", "pool_chain", "d_loaded", "x_again", "b_rows_loaded",
        )}

        def unit_view(buf, n, *shape):
            k, m = shape
            return buf[:, n % 2, 0:k * m].rearrange("p (k m) -> p k m", k=k)

        block = ctx.enter_context(nc.Block())

        @block.sync
        def _(sp):
            def load(dst, src, s):
                sp.dma_start(dst, src).then_inc(S[s], 16)

            def unit(n, dst, src):
                if n >= 2:
                    sp.wait_ge(S["lo_ready"], n - 1)
                sp.dma_start(dst, src).then_inc(S[f"raw_loaded{n % 2}"], 16)

            load(c_col[:, 0, :], c.rearrange("a (p k) -> p (a k)", p=P), "c_loaded")
            for t in range(TT):
                load(xh[:, t, :], x[0, t * P:(t + 1) * P, :], "x_loaded")
            sp.dma_start(pos_i, positions[0].rearrange("(a p) -> p a", p=P), allow_slow_non_contiguous=True
                         ).then_inc(S["pos_loaded"], 16)
            load(inv_bc, inv_freq[0].partition_broadcast(P), "bc_loaded")
            load(gq_bc, q_norm[0].partition_broadcast(P), "bc_loaded")
            load(gk_bc, k_norm[0].partition_broadcast(P), "bc_loaded")
            rows = lambda v, n: v.rearrange("(a p) -> a p", a=n)
            load(vec_rows[0:48, 0, :], rows(b_ada[0], 48), "rows_loaded")
            load(vec_rows[48:56, 0, :], rows(norm_mix[0], KD), "rows_loaded")
            load(vec_rows[56:64, 0, :], rows(norm_ffn[0], KD), "rows_loaded")
            load(vec_rows[64:68, 0, :], rows(out_norm_ssm[0], 4), "rows_loaded")
            load(vec_rows[68:72, 0, :], rows(out_norm_attn[0], 4), "rows_loaded")
            load(vec_rows[0:88, 1, :], conv_w[0, 0:2, :].rearrange("j (a p) -> (j a) p", p=P), "rows_loaded")
            load(vec_rows[0:44, 2, :], rows(conv_w[0, 2, :], 44), "rows_loaded")
            load(vec_rows[44:88, 2, :], rows(conv_b[0], 44), "rows_loaded")
            load(vec_rows[0:GP, 3, :], ssm_a_re[0].rearrange("(g q) p -> g (q p)", q=2), "rows_loaded")
            load(vec_rows[GP:2 * GP, 3, :], ssm_a_im[0].rearrange("(g q) p -> g (q p)", q=2), "rows_loaded")
            load(dt_rows[32:32 + GP, :], ssm_log_dt[0].rearrange("(g q) -> g q", q=2), "rows_loaded")
            load(b_glu_row, ssm_b_glu, "b_rows_loaded")
            load(d_bc, ssm_d[0].partition_broadcast(CH), "d_loaded")
            wa = w_ada[0].rearrange("(p k) n -> p k n", k=KD)
            for i in range(4):
                load(ada_first[:, i], wa[:, :, i * 512:(i + 1) * 512], f"ada_first_loaded{i}")
            sp.wait_ge(S["zero_ready"], 1)
            for i in range(2):
                sp.dma_start(lag_dram[:, NG * i:NG * (i + 1), 0:CHUNK - 1, :],
                             s5_mem[0:CH, 0:NG * (CHUNK - 1) * CH].rearrange("p (g l h) -> p g l h", g=NG, l=CHUNK - 1)
                             ).then_inc(S["zeros_stored"], 16)

            w_in_k = w_in[0].rearrange("(k p) n -> p k n", p=P)
            unit(U_TAIL, unit_view(w_raw, U_TAIL, KD, TAIL), w_in_k[:, :, 2560:2560 + TAIL])

            def later_ada(first, last):
                for n in range(first, last):
                    if n < 2:
                        sp.wait_ge(S["ada_acc_ready"], 4)
                    else:
                        sp.wait_ge(S["ada_used"], n - 1)
                    a = 2048 + 512 * n
                    load(ada_next[n % 2], wa[:, :, a:a + 512], f"ada_next_loaded{n % 2}")

            pieces = {U_QI: (0, 1), U_QI + 1: (1, 2), U_U: (2, 4), U_U + 1: (4, 6), U_K: (6, 8)}
            for n0 in (U_QI, U_U, U_K, U_Q, U_V):
                for kh in range(2):
                    unit(n0 + kh, unit_view(w_raw, n0 + kh, 4, 512),
                         w_in_k[:, 4 * kh:4 * kh + 4, COLS[n0]:COLS[n0] + 512])
                    later_ada(*pieces.get(n0 + kh, (0, 0)))
                if n0 == U_QI:
                    sp.wait_ge(S["x_t_ready"], KD)
                    for i, (bsrc, csrc) in enumerate(((ssm_b_re, ssm_c_re), (ssm_b_im, ssm_c_im))):
                        for q in range(2):
                            load(c_rows[:, i, :, q, :], csrc[0].rearrange("(a g) h p -> (g h) a p", a=4), "c_rows_loaded")
                        load(s5_b[:, i], bsrc[0].rearrange("(g q) p h -> (q p) g h", q=2), "s5_loaded")
                if n0 == U_K:
                    for t in range(TT):
                        sp.wait_ge(S["proj_read"], 4 * 2 + t + 1)
                        sp.dma_start(u_dram[t * P:(t + 1) * P, :], v_tok[:, t, :]).then_inc(S["u_stored"], 16)
            unit(U_GLU, unit_view(w_raw, U_GLU, 4, 512), ssm_w_glu[0].rearrange("(k p) n -> p k n", p=P))
            w_out_k = w_out[0].rearrange("(k p) n -> p k n", p=P)
            unit(U_OUT, unit_view(w_raw, U_OUT, 4, 512), w_out_k[:, 0:4, 0:512])

            sp.wait_ge(S["c_t"], 1)
            sp.wait_ge(S["u_stored"], 16 * TT)
            load(chunk_rows, u_dram.rearrange("(c i) n -> c (i n)", i=CHUNK), "u_loaded")
            sp.wait_ge(S["zeros_stored"], 32)
            for half in range(2):
                sp.wait_ge(S["lag_d_added"], 4 * half + 4)
                gs = slice(NG * half, NG * (half + 1))
                sp.dma_start(lag_dram[:, gs, CHUNK - 1:, :], lags).then_inc(S["lags_stored"], 16)
                sp.wait_ge(S["lags_stored"], 16 * (half + 1))
                sp.wait_ge(S["v_ready"], 4 * half + 4)
                for j in range(CHUNK):
                    load(s5_m[half][CH * j:CH * (j + 1)].rearrange("p g (l h) -> p g l h", l=CHUNK),
                         lag_dram[:, gs, CHUNK - 1 - j:2 * CHUNK - 1 - j, :], "m_loaded")
            sp.wait_ge(S["y_read"], 8)
            sp.dma_start(y_dram.rearrange("(c i) n -> c (i n)", i=CHUNK), chunk_rows).then_inc(S["y_stored"], 16)
            sp.wait_ge(S["y_stored"], 16)
            load(y_ssm, y_dram.rearrange("(a p) n -> p a n", p=P), "y_loaded")
            for t in range(TT):
                load(xh[:, t, :], x[0, t * P:(t + 1) * P, :], "x_again")

            for n in range(2):
                for kh in range(2):
                    i = U_OUT + 2 * n + kh
                    if i > U_OUT:
                        unit(i, unit_view(w_raw, i, 4, 512), w_out_k[:, 4 * kh:4 * kh + 4, 512 * n:512 * n + 512])

            w_up_k = w_up[0].rearrange("(k p) (s n) -> p k s n", p=P, s=2)
            with sp.Fori(0, UPS) as j:
                for kh in range(2):
                    sp.wait_ge(S["lo_ready"], j * 2 + (U_UP + kh - 1))
                    for s in range(2):
                        sp.dma_start(w_raw[:, (U_UP + kh) % 2, :].rearrange("p (k s n) -> p k s n", k=4, s=2)[:, :, s, :],
                                     w_up_k[:, 4 * kh:4 * kh + 4, s, bass.ds(j * 256, 256)]
                                     ).then_inc(S[f"raw_loaded{(U_UP + kh) % 2}"], 16)
            with sp.Fori(0, FT // 2 - 1, 2) as j:
                for i in range(2):
                    sp.wait_ge(S["lo_ready"], j + (U_DOWN + i - 1))
                    for k in range(2):
                        sp.dma_start(w_raw[:, (U_DOWN + i) % 2, 1024 * k:1024 * k + 1024],
                                     w_down[0][bass.ds(j * 256 + (256 * i + P * k), P), :]
                                     ).then_inc(S[f"raw_loaded{(U_DOWN + i) % 2}"], 16)
            sp.wait_ge(S["lo_ready"], UNITS - 2)
            for k in range(2):
                sp.dma_start(w_raw[:, (UNITS - 1) % 2, 1024 * k:1024 * k + 1024],
                             w_down[0, (FT - 2 + k) * P:(FT - 1 + k) * P, :]
                             ).then_inc(S[f"raw_loaded{(UNITS - 1) % 2}"], 16)
            for n in range(4):
                sp.wait_ge(S["sum_ready"], 2 * n + 2)
                sp.dma_start(out[0].rearrange("(a p) n -> p a n", p=P)[:, :, 256 * n:256 * n + 256],
                             xh[:, :, 256 * n:256 * n + 256]).then_inc(S["stored"], 16)
            sp.wait_ge(S["stored"], 64)

        def raw_count(n):
            total = 0
            for i in range(n % 2, n + 1, 2):
                total += 2 if i >= U_UP else 1
            return 16 * total

        @block.gpsimd
        def _(pool):
            G = nc.gpsimd
            chain = [0]

            def link(ins):
                chain[0] += 1
                ins.then_inc(S["pool_chain"], 1)
                pool.wait_ge(S["pool_chain"], chain[0])

            def lo(slot, width=UNIT):
                nc.gpsimd.tensor_tensor(w_lo[:, slot, 0:width], w_raw[:, slot, 0:width],
                                        w_hi[:, slot, 0:width].bitcast(F32), ALU.subtract).then_inc(S["lo_ready"], 1)

            link(nc.gpsimd.memset(ident[:], 0.0))
            nc.gpsimd.affine_select(out=ident[:], in_=ident[:], compare_op=ALU.not_equal, fill=1.0, base=0,
                                    pattern=[[-1, P]], channel_multiplier=1).then_inc(S["ident_ready"], 1)
            nc.gpsimd.memset(ones[:], 1.0).then_inc(S["ones_ready"], 1)
            nc.gpsimd.memset(s5_mem[:, 0:2048], 0.0).then_inc(S["zero_ready"], 1)
            link(nc.gpsimd.memset(bias[0], 0.0))
            link(nc.gpsimd.affine_select(out=bias[0], in_=bias[0], compare_op=ALU.is_ge, fill=MASK, base=0,
                                         pattern=[[-1, P]], channel_multiplier=1))

            def future(t):
                pool.wait_ge(S["relu_used"], HEADS * t)
                diag = score[t][:, t * P:(t + 1) * P]
                nc.gpsimd.affine_select(out=diag, in_=diag, compare_op=ALU.is_ge, fill=FUTURE, base=0,
                                        pattern=[[-1, P]], channel_multiplier=1).then_inc(S["future_set"], 1)

            def weigh_lags(half):
                gs = slice(GH * half, GH * (half + 1))
                w = lag_w[half]
                t1 = up32[:].rearrange("p a n -> p (a n)").rearrange("p (g l h) -> p g l h", g=GH, l=CHUNK)
                cr, ci = (s5_c[:, i, gs].unsqueeze(2).broadcast_to([P, GH, CHUNK, CH]) for i in range(2))
                pr, pi = (power[:, i, 1:, gs].rearrange("p l g -> p g l").unsqueeze(3).broadcast_to([P, GH, CHUNK, CH])
                          for i in range(2))
                o_r, o_i = w[:, 0, :, 1:, :], w[:, 1, :, 1:, :]
                G.tensor_copy(w[:, 0, :, 0, :], s5_c[:, 0, gs])
                G.tensor_scalar(w[:, 1, :, 0, :], s5_c[:, 1, gs], -1.0, None, ALU.mult)
                G.tensor_tensor(o_r, cr, pr, ALU.mult)
                link(G.tensor_tensor(t1, ci, pi, ALU.mult))
                link(G.tensor_tensor(o_r, o_r, t1, ALU.subtract))
                G.tensor_tensor(o_i, cr, pi, ALU.mult)
                link(G.tensor_tensor(t1, ci, pr, ALU.mult))
                link(G.tensor_tensor(o_i, o_i, t1, ALU.add))
                G.tensor_scalar(o_i, o_i, -1.0, None, ALU.mult).then_inc(S["lag_w_ready"], 1)

            def turn_step(n):
                w1, w2, w3, w4, q1, q2 = (s5_p[:, i] for i in (20, 21, 22, 23, 4, 5))
                if n == 1:
                    pool.wait_ge(S["s5_params"], 1)
                    pool.wait_ge(S["ada_used"], 8)
                    G.memset(turn[:, 0, :, 0:1], 1.0)
                    G.memset(turn[:, 1, :, 0:1], 0.0)
                    G.tensor_copy(w3, s5_p[:, 17])
                    link(G.tensor_copy(w4, s5_p[:, 18]))
                t1, t2 = (y_attn[:, i, 0:GP * n].rearrange("p (g c) -> p g c", g=GP) for i in range(2))
                a_r, a_i = turn[:, 0, :, 0:n], turn[:, 1, :, 0:n]
                o_r, o_i = turn[:, 0, :, n:2 * n], turn[:, 1, :, n:2 * n]
                f_r, f_i = (v.unsqueeze(2).broadcast_to([P, GP, n]) for v in (w3, w4))
                G.tensor_tensor(o_r, a_r, f_r, ALU.mult)
                G.tensor_tensor(t1, a_i, f_i, ALU.mult)
                G.tensor_tensor(o_i, a_r, f_i, ALU.mult)
                G.tensor_tensor(t2, a_i, f_r, ALU.mult)
                G.tensor_tensor(w1, w3, w3, ALU.mult)
                G.tensor_tensor(w2, w4, w4, ALU.mult)
                link(G.tensor_tensor(q1, w3, w4, ALU.mult))
                G.tensor_tensor(o_r, o_r, t1, ALU.subtract)
                ins = G.tensor_tensor(o_i, o_i, t2, ALU.add)
                if 2 * n == NCH:
                    ins.then_inc(S["turn_ready"], 1)
                    return
                G.tensor_tensor(w3, w1, w2, ALU.subtract)
                link(G.tensor_tensor(w4, q1, q1, ALU.add))

            for n in range(U_UP):
                pool.wait_ge(S["hi_ready"], n + 1)
                lo(n % 2, KD * TAIL if n == U_TAIL else UNIT)
                if n == U_K:
                    for t in range(1, TT):
                        future(t)
                if U_Q <= n <= U_V:
                    for i in (2 * (n - U_Q), 2 * (n - U_Q) + 1):
                        turn_step(2 ** i)
                if n == U_OUT:
                    pool.wait_ge(S["turned_ready"], 13)
                    pool.wait_ge(S["g1_spread"], 1)
                    for half in range(2):
                        weigh_lags(half)
            with pool.Fori(0, 2 * UPS + 10, 2) as j:
                for i in range(2):
                    pool.wait_ge(S["hi_ready"], j + (U_UP + i + 1))
                    lo((U_UP + i) % 2)
            pool.wait_ge(S["hi_ready"], UNITS)
            lo((UNITS - 1) % 2)

        @block.scalar
        def _(act):
            chain = [0]

            def link(ins):
                chain[0] += 1
                ins.then_inc(S["act_chain"], 1)
                act.wait_ge(S["act_chain"], chain[0])

            def hi(n, width=UNIT):
                act.wait_ge(S[f"raw_loaded{n % 2}"], raw_count(n))
                if n >= 2:
                    act.wait_ge(S["weights_used"], n - 1)
                nc.scalar.activation(w_hi[:, n % 2, 0:width], w_raw[:, n % 2, 0:width], ACT.Copy
                                     ).then_inc(S["hi_ready"], 1)

            act.wait_ge(S["c_loaded"], 16)
            nc.scalar.activation(c_col[:, 2, :], c_col[:, 0, :], ACT.Tanh, scale=0.5).then_inc(S["tanh_c"], 1)
            act.wait_ge(S["x_loaded"], 16 * TT)
            for t in range(TT):
                if t >= 2:
                    act.wait_ge(S["ss_x_ready"], t - 1)
                nc.scalar.activation(square_at[t % 2], xh[:, t, :], ACT.Square,
                                     accum_out=ss_x[:, t:t + 1]).then_inc(S["ss_x_ready"], 1)
            act.wait_ge(S["angle_ready"], 1)
            nc.scalar.activation(rope[:, 1], rope[:, 3], ACT.Sin).then_inc(S["sin_ready"], 1)
            nc.scalar.activation(rope[:, 0], rope[:, 2], ACT.Sin).then_inc(S["sin_ready"], 1)
            act.wait_ge(S["rstd_x_ready"], 1)
            for t in range(TT):
                nc.scalar.activation(xh[:, t, :], xh[:, t, :], ACT.Copy, scale=rstd_x[:, t:t + 1]
                                     ).then_inc(S["xn_ready"], 1)
            hi(U_TAIL, KD * TAIL)
            hi(U_QI)
            act.wait_ge(S["mod1_ready"], 1)
            for k in range(KD):
                act.wait_ge(S["x_t_ready"], k + 1)
                if k >= 2:
                    act.wait_ge(S["act_in_ready"], k - 1)
                nc.scalar.activation(up32[:, k % 2, :], bank[k % 4][:], ACT.Identity, scale=scale1[:, k:k + 1],
                                     bias=shift1[:, k:k + 1]).then_inc(S["x_t_read"], 1)
            act.wait_ge(S["s5_angle"], 1)
            nc.scalar.activation(s5_p[:, 8:10], s5_p[:, 6:8], ACT.Sin).then_inc(S["s5_sin"], 1)

            def results(nth, n_last, dst, width=512, before=None):
                for t in range(TT):
                    if t < TT - 1:
                        act.wait_ge(S["proj_ready"], 3 * nth + t + 1)
                    else:
                        act.wait_ge(S["weights_used"], n_last + 1)
                    if before is not None:
                        before(t)
                    nc.scalar.activation(dst[:, t, 0:width], bank[t][:, 0:width], ACT.Copy).then_inc(S["proj_read"], 1)

            turned = [0]

            def turned_read(dst):
                for t in range(TT):
                    act.wait_ge(S["turned_ready"], turned[0] + 1)
                    nc.scalar.activation(dst[:, :, t * P:(t + 1) * P],
                                         bank[4 + turned[0] % 2][:].rearrange("p (g t) -> p g t", g=4), ACT.Copy
                                         ).then_inc(S["turned_read"], 1)
                    turned[0] += 1

            def squares(which):
                for t in range(TT):
                    n = 4 * which + t
                    act.wait_ge(S["proj_read"], 4 * (3 + which) + t + 1)
                    if n >= 2:
                        act.wait_ge(S["sq_used"], n - 1)
                    nc.scalar.activation(up32[:, n % 2, :], pre[:, t, :], ACT.Square).then_inc(S["ss_qk_ready"], 1)

            results(0, U_TAIL, ki_w, TAIL)
            hi(U_QI + 1)
            hi(U_U)
            results(1, U_QI + 1, pre)
            hi(U_U + 1)
            hi(U_K)
            results(2, U_U + 1, v_tok)
            hi(U_K + 1)
            act.wait_ge(S["c_t"], 1)
            for r in range(2):
                for q in range(2):
                    hp = slice(64 * q, 64 * q + 64)
                    nc.scalar.activation(s5_c[hp, r],
                                         bank[5 + r][hp, :].rearrange("p (g q h) -> p g q h", g=GP, q=2)[:, :, q, :],
                                         ACT.Copy).then_inc(S["c_t_read"], 1)
            act.wait_ge(S["turned_ready"], 1)
            nc.scalar.activation(ki_t, bank[4][:], ACT.Copy).then_inc(S["turned_read"], 1)
            turned[0] = 1
            turned_read(qi_t)
            for i in range((TT - 1) * HEADS):
                t = 1 + i // HEADS
                act.wait_ge(S["score_mm"], i + 1)
                if i >= 2:
                    act.wait_ge(S["relu_used"], i - 1)
                nc.scalar.activation(relu[:, i % 2, 0:KEYS[t]], bank[6 + i % 2][:, 0:KEYS[t]], ACT.Relu
                                     ).then_inc(S["relu_ready"], 1)
            hi(U_Q)
            results(3, U_K + 1, pre, before=lambda t: act.wait_ge(S["rot_ready"], 1 + t + 1))
            squares(0)
            hi(U_Q + 1)
            hi(U_V)
            results(4, U_Q + 1, pre, before=lambda t: act.wait_ge(S["rot_ready"], 5 + t + 1))
            turned_read(k_t)
            squares(1)
            hi(U_V + 1)
            hi(U_GLU)
            results(5, U_V + 1, v_tok, before=lambda t: act.wait_ge(S["u_stored"], 16 * TT))
            turned_read(q_t)
            hi(U_OUT)

            act.wait_ge(S["u_loaded"], 16)
            for i in range(2):
                gs = slice(NG * i, NG * (i + 1))
                nc.scalar.activation(
                    group_in[:, gs, :].rearrange("c g (i h) -> c g i h", i=CHUNK),
                    chunk_in.rearrange("c i (g h) -> c g i h", g=GROUPS)[:, gs], ACT.Copy).then_inc(S["u_grouped"], 1)

            def s5(stage, half, part):
                for i in (2 * part, 2 * part + 1):
                    src = bank[6 + i % 2]
                    if stage == "V":
                        act.wait_ge(S["v_t"], 4 * half + i + 1)
                        if i == 0:
                            act.wait_ge(S["zeros_stored"], 32)
                            if half:
                                act.wait_ge(S["y_mm"], 4)
                        nc.scalar.activation(s5_v[half][:, 2 * i:2 * i + 2],
                                             src[:].rearrange("p (g r n) -> p g r n", g=2, r=2), ACT.Copy
                                             ).then_inc(S["v_ready"], 1)
                    elif stage == "lags":
                        act.wait_ge(S["lag_mm"], 4 * half + i + 1)
                        if i == 0 and half:
                            act.wait_ge(S["y_mm"], 4)
                        nc.scalar.activation(lags_of(i), src[0:CH, :].rearrange("p (g l h) -> p g l h", g=4, l=CHUNK),
                                             ACT.Copy).then_inc(S["lags_ready"], 1)
                    elif stage == "u":
                        act.wait_ge(S["u_t"], 2 * half + i + 1)
                        if i == 0:
                            act.wait_ge(S["lags_stored"], 16 * (half + 1))
                        nc.scalar.activation(s5_u[:, 8 * i:8 * i + 8], src[:].rearrange("p (g n) -> p g n", g=8),
                                             ACT.Copy).then_inc(S["u_t_read"], 1)
                    elif stage == "y":
                        act.wait_ge(S["y_mm"], 4 * half + i + 1)
                        for c in range(4):
                            g = NG * half + 8 * (i // 2) + 2 * c + i % 2
                            ins = nc.scalar.activation(
                                chunk_in[:, :, g * CH:(g + 1) * CH],
                                src[0:NCH, c * P:(c + 1) * P].rearrange("c (i h) -> c i h", i=CHUNK), ACT.Copy)
                        ins.then_inc(S["y_read"], 1)

            for i in range(ATT_UNITS):
                t = i // HEADS
                act.wait_ge(S["logit_ready"], i + 1)
                if i >= 2:
                    act.wait_ge(S["prob_turned"], i - 1)
                nc.scalar.activation(prob[:, i % 2, 0:KEYS[t]], logit[:, i % LOGITS, 0:KEYS[t]], ACT.Exp, scale=-1.0,
                                     bias=neg_max[:, i:i + 1], accum_out=psum_p[:, i:i + 1]
                                     ).then_inc(S["prob_ready"], 1)
                if i in S5_AT:
                    s5(*S5_AT[i])

            act.wait_ge(S["y_loaded"], 16)
            for t in range(TT):
                nc.scalar.activation(y_ssm[:, t, :], y_ssm[:, t, :], ACT.Gelu_apprx_tanh).then_inc(S["gelu_ready"], 1)
            for k in range(4):
                act.wait_ge(S["g_t"], k + 1)
                if k >= 2:
                    act.wait_ge(S["glu_in"], k - 1)
                nc.scalar.activation(up32[:, k % 2, :], bank[k][:], ACT.Copy).then_inc(S["g_t_read"], 1)
            for t in range(TT):
                act.wait_ge(S["y_attn_ready"], t + 1)
                if t >= 1:
                    act.wait_ge(S["ss_y_ready"], t)
                nc.scalar.activation(square_to[t % 2], y_attn[:, t, :], ACT.Square,
                                     accum_out=ss_y[:, TT + t:TT + t + 1]).then_inc(S["ss_y_ready"], 1)
            for t in range(TT):
                act.wait_ge(S["glu_mm"], t + 1)
                if t >= 2:
                    act.wait_ge(S["glu_read"], t - 1)
                if t == 0:
                    act.wait_ge(S["glu_in"], 4)
                nc.scalar.activation(up32[:, t % 2, :], bank[4 + t][:], ACT.Tanh, scale=0.5).then_inc(S["tanh_z"], 1)
            hi(U_OUT + 1)
            for t in range(TT):
                act.wait_ge(S["glu_read"], t + 1)
                nc.scalar.activation(square_to[t % 2], y_ssm[:, t, :], ACT.Square,
                                     accum_out=ss_y[:, t:t + 1]).then_inc(S["ss_y_ready"], 1)
                if t >= 1:
                    act.wait_ge(S["ss_y_ready"], TT + t)
            for k in MIX_ORDER:
                n = MIX_ORDER.index(k)
                act.wait_ge(S["mix_t"], n + 1)
                if n >= 2:
                    act.wait_ge(S["mix_in"], n - 1)
                nc.scalar.activation(up32[:, n % 2, :], bank[n % 4][:], ACT.Copy,
                                     scale=vec_cols[:, C_NSSM + k:C_NSSM + k + 1]).then_inc(S["mix_t_read"], 1)
            hi(U_OUT + 2)
            hi(U_OUT + 3)
            for t in range(TT):
                act.wait_ge(S["h_ready"], TT + t + 1)
                if t == 0:
                    act.wait_ge(S["mix_in"], KD)
                if t >= 2:
                    act.wait_ge(S["ss_h_ready"], t - 1)
                nc.scalar.activation(square_at[t % 2], xh[:, t, :], ACT.Square,
                                     accum_out=ss_h[:, t:t + 1]).then_inc(S["ss_h_ready"], 1)
            hi(U_UP)
            hi(U_UP + 1)
            for k in range(KD):
                act.wait_ge(S["h_t"], k + 1)
                if k >= 2:
                    act.wait_ge(S["mlp_in"], k - 1)
                nc.scalar.activation(up32[:, k % 2, :], bank[k % 4][:], ACT.Identity, scale=scale2[:, k:k + 1],
                                     bias=shift2[:, k:k + 1]).then_inc(S["h_t_read"], 1)
            act.wait_ge(S["mlp_in"], KD)

            def hi_ahead(j, kh):
                act.wait_ge(S[f"raw_loaded{kh}"], j * 32 + (raw_count(U_UP + kh) + 32))
                act.wait_ge(S["weights_used"], j * 2 + (U_UP + kh + 1))
                nc.scalar.activation(w_hi[:, kh, :], w_raw[:, kh, :], ACT.Copy).then_inc(S["hi_ready"], 1)

            with act.Fori(0, UPS) as j:
                hi_ahead(j, 0)
                for q in range(4):
                    f = (0, 1, FT, FT + 1)[q]
                    if q < 3:
                        act.wait_ge(S["up_mm"], j * 3 + (q + 1))
                    else:
                        act.wait_ge(S["weights_used"], j * 2 + (U_UP + 2))
                    nc.scalar.activation(conv[:, q, :], bank[q][:], ACT.Identity,
                                         scale=vec_cols[:, bass.ds(j * 2 + (C_W2 + f), 1)],
                                         bias=vec_cols[:, bass.ds(j * 2 + (C_CB + f), 1)]
                                         ).then_inc(S["tap_ready"], 1)
                hi_ahead(j, 1)
                for q in range(2):
                    act.wait_ge(S["conv_ready"], j * 4 + (q + 1))
                    nc.scalar.activation(conv[:, q, :], conv[:, q, :], ACT.Gelu_apprx_tanh
                                         ).then_inc(S["gelu_up"], 1)
                for q in range(2):
                    act.wait_ge(S["ff32_ready"], j * 2 + (q + 1))
                    nc.scalar.activation(ff_hi[:, bass.ds(j * 2 + q, 1), :].rearrange("p a t -> p (a t)"),
                                         up32[:, q, :], ACT.Copy).then_inc(S["ff_hi_ready"], 1)
            for n in range(U_DOWN + 2, UNITS):
                hi(n)
            for n in range(KD):
                act.wait_ge(S["down_mm"], n + 1)
                if n >= 2:
                    act.wait_ge(S["down_t"], n - 1)
                nc.scalar.activation(up32[:, n % 2, :], bank[n][:], ACT.Copy, scale=gate2[:, n:n + 1]
                                     ).then_inc(S["down_scaled"], 1)

        @block.vector
        def _(dve):
            V = nc.vector
            count = {}

            def link(ins, s="dve_chain"):
                count[s] = count.get(s, 0) + 1
                ins.then_inc(S[s], 1)
                dve.wait_ge(S[s], count[s])

            def signal(ins, s):
                count[s] = count.get(s, 0) + 1
                ins.then_inc(S[s], 1)

            def rsqrt(y, v, t, s="dve_chain"):
                link(V.tensor_scalar(y.bitcast(I32), v.bitcast(I32), 1, None, ALU.logical_shift_right))
                link(V.tensor_scalar(y.bitcast(I32), y.bitcast(I32), -1.0, RSQRT_GUESS, ALU.mult, ALU.add))
                for n in range(4):
                    link(V.scalar_tensor_tensor(t, y, 1.0, y, ALU.mult, ALU.mult))
                    link(V.scalar_tensor_tensor(t, t, -0.5, v, ALU.mult, ALU.mult))
                    link(V.scalar_tensor_tensor(y, t, 1.5, y, ALU.add, ALU.mult), s if n == 3 else "dve_chain")

            def reduce_angle(r, k):
                link(V.tensor_scalar(k, r, 1 / (2 * math.pi), MAGIC, ALU.mult, ALU.add))
                link(V.tensor_scalar(k, k, -MAGIC, None, ALU.add))
                for part in TWO_PI:
                    link(V.scalar_tensor_tensor(r, k, -part, r, ALU.mult, ALU.add))
                pi = float(np.nextafter(np.float32(math.pi), np.float32(0)))
                link(V.tensor_scalar(r, r, pi, -pi, ALU.min, ALU.max))

            def cos_angle(out, r, s):
                link(V.scalar_tensor_tensor(out, r, -1.0, r, ALU.mult, ALU.min))
                link(V.tensor_scalar(out, out, math.pi / 2, None, ALU.add), s)

            def exp(y, x, k, k1, r):
                link(V.tensor_scalar(r, x, -174.0, 178.0, ALU.max, ALU.min))
                link(V.tensor_scalar(k, r, 1 / math.log(2.0), MAGIC, ALU.mult, ALU.add))
                link(V.tensor_scalar(k, k, -MAGIC, None, ALU.add))
                for part in LN2:
                    link(V.scalar_tensor_tensor(r, k, -part, r, ALU.mult, ALU.add))
                link(V.tensor_scalar(y, r, 1 / 5040, 1 / 720, ALU.mult, ALU.add))
                for i in (5, 4, 3, 2, 1, 0):
                    link(V.tensor_tensor(y, y, r, ALU.mult))
                    link(V.tensor_scalar(y, y, 1 / math.factorial(i), None, ALU.add))
                link(V.tensor_scalar(k1, k, 0.5, MAGIC, ALU.mult, ALU.add))
                link(V.tensor_scalar(k1, k1, -MAGIC, None, ALU.add))
                link(V.tensor_tensor(k, k, k1, ALU.subtract))
                for e in (k1, k):
                    link(V.tensor_scalar(r.bitcast(I32), e, 127.0, 8388608.0, ALU.add, ALU.mult))
                    link(V.tensor_tensor(y, y, r, ALU.mult))

            dve.wait_ge(S["rows_loaded"], 16 * 11)
            V.tensor_copy(vec_rows[32:32 + GP, 3, :].rearrange("g (q p) -> g q p", q=2),
                          dt_rows[32:32 + GP, :].unsqueeze(2).broadcast_to([GP, 2, 64])).then_inc(S["dt_spread"], 1)
            dve.wait_ge(S["tanh_c"], 1)
            link(V.scalar_tensor_tensor(silu_c, c_col[:, 2, :], 1.0, c_col[:, 0, :], ALU.add, ALU.mult))
            link(V.tensor_scalar(silu_c, silu_c, 0.5, None, ALU.mult), "silu_ready")
            dve.wait_ge(S["pos_loaded"], 16)
            dve.wait_ge(S["bc_loaded"], 48)
            link(V.tensor_copy(pos_f, pos_i))
            ang = rope[:, 3]
            for i in range(2):
                link(V.tensor_tensor(ang[:, :, HALF * i:HALF * (i + 1)], pos_f.unsqueeze(2).broadcast_to([P, TT, HALF]),
                                     inv_bc.unsqueeze(1).broadcast_to([P, TT, HALF]), ALU.mult))
            reduce_angle(ang, rope[:, 4])
            cos_angle(rope[:, 2], ang, "angle_ready")

            dve.wait_ge(S["ss_x_ready"], TT)
            link(V.tensor_scalar(ss_x, ss_x, 1 / D_MODEL, EPS, ALU.mult, ALU.add))
            rsqrt(rstd_x, ss_x, work[:, 0:4], "rstd_x_ready")

            dve.wait_ge(S["vec_t"], 1)
            link(V.tensor_copy(vec_cols[:], bank[4][:, 0:296]))
            dve.wait_ge(S["sin_ready"], 2)
            link(V.tensor_scalar(rope[:, 1, :, 0:HALF], rope[:, 1, :, 0:HALF], -1.0, None, ALU.mult))
            for i, g in ((2, gq_bc), (4, gk_bc)):
                link(V.tensor_tensor(rope[:, i], rope[:, 0], g.unsqueeze(1).broadcast_to([P, TT, HD]), ALU.mult))
                for a in range(2):
                    link(V.tensor_tensor(rope[:, i + 1, :, HALF * a:HALF * (a + 1)], rope[:, 1, :, HALF * a:HALF * (a + 1)],
                                         g[:, HALF * (1 - a):HALF * (2 - a)].unsqueeze(1).broadcast_to([P, TT, HALF]),
                                         ALU.mult))

            def ada(dst, src, s):
                link(V.tensor_scalar(dst, src[:, 0, :], silu_c[:, 0:1], None, ALU.mult))
                for k in range(1, KD):
                    ins = V.scalar_tensor_tensor(dst, src[:, k, :], silu_c[:, k:k + 1], dst, ALU.mult, ALU.add)
                    link(ins, s if k == KD - 1 else "dve_chain")

            def later_ada(first, last):
                for n in range(first, last):
                    dve.wait_ge(S[f"ada_next_loaded{n % 2}"], 16 * (n // 2 + 1))
                    if n >= 2:
                        dve.wait_ge(S["ada_sum_ready"], n - 1)
                    ada(ada_next_acc[:, n % 2], ada_next[n % 2], "ada_used")

            for i in range(4):
                dve.wait_ge(S[f"ada_first_loaded{i}"], 16)
                ada(ada_first_acc[:, i], ada_first[:, i], "ada_acc_ready")
            dve.wait_ge(S["mod_ready"], 1)
            link(V.tensor_tensor(shift1, bank[5][:, 0:KD], vec_cols[:, C_BADA:C_BADA + KD], ALU.add))
            link(V.tensor_tensor(scale1, bank[5][:, KD:2 * KD], vec_cols[:, C_BADA + KD:C_BADA + 2 * KD], ALU.add))
            link(V.scalar_tensor_tensor(scale1, scale1, 1.0, vec_cols[:, C_NMIX:C_NMIX + KD], ALU.add, ALU.mult),
                 "mod1_ready")

            def split(k, s, ready, nth=None):
                n = k if nth is None else nth
                dve.wait_ge(S[s], n + 1)
                link(V.tensor_copy(act_hi[:, k, :], up32[:, n % 2, :]))
                signal(V.tensor_tensor(act_lo[:, k, :], up32[:, n % 2, :], act_hi[:, k, :].bitcast(F32), ALU.subtract),
                       ready)

            dve.wait_ge(S["zeros_stored"], 32)
            for k in range(KD):
                split(k, "x_t_read", "act_in_ready")

            later_ada(0, 1)
            lr, li, ldt = (vec_cols[:, a:a + GP] for a in (C_ARE, C_AIM, C_LDT))
            dt_, mag, th, cth, kk, k1, tc, ts, snt, cst = (s5_p[:, i] for i in range(10))
            ang_s, ang_c = s5_p[:, 6], s5_p[:, 7]
            sin_t, cos_t = s5_p[:, 8], s5_p[:, 9]
            lb_r, lb_i, cf_r, cf_i, den, n1, n2, ur, ui, r8, w1, w2, w3, w4 = (s5_p[:, i] for i in range(10, 24))
            exp(dt_, ldt, kk, k1, w1)
            link(V.tensor_tensor(w2, lr, dt_, ALU.mult))
            exp(mag, w2, kk, k1, w1)
            link(V.tensor_tensor(ang_s, li, dt_, ALU.mult))
            reduce_angle(ang_s, kk)
            cos_angle(ang_c, ang_s, "s5_angle")
            later_ada(1, 2)
            dve.wait_ge(S["s5_sin"], 1)
            link(V.tensor_tensor(lb_r, mag, cos_t, ALU.mult))
            link(V.tensor_tensor(lb_i, mag, sin_t, ALU.mult))
            link(V.tensor_tensor(den, lr, lr, ALU.mult))
            link(V.tensor_tensor(w1, li, li, ALU.mult))
            link(V.tensor_tensor(den, den, w1, ALU.add))
            link(V.reciprocal(den, den))
            link(V.tensor_scalar(n1, lb_r, -1.0, None, ALU.add))
            link(V.tensor_tensor(cf_r, n1, lr, ALU.mult))
            link(V.tensor_tensor(w1, lb_i, li, ALU.mult))
            link(V.tensor_tensor(cf_r, cf_r, w1, ALU.add))
            link(V.tensor_tensor(cf_r, cf_r, den, ALU.mult))
            link(V.tensor_tensor(cf_i, lb_i, lr, ALU.mult))
            link(V.tensor_tensor(w1, n1, li, ALU.mult))
            link(V.tensor_tensor(cf_i, cf_i, w1, ALU.subtract))
            link(V.tensor_tensor(cf_i, cf_i, den, ALU.mult))

            def cmul(o_r, o_i, a_r, a_i, b_r, b_i, t1, t2, s="dve_chain"):
                V.tensor_tensor(o_r, a_r, b_r, ALU.mult)
                V.tensor_tensor(t1, a_i, b_i, ALU.mult)
                V.tensor_tensor(o_i, a_r, b_i, ALU.mult)
                link(V.tensor_tensor(t2, a_i, b_r, ALU.mult))
                V.tensor_tensor(o_r, o_r, t1, ALU.subtract)
                link(V.tensor_tensor(o_i, o_i, t2, ALU.add), s)

            link(V.memset(power[:, 0, 0, :], 1.0))
            link(V.memset(power[:, 1, 0, :], 0.0))
            link(V.tensor_copy(power[:, 0, 1, :], lb_r))
            link(V.tensor_copy(power[:, 1, 1, :], lb_i))
            for n in range(2, CHUNK + 1):
                a, b = n // 2, n - n // 2
                cmul(power[:, 0, n, :], power[:, 1, n, :], power[:, 0, a, :], power[:, 1, a, :], power[:, 0, b, :],
                     power[:, 1, b, :], w1, w2)
            cmul(ur, ui, cos_t, sin_t, cos_t, sin_t, w1, w2)
            cmul(w3, w4, ur, ui, ur, ui, w1, w2)
            cmul(ur, ui, w3, w4, w3, w4, w1, w2)
            link(V.tensor_tensor(r8, mag, mag, ALU.mult))
            link(V.tensor_tensor(r8, r8, r8, ALU.mult))
            link(V.tensor_tensor(r8, r8, r8, ALU.mult))
            for j in range(CHUNK - 1):
                V.tensor_copy(power_back[:, :, j, :], power[:, :, CHUNK - 1 - j, :])
            link(V.tensor_copy(power_back[:, :, CHUNK - 1, :], power[:, :, 0, :]), "s5_params")

            def rotate(src, dst, tab, t, heads, s):
                cos, sin = rope[:, tab, t, :], rope[:, tab + 1, t, :]
                sh = src.rearrange("p (h d) -> p h d", h=heads)
                dh = dst.rearrange("p (h d) -> p h d", h=heads)
                th = tmp[:, 0:heads * HD].rearrange("p (h d) -> p h d", h=heads)
                V.tensor_tensor(dh, sh, cos.unsqueeze(1).broadcast_to([P, heads, HD]), ALU.mult)
                for a in range(2):
                    o = slice(HALF * a, HALF * (a + 1))
                    w = slice(HALF * (1 - a), HALF * (2 - a))
                    ins = V.tensor_tensor(th[:, :, o], sh[:, :, w],
                                          sin[:, o].unsqueeze(1).broadcast_to([P, heads, HALF]), ALU.mult)
                link(ins)
                link(V.tensor_tensor(dst, dst, tmp[:, 0:heads * HD], ALU.add), s)

            later_ada(2, 3)
            dve.wait_ge(S["proj_read"], 4)
            link(V.tensor_scalar(wi[:], ki_w[:, :, HD:TAIL], WI_SCALE, None, ALU.mult))
            for t in range(TT):
                rotate(ki_w[:, t, 0:HD], rot[:, 0, P * t:P * t + HD], 0, t, 1, "dve_chain")
            signal(V.tensor_copy(rot[:, 0, :].rearrange("p (t a d) -> p t a d", t=TT, a=2)[:, :, 1, :],
                                 rot[:, 0, :].rearrange("p (t a d) -> p t a d", t=TT, a=2)[:, :, 0, :]), "rot_ready")
            later_ada(3, 4)
            for t in range(TT):
                dve.wait_ge(S["proj_read"], 4 + t + 1)
                if t == 0:
                    dve.wait_ge(S["turned_ready"], 1)
                rotate(pre[:, t, :], rot[:, t, :], 0, t, HEADS, "rot_ready")
            later_ada(4, 8)
            dve.wait_ge(S["ada_sum_ready"], 8)
            sums = bank[7][:, 0:4 * KD].rearrange("p (v k) -> p v k", v=4)
            b = vec_cols[:, C_BADA + 2 * KD:C_BADA + 6 * KD].rearrange("p (v k) -> p v k", v=4)
            link(V.tensor_tensor(mod_cols[:, 2:6, :], sums, b, ALU.add), "ada_sums_read")
            link(V.scalar_tensor_tensor(scale2, scale2, 1.0, vec_cols[:, C_NFFN:C_NFFN + KD], ALU.add, ALU.mult))

            def scores(t):
                for h in range(HEADS):
                    i = (t - 1) * HEADS + h
                    dve.wait_ge(S["relu_ready"], i + 1)
                    if h == 0:
                        link(V.tensor_scalar(score[t], relu[:, i % 2, 0:KEYS[t]], wi[:, t, h:h + 1], None, ALU.mult),
                             "relu_used")
                    else:
                        link(V.scalar_tensor_tensor(score[t], relu[:, i % 2, 0:KEYS[t]], wi[:, t, h:h + 1], score[t],
                                                    ALU.mult, ALU.add), "relu_used")

            def top_k(t, first=0, last=TOPK // 8):
                dve.wait_ge(S["future_set"], t)
                for _ in range(first, last):
                    link(V.max(top8, score[t]))
                    link(V.match_replace(score[t], top8, score[t], TAKEN))
                if last == TOPK // 8:
                    link(V.tensor_scalar(bias[t], score[t], TAKEN, MASK, ALU.not_equal, ALU.mult))

            def head_sums(which):
                for t in range(TT):
                    n = 4 * which + t
                    dve.wait_ge(S["ss_qk_ready"], n + 1)
                    link(V.tensor_reduce(ss_qk[:, 32 * which + 8 * t:32 * which + 8 * t + 8],
                                         up32[:, n % 2, :].rearrange("p (h d) -> p h d", h=HEADS), AX, ALU.add), "sq_used")
                w = slice(32 * which, 32 * which + 32)
                link(V.tensor_scalar(ss_qk[:, w], ss_qk[:, w], 1 / HD, EPS, ALU.mult, ALU.add))
                rsqrt(rstd_qk[:, w], ss_qk[:, w], work[:, 0:32])

            def norm_rotate(which, t):
                dve.wait_ge(S["turned_ready"], 1 + 4 + (4 if which else 0))
                rotate(pre[:, t, :], rot[:, t, :], 2 if which else 4, t, HEADS, "rot_ready" if which else "dve_chain")
                if not which:
                    rs = rstd_qk[:, 8 * t:8 * t + 8].unsqueeze(2).broadcast_to([P, HEADS, HD])
                    r3 = rot[:, t, :].rearrange("p (h d) -> p h d", h=HEADS)
                    link(V.tensor_tensor(r3, r3, rs, ALU.mult), "rot_ready")

            for t in range(1, TT):
                scores(t)
            top_k(1)
            head_sums(0)
            for t in range(TT):
                norm_rotate(0, t)
            top_k(2)
            head_sums(1)
            for t in range(TT):
                norm_rotate(1, t)
            for k in range(KD):
                ins = V.tensor_scalar(diag[:, k, :], ident[:], gate1[:, k:k + 1], None, ALU.mult)
            signal(ins, "diag_ready")
            link(V.tensor_scalar(q_scale, rstd_qk[:, 32:64], -ATT_SCALE, None, ALU.mult))
            dve.wait_ge(S["g1_spread"], 1)
            for i in range(2):
                ins = V.tensor_copy(g1_row[:, 512 * i:512 * i + 512], bank[6 + i][:])
            signal(ins, "g1_read")

            def logits(i):
                t = i // HEADS
                dve.wait_ge(S["logit_mm"], i + 1)
                if i >= LOGITS:
                    dve.wait_ge(S["prob_ready"], i - LOGITS + 1)
                signal(V.tensor_tensor_reduce(out=logit[:, i % LOGITS, 0:KEYS[t]], in0=bank[i % 2][:, 0:KEYS[t]], in1=bias[t],
                                              scale=q_scale[:, i:i + 1], scalar=3.0e38, op0=ALU.add, op1=ALU.min,
                                              accum_out=neg_max[:, i:i + 1]), "logit_ready")

            def turned_probs(i):
                t = i // HEADS
                dve.wait_ge(S["prob_turned"], i + 1)
                if i >= 2:
                    dve.wait_ge(S["pv_done"], i - 1)
                signal(V.tensor_copy(prob_t[:, i % 2, 0:KEYS[t]], bank[2 + i % 2][:, 0:KEYS[t]]), "prob_t_ready")

            def heads_out(t):
                dve.wait_ge(S["pv_done"], HEADS * (t + 1))
                w = slice(HEADS * t, HEADS * (t + 1))
                link(V.reciprocal(rinv[:, w], psum_p[:, w]))
                signal(V.tensor_tensor(y_attn[:, t, :].rearrange("p (h d) -> p h d", h=HEADS),
                                       bank[4 + t % 2][:].rearrange("p (h d) -> p h d", h=HEADS),
                                       rinv[:, w].unsqueeze(2).broadcast_to([P, HEADS, HD]), ALU.mult), "y_attn_ready")

            def by_channel(v, n=GP):
                return v.unsqueeze(2).broadcast_to([P, n, CH])
            dve.wait_ge(S["s5_loaded"], 32)
            t1, t2 = (s5_t[:, i, 0:GP * CH].rearrange("p (g h) -> p g h", g=GP) for i in range(2))
            dve.wait_ge(S["weights_used"], U_V + 2)
            cmul(s5_bb[:, 0], s5_bb[:, 1], s5_b[:, 0], s5_b[:, 1], by_channel(cf_r), by_channel(cf_i), t1, t2)

            d_eye = d_bc.rearrange("p (g h) -> p g h", g=GROUPS)
            dve.wait_ge(S["d_loaded"], 16)
            dve.wait_ge(S["ident_ready"], 1)
            link(V.tensor_tensor(d_eye, d_eye, ident[0:CH, 0:CH].unsqueeze(1).broadcast_to([CH, GROUPS, CH]), ALU.mult))

            def source_v(half):
                gs = slice(GH * half, GH * (half + 1))
                vt, t1 = s5_vt[half], s5_mem[:, 7168:8192].rearrange("p (g j h) -> p g j h", g=GH, j=CHUNK)
                br, bi = (s5_bb[:, i, gs].unsqueeze(2).broadcast_to([P, GH, CHUNK, CH]) for i in range(2))
                pr, pi = (power_back[:, i, :, gs].rearrange("p j g -> p g j").unsqueeze(3).broadcast_to(
                    [P, GH, CHUNK, CH]) for i in range(2))
                V.tensor_tensor(vt[:, 0], br, pr, ALU.mult)
                link(V.tensor_tensor(t1, bi, pi, ALU.mult))
                link(V.tensor_tensor(vt[:, 0], vt[:, 0], t1, ALU.subtract))
                V.tensor_tensor(vt[:, 1], br, pi, ALU.mult)
                link(V.tensor_tensor(t1, bi, pr, ALU.mult))
                link(V.tensor_tensor(vt[:, 1], vt[:, 1], t1, ALU.add), "vt_ready")

            def add_d(half, part):
                d = d_eye[:, NG * half:NG * (half + 1), :].rearrange("p (b c q) h -> p b q c h", b=2, q=2)
                for i in (2 * part, 2 * part + 1):
                    dve.wait_ge(S["lags_ready"], 4 * half + i + 1)
                    signal(V.tensor_tensor(lags_of(i)[:, :, 0, :], lags_of(i)[:, :, 0, :], d[:, i // 2, i % 2],
                                           ALU.add), "lag_d_added")

            def scan(half):
                gs = slice(GH * half, GH * (half + 1))
                link(V.tensor_copy(scan_r, r8[:, gs].unsqueeze(2).broadcast_to([P, GH, NCH])))
                V.memset(scan_r[:, :, 0:1], 0.0)
                flat = lambda v: v.rearrange("p g c -> p (g c)")
                er, ei = flat(turn[:, 0, gs]), flat(turn[:, 1, gs])
                dve.wait_ge(S["turn_ready"], 1)
                dve.wait_ge(S["state_mm"], half + 1)
                sr, si = bank[6][:], bank[7][:]
                zr, zi = s5_z[:, 0, :], s5_z[:, 1, :]
                t1, t2 = s5_t[:, 0, :], s5_t[:, 1, :]
                V.tensor_tensor(zr, sr, er, ALU.mult)
                V.tensor_tensor(t1, si, ei, ALU.mult)
                V.tensor_tensor(zi, si, er, ALU.mult)
                link(V.tensor_tensor(t2, sr, ei, ALU.mult), "state_read")
                V.tensor_tensor(zr, zr, t1, ALU.add)
                link(V.tensor_tensor(zi, zi, t2, ALU.subtract))
                fr = flat(scan_r)
                V.tensor_tensor_scan(t1, fr, zr, 0.0, ALU.mult, ALU.add)
                link(V.tensor_tensor_scan(t2, fr, zi, 0.0, ALU.mult, ALU.add))
                a, b = (v.rearrange("p (g c) -> p g c", g=GH)[:, :, 0:NCH - 1] for v in (t1, t2))
                e1, e2 = turn[:, 0, gs, 0:NCH - 1], turn[:, 1, gs, 0:NCH - 1]
                z1, z2 = (v.rearrange("p (g c) -> p g c", g=GH)[:, :, 0:NCH - 1] for v in (zr, zi))
                V.memset(s5_x[:, :, :, 0:1], 0.0)
                V.tensor_tensor(s5_x[:, 0, :, 1:NCH], a, e1, ALU.mult)
                V.tensor_tensor(z1, b, e2, ALU.mult)
                V.tensor_tensor(s5_x[:, 1, :, 1:NCH], a, e2, ALU.mult)
                link(V.tensor_tensor(z2, b, e1, ALU.mult))
                V.tensor_tensor(s5_x[:, 0, :, 1:NCH], s5_x[:, 0, :, 1:NCH], z1, ALU.subtract)
                link(V.tensor_tensor(s5_x[:, 1, :, 1:NCH], s5_x[:, 1, :, 1:NCH], z2, ALU.add), "s5_state")

            def s5(stage, half, part):
                if stage == "lags":
                    add_d(half, part)
                elif stage == "states":
                    scan(half)
                    if half == 0:
                        source_v(1)

            source_v(0)
            dve.wait_ge(S["turn_ready"], 1)
            for i in range(ATT_UNITS + 1):
                if i < ATT_UNITS:
                    logits(i)
                if i >= 1:
                    turned_probs(i - 1)
                    if i % HEADS == 0 and i // HEADS >= 2:
                        heads_out(i // HEADS - 2)
                if i < TOPK // 8:
                    top_k(TT - 1, i, i + 1)
                if i - 1 in S5_AT:
                    s5(*S5_AT[i - 1])
            heads_out(TT - 1)

            for k in range(4):
                dve.wait_ge(S["g_t_read"], k + 1)
                link(V.tensor_copy(act_hi[:, k, :], up32[:, k % 2, :]))
                signal(V.tensor_tensor(act_lo[:, k, :], up32[:, k % 2, :], act_hi[:, k, :].bitcast(F32), ALU.subtract),
                       "glu_in")
            def norm_y(w, y, scale):
                ws = slice(4 * w, 4 * w + 4)
                link(V.tensor_scalar(ss_y[:, ws], ss_y[:, ws], scale * scale / 512, EPS, ALU.mult, ALU.add))
                rsqrt(rstd_y[:, ws], ss_y[:, ws], work[:, 0:4])
                if scale != 1:
                    link(V.tensor_scalar(rstd_y[:, ws], rstd_y[:, ws], scale, None, ALU.mult))
                for t in range(TT):
                    signal(V.tensor_scalar(y[:, t, :], y[:, t, :], rstd_y[:, 4 * w + t:4 * w + t + 1], None, ALU.mult),
                           "yn_ready")

            dve.wait_ge(S["ss_y_ready"], TT)
            norm_y(1, y_attn, 1)
            for t in range(TT):
                dve.wait_ge(S["tanh_z"], t + 1)
                signal(V.scalar_tensor_tensor(y_ssm[:, t, :], up32[:, t % 2, :], 1.0, y_ssm[:, t, :], ALU.add, ALU.mult),
                       "glu_read")
            dve.wait_ge(S["ss_y_ready"], 2 * TT)
            norm_y(0, y_ssm, 0.5)
            dve.wait_ge(S["weights_used"], U_GLU + 1)
            for n, k in enumerate(MIX_ORDER):
                split(k, "mix_t_read", "mix_in", n)
            dve.wait_ge(S["x_again"], 16 * TT)
            for n in range(2):
                for t in range(TT):
                    if t < TT - 1:
                        dve.wait_ge(S["out_mm"], 3 * n + t + 1)
                    else:
                        dve.wait_ge(S["weights_used"], U_OUT + 2 * n + 2)
                    o = xh[:, t, 512 * n:512 * n + 512]
                    tb = logit[:, t % 2, :]
                    link(V.tensor_tensor(tb, bank[4 * n + t][:], g1_row[:, 512 * n:512 * n + 512], ALU.mult))
                    signal(V.tensor_tensor(o, o, tb, ALU.add), "h_ready")
            dve.wait_ge(S["ss_h_ready"], TT)
            link(V.tensor_scalar(ss_h, ss_h, 1 / D_MODEL, EPS, ALU.mult, ALU.add))
            rsqrt(rstd_h, ss_h, work[:, 64:68])
            for t in range(TT):
                signal(V.tensor_scalar(hn_tok[:, t, :], xh[:, t, :], rstd_h[:, t:t + 1], None, ALU.mult), "hn_ready")
            dve.wait_ge(S["weights_used"], U_OUT + 4)
            for k in range(KD):
                split(k, "h_t_read", "mlp_in")

            with dve.Fori(0, UPS) as j:
                for q in range(4):
                    f = (0, 1, FT, FT + 1)[q]
                    dve.wait_ge(S["tap_ready"], j * 4 + (q + 1))
                    V.scalar_tensor_tensor(conv[:, q, 1:], bank[q][:, 0:SEQ - 1],
                                           vec_cols[:, bass.ds(j * 2 + (C_W1 + f), 1)], conv[:, q, 1:],
                                           ALU.mult, ALU.add).then_inc(S["conv_read"], 1)
                    dve.wait_ge(S["conv_read"], j * 4 + (q + 1))
                    V.scalar_tensor_tensor(conv[:, q, 2:], bank[q][:, 0:SEQ - 2],
                                           vec_cols[:, bass.ds(j * 2 + (C_W0 + f), 1)], conv[:, q, 2:],
                                           ALU.mult, ALU.add).then_inc(S["conv_ready"], 1)
                for q in range(2):
                    dve.wait_ge(S["gelu_up"], j * 2 + (q + 1))
                    dve.wait_ge(S["conv_ready"], j * 4 + 4)
                    V.tensor_tensor(up32[:, q, :], conv[:, q, :], conv[:, 2 + q, :], ALU.mult
                                    ).then_inc(S["ff32_ready"], 1)
                for q in range(2):
                    dve.wait_ge(S["ff_hi_ready"], j * 2 + (q + 1))
                    V.tensor_tensor(ff_lo[:, bass.ds(j * 2 + q, 1), :].rearrange("p a t -> p (a t)"), up32[:, q, :],
                                    ff_hi[:, bass.ds(j * 2 + q, 1), :].rearrange("p a t -> p (a t)").bitcast(F32),
                                    ALU.subtract).then_inc(S["ff_lo_ready"], 1)
            for n in range(KD):
                dve.wait_ge(S["down_t"], n + 1)
                o = xh[:, :, n * P:(n + 1) * P]
                signal(V.tensor_tensor(o, o, bank[n][:].rearrange("p (t d) -> p t d", t=TT), ALU.add), "sum_ready")

        @block.tensor
        def _(pe):
            T = nc.tensor

            def mm3(dst, lhs_hi, lhs_lo, rhs_hi, rhs_lo, start, stop):
                T.matmul(dst, lhs_hi, rhs_hi, start=start, stop=False)
                T.matmul(dst, lhs_hi, rhs_lo, start=False, stop=False)
                return T.matmul(dst, lhs_lo, rhs_hi, start=False, stop=stop)

            def flip(dst, src, n=P, at=0):
                return T.matmul(dst, src, ident[at:at + n, at:at + n], is_transpose=True, start=True, stop=True)

            def over_partitions(dst, acc):
                for i in range(4):
                    ins = T.matmul(dst[:, i:i + 1], acc[:, i * P:(i + 1) * P], ones[:, 0:1], start=True, stop=True)
                return ins

            pe.wait_ge(S["ident_ready"], 1)
            pe.wait_ge(S["rows_loaded"], 16 * 11)
            pe.wait_ge(S["dt_spread"], 1)
            at = 0
            for i, n in enumerate((72, 88, 88, 48)):
                ins = flip(bank[4][:, at:at + n], vec_rows[0:n, i, :], n)
                at += n
            ins.then_inc(S["vec_t"], 1)
            pe.wait_ge(S["xn_ready"], TT)
            for k in range(KD):
                if k >= 4:
                    pe.wait_ge(S["x_t_read"], k - 3)
                for t in range(TT):
                    ins = flip(bank[k % 4][:, t * P:(t + 1) * P], xh[:, t, k * P:(k + 1) * P])
                ins.then_inc(S["x_t_ready"], 1)
                if k == 3:
                    pe.wait_ge(S["ones_ready"], 1)
                    for i in range(4):
                        pe.wait_ge(S["ada_acc_ready"], i + 1)
                        ins = over_partitions(bank[5][:, 4 * i:4 * i + 4], ada_first_acc[:, i])
                    ins.then_inc(S["mod_ready"], 1)

            def tail():
                n = U_TAIL
                pe.wait_ge(S["lo_ready"], n + 1)
                pe.wait_ge(S["x_t_read"], KD)
                wh, wl = unit_view(w_hi, n, KD, TAIL), unit_view(w_lo, n, KD, TAIL)
                for t in range(TT):
                    ts = slice(t * P, (t + 1) * P)
                    for k in range(KD):
                        if t == 0:
                            pe.wait_ge(S["act_in_ready"], k + 1)
                        ins = mm3(bank[t][:, 0:TAIL], act_hi[:, k, ts], act_lo[:, k, ts], wh[:, k, :], wl[:, k, :],
                                  k == 0, k == KD - 1)
                    ins.then_inc(S["proj_ready" if t < TT - 1 else "weights_used"], 1)

            def later_ada(n):
                pe.wait_ge(S["ada_used"], n + 1)
                over_partitions(bank[7][:, 4 * n:4 * n + 4], ada_next_acc[:, n % 2]).then_inc(S["ada_sum_ready"], 1)

            def project(n0, nth, banks=0, out_sem="proj_ready", free=None, adas={}):
                for kh in range(2):
                    n = n0 + kh
                    pe.wait_ge(S["lo_ready"], n + 1)
                    wh, wl = unit_view(w_hi, n, 4, 512), unit_view(w_lo, n, 4, 512)
                    for t in range(TT):
                        ts = slice(t * P, (t + 1) * P)
                        if kh == 0 and free is not None:
                            pe.wait_ge(S[free], 4 * nth + t + 1)
                        for i in range(4):
                            k = 4 * kh + i
                            ins = mm3(bank[banks + t][:], act_hi[:, k, ts], act_lo[:, k, ts], wh[:, i, :], wl[:, i, :],
                                      k == 0, k == KD - 1)
                        if t == TT - 1:
                            ins.then_inc(S["weights_used"], 1)
                        elif kh == 1:
                            ins.then_inc(S[out_sem], 1)
                        if (kh, t) in adas:
                            later_ada(adas[kh, t])

            turned = [0]

            def turn_heads(rot_before):
                for t in range(TT):
                    pe.wait_ge(S["rot_ready"], rot_before + t + 1)
                    pe.wait_ge(S["turned_read"], max(turned[0] - 1, 1))
                    for g in range(4):
                        ins = flip(bank[4 + turned[0] % 2][:, g * P:(g + 1) * P], rot[:, t, g * P:(g + 1) * P])
                    ins.then_inc(S["turned_ready"], 1)
                    turned[0] += 1

            tail()
            project(U_QI, 0, free="proj_read", adas={(0, 3): 0, (1, 1): 1, (1, 3): 2})
            pe.wait_ge(S["rot_ready"], 1)
            pe.wait_ge(S["mod1_ready"], 1)
            for t in range(TT):
                ins = flip(bank[4][:, t * P:(t + 1) * P], rot[:, 0, t * P:(t + 1) * P])
            ins.then_inc(S["turned_ready"], 1)
            turned[0] = 1
            project(U_U, 1, free="proj_read", adas={(0, 1): 3, (0, 3): 4, (1, 1): 5, (1, 3): 6})
            pe.wait_ge(S["c_rows_loaded"], 64)
            for r in range(2):
                for a in range(4):
                    ins = flip(bank[5 + r][:, P * a:P * (a + 1)], c_rows[:, r, a].rearrange("p q n -> p (q n)"))
            ins.then_inc(S["c_t"], 1)
            pe.wait_ge(S["c_t_read"], 4)
            turn_heads(1)
            later_ada(7)
            pe.wait_ge(S["turned_read"], 5)
            pe.wait_ge(S["ada_sums_read"], 1)
            for i in range((TT - 1) * HEADS):
                t, h = 1 + i // HEADS, i % HEADS
                if i >= 2:
                    pe.wait_ge(S["relu_ready"], i - 1)
                hp = slice(64 * (h % 2), 64 * (h % 2) + 64)
                T.matmul(bank[6 + i % 2][:, 0:KEYS[t]], qi_t[hp, h // 2, t * P:(t + 1) * P], ki_t[hp, 0:KEYS[t]],
                         start=True, stop=True).then_inc(S["score_mm"], 1)

            project(U_K, 2, free="proj_read")
            project(U_Q, 3, free="proj_read")
            turn_heads(5)
            project(U_V, 4, free="proj_read")
            turn_heads(9)
            pe.wait_ge(S["diag_ready"], 1)
            for k in range(KD):
                ins = T.matmul(bank[6 + k // 4][:, (k % 4) * P:(k % 4 + 1) * P], ones[:], diag[:, k, :],
                               start=True, stop=True)
            ins.then_inc(S["g1_spread"], 1)

            pe.wait_ge(S["proj_read"], 24)
            pe.wait_ge(S["turned_read"], 13)

            def logits(i):
                t, h = i // HEADS, i % HEADS
                hp = slice(64 * (h % 2), 64 * (h % 2) + 64)
                if i >= 2:
                    pe.wait_ge(S["logit_ready"], i - 1)
                T.matmul(bank[i % 2][:, 0:KEYS[t]], q_t[hp, h // 2, t * P:(t + 1) * P], k_t[hp, h // 2, 0:KEYS[t]],
                         start=True, stop=True).then_inc(S["logit_mm"], 1)

            def turn_probs(i):
                t = i // HEADS
                pe.wait_ge(S["prob_ready"], i + 1)
                if i >= 2:
                    pe.wait_ge(S["prob_t_ready"], i - 1)
                for s in range(t + 1):
                    ins = flip(bank[2 + i % 2][:, s * P:(s + 1) * P], prob[:, i % 2, s * P:(s + 1) * P])
                ins.then_inc(S["prob_turned"], 1)

            def values(i):
                t, h = i // HEADS, i % HEADS
                pe.wait_ge(S["prob_t_ready"], i + 1)
                if h == 0 and t >= 2:
                    pe.wait_ge(S["y_attn_ready"], t - 1)
                for s in range(t + 1):
                    ins = T.matmul(bank[4 + t % 2][:, h * HD:(h + 1) * HD], prob_t[:, i % 2, s * P:(s + 1) * P],
                                   v_tok[:, s, h * HD:(h + 1) * HD], start=(s == 0), stop=(s == t))
                ins.then_inc(S["pv_done"], 1)

            def group_place(g, n):
                return bank[6 + g % 2][0:n, (g % 8 // 2) * P:(g % 8 // 2 + 1) * P]

            def s5(stage, half, part):
                b0 = 4 * half
                if stage == "V":
                    if part:
                        pe.wait_ge(S["v_ready"], b0 + 2)
                    else:
                        pe.wait_ge(S["vt_ready"], half + 1)
                        pe.wait_ge(S["y_read" if half else "g1_read"], 4 if half else 1)
                    for g in range(4 * part, 4 * part + 4):
                        for r in range(2):
                            ins = flip(bank[6 + g % 4 // 2][:, ((g % 2) * 2 + r) * P:((g % 2) * 2 + r + 1) * P],
                                       s5_vt[half][:, r, g].rearrange("p j h -> p (j h)"))
                        if g % 2:
                            ins.then_inc(S["v_t"], 1)
                elif stage == "lags":
                    if part:
                        pe.wait_ge(S["lags_ready"], b0 + 2)
                    else:
                        pe.wait_ge(S["lag_w_ready"], half + 1)
                        pe.wait_ge(S["v_ready"], b0 + 4)
                    for g in range(8 * part, 8 * part + 8):
                        hp = slice(64 * (g % 2), 64 * (g % 2) + 64)
                        for r in range(2):
                            ins = T.matmul(group_place(g, CH), s5_bb[hp, r, GH * half + g // 2, :],
                                           lag_w[half][hp, r, g // 2, 0:CHUNK, :].rearrange("p l h -> p (l h)"),
                                           start=(r == 0), stop=(r == 1))
                        if g % 8 >= 6:
                            ins.then_inc(S["lag_mm"], 1)
                elif stage == "u":
                    pe.wait_ge(S["u_grouped"], 2)
                    pe.wait_ge(S["lags_ready"], b0 + 4)
                    for g in range(NG):
                        ins = flip(bank[6 + g // 8][:, (g % 8) * NCH:(g % 8 + 1) * NCH], group_in[:, NG * half + g, :],
                                   NCH, NCH)
                        if g % 8 == 7:
                            ins.then_inc(S["u_t"], 1)
                elif stage == "states":
                    pe.wait_ge(S["u_t_read"], 2 * half + 2)
                    for g in range(NG):
                        hp = slice(64 * (g % 2), 64 * (g % 2) + 64)
                        for r in range(2):
                            ins = T.matmul(bank[6 + r][hp, (g // 2) * NCH:(g // 2 + 1) * NCH],
                                           s5_v[half][:, g // 2, r, hp], s5_u[:, g, :], start=True, stop=True)
                    ins.then_inc(S["state_mm"], 1)
                else:
                    if part:
                        pe.wait_ge(S["y_read"], b0 + 2)
                    else:
                        pe.wait_ge(S["state_read"], half + 1)
                        pe.wait_ge(S["m_loaded"], 16 * CHUNK * (half + 1))
                        pe.wait_ge(S["s5_state"], half + 1)
                    for g in range(8 * part, 8 * part + 8):
                        hp = slice(64 * (g % 2), 64 * (g % 2) + 64)
                        T.matmul(group_place(g, NCH), s5_u[:, g, :], s5_m[half][:, g, :], start=True, stop=False)
                        for r in range(2):
                            ins = T.matmul(group_place(g, NCH), s5_x[hp, r, g // 2, :],
                                           lag_w[half][hp, r, g // 2, 1:, :].rearrange("p l h -> p (l h)"),
                                           start=False, stop=(r == 1))
                        if g % 8 >= 6:
                            ins.then_inc(S["y_mm"], 1)

            for i in range(ATT_UNITS + 2):
                if i < ATT_UNITS:
                    logits(i)
                if 1 <= i <= ATT_UNITS:
                    turn_probs(i - 1)
                if i >= 2:
                    values(i - 2)
                if i in S5_AT:
                    s5(*S5_AT[i])
            pe.wait_ge(S["prob_t_ready"], ATT_UNITS)
            pe.wait_ge(S["y_attn_ready"], TT)

            pe.wait_ge(S["gelu_ready"], TT)
            for k in range(4):
                for t in range(TT):
                    ins = flip(bank[k][:, t * P:(t + 1) * P], y_ssm[:, t, k * P:(k + 1) * P])
                ins.then_inc(S["g_t"], 1)
            pe.wait_ge(S["lo_ready"], U_GLU + 1)
            pe.wait_ge(S["glu_in"], 4)
            pe.wait_ge(S["y_read"], 8)
            pe.wait_ge(S["b_rows_loaded"], 16)
            wh, wl = unit_view(w_hi, U_GLU, 4, 512), unit_view(w_lo, U_GLU, 4, 512)
            for t in range(TT):
                ts = slice(t * P, (t + 1) * P)
                T.matmul(bank[4 + t][:], ones[0:1, :], b_glu_row, start=True, stop=False)
                for k in range(4):
                    ins = mm3(bank[4 + t][:], act_hi[:, k, ts], act_lo[:, k, ts], wh[:, k, :], wl[:, k, :],
                              False, k == 3)
                ins.then_inc(S["glu_mm"], 1)
            pe.wait_ge(S["g_t_read"], 4)
            flip(bank[0][:, 0:P], ident[:]).then_inc(S["weights_used"], 1)

            for n, k in enumerate(MIX_ORDER):
                pe.wait_ge(S["yn_ready"], 4 * (n // 4) + 4)
                if n >= 4:
                    pe.wait_ge(S["mix_t_read"], n - 3)
                y = y_ssm if k < 4 else y_attn
                for t in range(TT):
                    ins = flip(bank[n % 4][:, t * P:(t + 1) * P], y[:, t, (k % 4) * P:(k % 4 + 1) * P])
                ins.then_inc(S["mix_t"], 1)
            pe.wait_ge(S["mix_t_read"], KD)
            pe.wait_ge(S["mix_in"], KD)
            pe.wait_ge(S["tanh_z"], TT)
            project(U_OUT, 0, 0, "out_mm")
            project(U_OUT + 2, 0, 4, "out_mm")
            pe.wait_ge(S["hn_ready"], TT)
            for k in range(KD):
                if k >= 4:
                    pe.wait_ge(S["h_t_read"], k - 3)
                for t in range(TT):
                    ins = flip(bank[k % 4][:, t * P:(t + 1) * P], hn_tok[:, t, k * P:(k + 1) * P])
                ins.then_inc(S["h_t"], 1)
            pe.wait_ge(S["h_t_read"], KD)
            pe.wait_ge(S["mlp_in"], KD)

            def up(j, first):
                for kh in range(2):
                    pe.wait_ge(S["lo_ready"], j * 2 + (U_UP + kh + 1))
                    wh, wl = unit_view(w_hi, U_UP + kh, 4, 512), unit_view(w_lo, U_UP + kh, 4, 512)
                    for q in range(4):
                        if kh == 0 and not first:
                            pe.wait_ge(S["conv_ready"], j * 4 + (q - 3))
                        for i in range(4):
                            k = 4 * kh + i
                            qs = slice(q * P, (q + 1) * P)
                            ins = mm3(bank[q][:], wh[:, i, qs], wl[:, i, qs], act_hi[:, k, :], act_lo[:, k, :],
                                      k == 0, k == KD - 1)
                        if q == 3:
                            ins.then_inc(S["weights_used"], 1)
                        elif kh == 1:
                            ins.then_inc(S["up_mm"], 1)

            up(0, True)
            with pe.Fori(1, UPS) as j:
                up(j, False)

            def down(slot, k0, first, last, dyn):
                wh = w_hi[:, slot, :].rearrange("p (k n) -> p k n", k=2)
                wl = w_lo[:, slot, :].rearrange("p (k n) -> p k n", k=2)
                for i in range(2):
                    if dyn:
                        fh = ff_hi[:, bass.ds(k0 + i, 1), :].rearrange("p a t -> p (a t)")
                        fl = ff_lo[:, bass.ds(k0 + i, 1), :].rearrange("p a t -> p (a t)")
                    else:
                        fh, fl = ff_hi[:, k0 + i, :], ff_lo[:, k0 + i, :]
                    for n in range(KD):
                        ns = slice(n * P, (n + 1) * P)
                        ins = mm3(bank[n][:], wh[:, i, ns], wl[:, i, ns], fh, fl, first and i == 0, last and i == 1)
                        if last and i == 1:
                            ins.then_inc(S["down_mm"], 1)
                if not last:
                    ins.then_inc(S["weights_used"], 1)

            pe.wait_ge(S["ff_lo_ready"], FT)
            pe.wait_ge(S["lo_ready"], U_DOWN + 1)
            down(U_DOWN % 2, 0, True, False, False)
            with pe.Fori(0, FT // 2 - 3, 2) as j:
                for i in range(2):
                    pe.wait_ge(S["lo_ready"], j + (U_DOWN + 2 + i))
                    down((U_DOWN + 1 + i) % 2, j * 2 + (2 + 2 * i), False, False, True)
            pe.wait_ge(S["lo_ready"], UNITS - 1)
            down((UNITS - 2) % 2, FT - 4, False, False, False)
            pe.wait_ge(S["lo_ready"], UNITS)
            down((UNITS - 1) % 2, FT - 2, False, True, False)
            for n in range(KD):
                pe.wait_ge(S["down_scaled"], n + 1)
                for t in range(TT):
                    ins = flip(bank[n][:, t * P:(t + 1) * P], up32[:, n % 2, t * P:(t + 1) * P])
                ins.then_inc(S["down_t"], 1)


INPUTS = ["x", "c", "positions", "w_ada", "b_ada", "norm_mix", "w_in", "ssm_log_dt", "ssm_a_re", "ssm_a_im",
          "ssm_b_re", "ssm_b_im", "ssm_c_re", "ssm_c_im", "ssm_d", "ssm_w_glu", "ssm_b_glu", "q_norm", "k_norm",
          "out_norm_ssm", "out_norm_attn", "w_out", "norm_ffn", "w_up", "conv_w", "conv_b", "w_down"]


def kernel(**inputs):
    import concourse.bacc as bacc
    from concourse.bass_utils import run_bass_kernel_spmd

    nc = bacc.Bacc("TRN2", target_bir_lowering=False, num_devices=1)
    arrays, args = {}, []
    given = [(n, inputs[n]) for n in INPUTS]
    given.append(("inv_freq", (10000.0 ** (-np.arange(0, HD, 2, dtype=np.float64) / HD)).astype(np.float32)[None]))
    for name, a in given:
        a = np.ascontiguousarray(a)
        arrays[f"in_{name}"] = a
        args.append(nc.dram_tensor(f"in_{name}", a.shape, mybir.dt.from_np(a.dtype), kind="ExternalInput").ap())
    out = nc.dram_tensor("out", (1, SEQ, D_MODEL), F32, kind="ExternalOutput").ap()
    layer(nc, *args, out)
    result = run_bass_kernel_spmd(nc, [arrays], core_ids=[0])
    return result.results[0]["out"]
```

```python
import math
from contextlib import ExitStack

import numpy as np
import concourse.bass as bass
from concourse import mybir

F32 = mybir.dt.float32
F32R = mybir.dt.float32r
I32 = mybir.dt.int32
ALU = mybir.AluOpType
ACT = mybir.ActivationFunctionType
AX = mybir.AxisListType.X

P = 128
SEQ, D_MODEL = 512, 1024
TT, KD = SEQ // P, D_MODEL // P
HEADS, HD = 8, 64
HALF = HD // 2
CH, GROUPS, STATE = 16, 32, 64
GP = GROUPS // 2
GH = GP // 2
NG = 2 * GH
CHUNK = 8
NCH = SEQ // CHUNK
TOPK = min(256, SEQ // 4)
D_FF, CONV_W = 2816, 3
FT = D_FF // P
UPS = FT // 2
EPS = 1e-6
ARENA = 26024
UNIT = 2048
TAIL = HD + HEADS
ATT_SCALE = 1.0 / math.sqrt(HD)
WI_SCALE = HEADS ** -0.5 * HD ** -0.5
MAGIC = 12582912.0
RSQRT_GUESS = 1597463007.0
TAKEN = -3.4028234663852886e38
FUTURE = -3.0e38
MASK = -1.0e30


def parts(x, bits, n):
    out = []
    for _ in range(n - 1):
        e = math.frexp(x)[1] - bits
        out.append(math.ldexp(float(round(math.ldexp(x, -e))), e))
        x -= out[-1]
    return out + [float(np.float32(x))]


TWO_PI = parts(2 * math.pi, 8, 4)
LN2 = parts(math.log(2.0), 12, 2)

U_TAIL, U_QI, U_U, U_K, U_Q, U_V, U_GLU, U_OUT = 0, 1, 3, 5, 7, 9, 11, 12
U_UP = U_OUT + 4
U_DOWN = U_UP + 2 * UPS
UNITS = U_DOWN + FT // 2
COLS = {U_U: 0, U_Q: 512, U_K: 1024, U_V: 1536, U_QI: 2048}


ATT_UNITS = TT * HEADS
S5_AT = {2: ("V", 0, 0), 3: ("V", 0, 1), 4: ("u", 0, 0), 5: ("states", 0, 0), 7: ("lags", 0, 0), 11: ("y", 0, 0),
         12: ("V", 1, 0), 13: ("V", 1, 1), 14: ("u", 1, 0), 16: ("states", 1, 0), 17: ("lags", 1, 0), 21: ("y", 1, 0),
         27: ("x", 0, 0), 28: ("x", 1, 0), 29: ("x", 2, 0), 30: ("x", 3, 0)}
MIX_ORDER = (4, 5, 6, 7, 0, 1, 2, 3)
LOGITS = 3


def layer(nc, x, c, positions, w_ada, b_ada, norm_mix, w_in, ssm_log_dt, ssm_a_re, ssm_a_im, ssm_b_re,
          ssm_b_im, ssm_c_re, ssm_c_im, ssm_d, ssm_w_glu, ssm_b_glu, q_norm, k_norm, out_norm_ssm,
          out_norm_attn, w_out, norm_ffn, w_up, conv_w, conv_b, w_down, inv_freq, out):
    u_dram = nc.dram_tensor("u_dram", (SEQ, 512), F32, kind="Internal").ap()
    y_dram = nc.dram_tensor("y_dram", (SEQ, 512), F32, kind="Internal").ap()
    lag_dram = nc.dram_tensor("lag_dram", (CH, GROUPS, 2 * CHUNK - 1, CH), F32, kind="Internal").ap()

    with ExitStack() as ctx:
        def sb(name, shape, dt=F32, stack=ctx):
            return stack.enter_context(nc.sbuf_tensor(name, shape, dt))

        def sem(name):
            return ctx.enter_context(nc.semaphore(name))

        bank = [ctx.enter_context(nc.psum_tensor(f"bank{i}", [P, 512], F32)) for i in range(8)]

        xh = sb("xh", [P, TT, D_MODEL])
        w_raw = sb("w_raw", [P, 2, UNIT])
        w_hi = sb("w_hi", [P, 2, UNIT], F32R)
        w_lo = sb("w_lo", [P, 2, UNIT], F32R)
        ident = sb("ident", [P, P])
        ones = sb("ones", [P, P])
        vec_cols = sb("vec_cols", [P, 296])
        c_col = sb("c_col", [P, 3, KD])
        mod_cols = sb("mod_cols", [P, 6, KD])
        silu_c = c_col[:, 1, :]
        scale1, shift1, gate1, shift2, scale2, gate2 = (mod_cols[:, i, :] for i in range(6))
        wi = sb("wi", [P, TT, HEADS])
        stat = sb("stat", [P, 640])
        up32 = sb("up32", [P, 2, 512])

        act_in = ExitStack()
        act_hi = sb("act_hi", [P, KD, SEQ], F32R, act_in)
        act_lo = sb("act_lo", [P, KD, SEQ], F32R, act_in)
        act_in.close()
        s5_mem = sb("s5_mem", [P, 8192])

        mixer = ExitStack()
        arena = sb("arena", [P, ARENA], stack=mixer)

        def cut(a, *shape):
            n = math.prod(shape)
            assert a + n <= ARENA
            v = arena[:, a:a + n]
            names = "abcd"[:len(shape)]
            if len(shape) == 1:
                return v
            return v.rearrange(f"p ({' '.join(names)}) -> p {' '.join(names)}",
                               **{k: s for k, s in zip(names, shape)})

        KEYS = [P * (t + 1) for t in range(TT)]
        KEYS_AT = [sum(KEYS[:t]) for t in range(TT)]
        q_t, k_t = cut(0, 4, SEQ), cut(2048, 4, SEQ)
        v_tok = cut(4096, TT, 512)
        y_attn, y_ssm = cut(6144, TT, 512), cut(8192, TT, 512)
        pre, rot = cut(12800, TT, 512), cut(14848, TT, 512)
        tmp = cut(16896, 512)
        relu = cut(17408, 2, 512)
        score = [cut(19880 + KEYS_AT[t], KEYS[t]) for t in range(TT)]
        bias = [cut(21160, P)] + score[1:]
        rope = cut(22440, 6, TT, HD)
        vec_rows = cut(18432, 4, P)
        tail_t = cut(17408, 512)[0:TAIL]
        ki_w = cut(19616, TT, TAIL)
        d_eye = cut(25000, GP, CH)[0:2 * CH]
        b_glu_row = cut(25512, 512)[0:1]
        square_at = [up32[:].rearrange("p a n -> p (a n)"), cut(18944, D_MODEL)]
        ada_first = cut(0, 4, KD, 512)
        ada_first_acc = cut(16384, 4, 512)
        ada_next = [cut(0, KD, 512), cut(6144, KD, 512)]
        ada_next_acc = cut(23976, 2, 512)
        ada_late = [cut(0, KD, 512), cut(12032, KD, 512)]
        gate2_w = [cut(7168, KD, 512), cut(3072, KD, 512)]
        ada_late_acc = [cut(20480 + 512 * i, 512) for i in range(4)]
        gate2_acc = [cut(25512, 512), cut(25000, 512)]
        logit = cut(10240, LOGITS, 512)
        prob, prob_t = cut(14336, 2, 512), cut(15360, 2, 512)
        lag_w = [cut(16384, 2, GH, CHUNK + 1, CH), cut(12032, 2, GH, CHUNK + 1, CH)]
        turn = cut(8192, 2, GP, NCH)
        s5_b, s5_c = cut(21288, 2, GP, CH), cut(21800, 2, GP, CH)
        power = cut(19072, 2, CHUNK + 1, GP)
        power_neg = cut(22312, CHUNK, GP)
        power_back = cut(19360, 2, CHUNK, GP)
        s5_bb = cut(22440, 2, GP, CH)
        s5_p = cut(18688, 24, GP)
        scan_r = cut(23464, GH, NCH)
        s5_v = [s5_mem[:, a:a + 2048].rearrange("p (g r n) -> p g r n", g=GH, r=2) for a in (0, 2048)]
        s5_vt = [s5_mem[:, a:a + 2048].rearrange("p (r g j h) -> p r g j h", r=2, g=GH, j=CHUNK) for a in (2048, 0)]
        s5_m = [s5_mem[:, a:a + 2048].rearrange("p (g n) -> p g n", g=NG) for a in (2048, 0)]
        s5_u = s5_mem[:, 4096:5120].rearrange("p (g n) -> p g n", g=NG)
        s5_z = [cut(21288, 512), cut(22952, 512)]
        lags = [s5_mem[0:2 * CH, a:a + 1024].rearrange("p (g l h) -> p g l h", g=GH, l=CHUNK) for a in (0, 2048)]
        c_rows = xh[:, 0:2, :].rearrange("p t n -> p (t n)")[:, 0:1024].rearrange(
            "p (r a q n) -> p r a q n", r=2, a=4, q=2)
        s5_x = s5_mem[:, 5120:7168].rearrange("p (r g q c) -> p r g q c", r=2, g=GH, q=2)
        bb_diag = cut(23976, 2, GP, 2 * CH)
        s5_t = s5_mem[:, 7168:8192].rearrange("p (r n) -> p r n", r=2)
        square_to = [logit[:, i] for i in range(2)]
        chunk_rows = xh[0:NCH, :, :].rearrange("c a n -> c (a n)")
        chunk_in = chunk_rows.rearrange("c (i n) -> c i n", i=CHUNK)
        group_in = xh[NCH:2 * NCH, :, :].rearrange("c a n -> c (a n)").rearrange("c (g m) -> c g m", g=GROUPS)
        x_tok = cut(16384, TT, D_MODEL)
        h_t = xh[:].rearrange("p t n -> p (t n)").rearrange("p (k s) -> p k s", k=KD)
        h_sq, h_sq_sum = cut(16384, KD, 512), cut(23552, 512)
        out_tok = s5_mem[:, 0:TT * D_MODEL].rearrange("p (t n) -> p t n", t=TT)
        rstd_diag = cut(25000, TT, P)
        mixer.close()
        index_at = ExitStack()
        sb("before_lo", [P, 6144], stack=index_at)
        qi_lo = sb("qi_lo", [P, 4, SEQ], F32R, index_at)
        sb("before_hi", [P, 10240 - 8192], stack=index_at)
        qi_hi = sb("qi_hi", [P, 4, SEQ], F32R, index_at)
        ki_hi = sb("ki_hi", [P, SEQ], F32R, index_at)
        index_at.close()
        late_index = ExitStack()
        sb("before_ki_lo", [P, 24000], stack=late_index)
        ki_lo = sb("ki_lo", [P, SEQ], F32R, late_index)
        late_index.close()

        ff_hi = sb("ff_hi", [P, FT, SEQ], F32R)
        ff_lo = sb("ff_lo", [P, FT, SEQ], F32R)
        conv = sb("conv", [P, 4, SEQ])

        ss_x, rstd_x = stat[:, 0:4], stat[:, 4:8]
        ss_qk, rstd_qk = stat[:, 8:72], stat[:, 72:136]
        top8 = [stat[:, 136:144], stat[:, 600:608]]
        neg_max = stat[:, 144:176]
        psum_p = stat[:, 176:208]
        q_scale = stat[:, 208:240]
        ss_y, rstd_y = stat[:, 240:248], stat[:, 248:256]
        work = stat[:, 256:384]
        ss_h, rstd_h = stat[:, 384:388], stat[:, 388:392]
        rinv = stat[:, 392:424]
        pos_f = stat[:, 424:428]
        pos_i = stat[:, 428:432].bitcast(I32)
        inv_bc = stat[:, 432:464]
        gq_bc, gk_bc = stat[:, 464:528], stat[:, 528:592]
        dt_rows = stat[:, 592:594]

        C_BADA, C_NMIX, C_NFFN, C_NSSM, C_NATT, C_W0, C_W1, C_W2, C_CB, C_ARE, C_AIM, C_LDT = (
            0, 48, 56, 64, 68, 72, 116, 160, 204, 248, 264, 280)

        S = {n: sem(n) for n in (
            "ident_ready", "ones_ready", "rows_loaded", "dt_spread", "vec_t", "c_loaded", "pos_loaded",
            "bc_loaded", "x_loaded", "ss_x_ready", "rstd_x_ready", "xn_ready", "tanh_c", "silu_ready",
            "angle_ready", "sin_ready", "ada_first_loaded0", "ada_first_loaded1", "ada_first_loaded2",
            "ada_first_loaded3", "ada_acc_ready", "ada_acc_pool", "mod_ready", "mod1_ready", "x_t_ready",
            "x_t_read", "act_in_ready", "raw_loaded0", "raw_loaded1", "hi_ready", "lo_ready", "weights_used",
            "tail_read", "tail_t", "tail_t_read", "proj_ready", "proj_read", "rot_ready", "turned_ready",
            "turned_read", "u_stored", "ada_next_loaded0", "ada_next_loaded1", "ada_used", "ada_sum_ready",
            "ss_qk_ready", "sq_used", "score_mm", "relu_ready", "relu_used", "future_set", "logit_mm",
            "logit_ready", "prob_ready", "prob_turned", "prob_t_ready", "pv_done", "y_attn_ready", "u_loaded",
            "u_grouped", "s5_loaded", "c_rows_loaded", "lag_w_ready", "turn_ready", "ada_sums_read",
            "gate2_ready", "bb_ready", "index_hi_ready", "x_turned", "x_turned_read", "sq_summed",
            "hn_hi_ready", "ss_h_mm", "rstd_diag_ready", "rstd_spread", "c_t", "c_t_read", "s5_angle",
            "s5_sin", "s5_params", "vt_ready", "v_t", "v_ready", "lag_mm", "lags_ready", "lags_stored",
            "zeros_stored", "m_loaded", "zero_ready", "lag_d_added", "u_t", "u_t_read", "state_mm",
            "state_read", "s5_state", "y_mm", "y_read", "y_stored", "y_loaded", "gelu_ready", "g_t",
            "g_t_read", "glu_in", "glu_mm", "tanh_z", "glu_read", "ss_y_ready", "yn_ready", "mix_t",
            "mix_t_read", "mix_in", "out_mm", "h_ready", "ss_h_ready", "hn_ready", "mlp_in", "up_mm",
            "tap_ready", "conv_read", "conv_ready", "gelu_up", "ff32_ready", "ff_hi_ready", "ff_lo_ready",
            "down_mm", "down_scaled", "down_t", "sum_ready", "stored", "dve_chain", "act_chain", "pool_chain",
            "d_loaded", "x_again", "b_rows_loaded",
        )}

        def unit_view(buf, n, *shape):
            k, m = shape
            return buf[:, n % 2, 0:k * m].rearrange("p (k m) -> p k m", k=k)

        def source_of_v(E, link, half, scratch):
            gs = slice(GH * half, GH * (half + 1))
            vt, t1 = s5_vt[half], scratch.rearrange("p (g j h) -> p g j h", g=GH, j=CHUNK)
            br, bi = (s5_bb[:, i, gs].unsqueeze(2).broadcast_to([P, GH, CHUNK, CH]) for i in range(2))
            pr, pi = (power_back[:, i, :, gs].rearrange("p j g -> p g j").unsqueeze(3).broadcast_to(
                [P, GH, CHUNK, CH]) for i in range(2))
            E.tensor_tensor(vt[:, 0], br, pr, ALU.mult)
            link(E.tensor_tensor(t1, bi, pi, ALU.mult))
            link(E.tensor_tensor(vt[:, 0], vt[:, 0], t1, ALU.subtract))
            E.tensor_tensor(vt[:, 1], br, pi, ALU.mult)
            link(E.tensor_tensor(t1, bi, pr, ALU.mult))
            E.tensor_tensor(vt[:, 1], vt[:, 1], t1, ALU.add).then_inc(S["vt_ready"], 1)

        block = ctx.enter_context(nc.Block())

        @block.sync
        def _(sp):
            def load(dst, src, s):
                sp.dma_start(dst, src).then_inc(S[s], 16)

            def unit(n, dst, src):
                if n >= 2:
                    sp.wait_ge(S["lo_ready"], n - 1)
                sp.dma_start(dst, src).then_inc(S[f"raw_loaded{n % 2}"], 16)

            load(c_col[:, 0, :], c.rearrange("a (p k) -> p (a k)", p=P), "c_loaded")
            for t in range(TT):
                load(xh[:, t, :], x[0, t * P:(t + 1) * P, :], "x_loaded")
            sp.dma_start(pos_i, positions[0].rearrange("(a p) -> p a", p=P), allow_slow_non_contiguous=True
                         ).then_inc(S["pos_loaded"], 16)
            load(inv_bc, inv_freq[0].partition_broadcast(P), "bc_loaded")
            load(gq_bc, q_norm[0].partition_broadcast(P), "bc_loaded")
            load(gk_bc, k_norm[0].partition_broadcast(P), "bc_loaded")
            rows = lambda v, n: v.rearrange("(a p) -> a p", a=n)
            load(vec_rows[0:48, 0, :], rows(b_ada[0], 48), "rows_loaded")
            load(vec_rows[48:56, 0, :], rows(norm_mix[0], KD), "rows_loaded")
            load(vec_rows[56:64, 0, :], rows(norm_ffn[0], KD), "rows_loaded")
            load(vec_rows[64:68, 0, :], rows(out_norm_ssm[0], 4), "rows_loaded")
            load(vec_rows[68:72, 0, :], rows(out_norm_attn[0], 4), "rows_loaded")
            load(vec_rows[0:88, 1, :], conv_w[0, 0:2, :].rearrange("j (a p) -> (j a) p", p=P), "rows_loaded")
            load(vec_rows[0:44, 2, :], rows(conv_w[0, 2, :], 44), "rows_loaded")
            load(vec_rows[44:88, 2, :], rows(conv_b[0], 44), "rows_loaded")
            load(vec_rows[0:GP, 3, :], ssm_a_re[0].rearrange("(g q) p -> g (q p)", q=2), "rows_loaded")
            load(vec_rows[GP:2 * GP, 3, :], ssm_a_im[0].rearrange("(g q) p -> g (q p)", q=2), "rows_loaded")
            load(dt_rows[32:32 + GP, :], ssm_log_dt[0].rearrange("(g q) -> g q", q=2), "rows_loaded")
            load(b_glu_row, ssm_b_glu, "b_rows_loaded")
            for q in range(2):
                load(d_eye[CH * q:CH * q + CH], ssm_d[0].rearrange("(g q h) -> q g h", q=2, h=CH)[q].partition_broadcast(CH),
                     "d_loaded")
            wa = w_ada[0].rearrange("(p k) n -> p k n", k=KD)
            for i in range(4):
                load(ada_first[:, i], wa[:, :, i * 512:(i + 1) * 512], f"ada_first_loaded{i}")
            sp.wait_ge(S["zero_ready"], 1)
            for i in range(2):
                sp.dma_start(lag_dram[:, NG * i:NG * (i + 1), 0:CHUNK - 1, :],
                             s5_mem[0:CH, 0:NG * (CHUNK - 1) * CH].rearrange("p (g l h) -> p g l h", g=NG, l=CHUNK - 1)
                             ).then_inc(S["zeros_stored"], 16)

            w_in_k = w_in[0].rearrange("(k p) n -> p k n", p=P)
            unit(U_TAIL, unit_view(w_raw, U_TAIL, KD, TAIL), w_in_k[:, :, 2560:2560 + TAIL])

            def later_ada(first, last):
                for n in range(first, last):
                    if n < 2:
                        sp.wait_ge(S["mod_ready"], 1)
                        dst = ada_next[n]
                    elif n < 6:
                        sp.wait_ge(*((S["y_attn_ready"], TT) if n < 4 else (S["ada_used"], n - 1)))
                        dst = ada_late[n % 2]
                    else:
                        sp.wait_ge(S["ada_used"], 6)
                        sp.wait_ge(S["mix_t"], KD)
                        dst = gate2_w[n - 6]
                    a = 2048 + 512 * n
                    load(dst, wa[:, :, a:a + 512], f"ada_next_loaded{n % 2}")

            pieces = {U_QI: (0, 1), U_QI + 1: (1, 2)}
            for n0 in (U_QI, U_U, U_K, U_Q, U_V):
                for kh in range(2):
                    unit(n0 + kh, unit_view(w_raw, n0 + kh, 4, 512),
                         w_in_k[:, 4 * kh:4 * kh + 4, COLS[n0]:COLS[n0] + 512])
                    later_ada(*pieces.get(n0 + kh, (0, 0)))
                if n0 == U_QI:
                    sp.wait_ge(S["x_t_ready"], KD)
                    for i, (bsrc, csrc) in enumerate(((ssm_b_re, ssm_c_re), (ssm_b_im, ssm_c_im))):
                        for q in range(2):
                            load(c_rows[:, i, :, q, :], csrc[0].rearrange("(a g) h p -> (g h) a p", a=4), "c_rows_loaded")
                        load(s5_b[:, i], bsrc[0].rearrange("(g q) p h -> (q p) g h", q=2), "s5_loaded")
                if n0 == U_K:
                    for t in range(TT):
                        sp.wait_ge(S["proj_read"], 4 + t + 1)
                        sp.dma_start(u_dram[t * P:(t + 1) * P, :], v_tok[:, t, :]).then_inc(S["u_stored"], 16)
            unit(U_GLU, unit_view(w_raw, U_GLU, 4, 512), ssm_w_glu[0].rearrange("(k p) n -> p k n", p=P))
            w_out_k = w_out[0].rearrange("(k p) n -> p k n", p=P)
            for n in range(2):
                unit(U_OUT + n, unit_view(w_raw, U_OUT + n, KD, 256), w_out_k[:, :, 256 * n:256 * n + 256])

            sp.wait_ge(S["c_t"], 1)
            sp.wait_ge(S["u_stored"], 16 * TT)
            load(chunk_rows, u_dram.rearrange("(c i) n -> c (i n)", i=CHUNK), "u_loaded")
            sp.wait_ge(S["zeros_stored"], 32)
            for half in range(2):
                sp.wait_ge(S["lag_d_added"], 2 * half + 2)
                gs = slice(NG * half, NG * (half + 1))
                for q in range(2):
                    sp.dma_start(lag_dram[:, gs].rearrange("c (g q) l h -> c q g l h", q=2)[:, q, :, CHUNK - 1:, :],
                                 lags[half][CH * q:CH * q + CH]).then_inc(S["lags_stored"], 16)
                sp.wait_ge(S["lags_stored"], 32 * (half + 1))
                sp.wait_ge(S["v_ready"], 4 * half + 4)
                for j in range(CHUNK):
                    load(s5_m[half][CH * j:CH * (j + 1)].rearrange("p g (l h) -> p g l h", l=CHUNK),
                         lag_dram[:, gs, CHUNK - 1 - j:2 * CHUNK - 1 - j, :], "m_loaded")
            sp.wait_ge(S["y_mm"], 4)
            sp.wait_ge(S["logit_ready"], 3 * HEADS)
            for t in range(TT):
                load(x_tok[:, t, :], x[0, t * P:(t + 1) * P, :], "x_again")
            sp.wait_ge(S["y_read"], 4)
            sp.dma_start(y_dram.rearrange("(c i) n -> c (i n)", i=CHUNK), chunk_rows).then_inc(S["y_stored"], 16)
            sp.wait_ge(S["y_stored"], 16)
            load(y_ssm, y_dram.rearrange("(a p) n -> p a n", p=P), "y_loaded")
            later_ada(2, 4)
            for n in range(2, 4):
                unit(U_OUT + n, unit_view(w_raw, U_OUT + n, KD, 256), w_out_k[:, :, 256 * n:256 * n + 256])
                later_ada(2 * n, 2 * n + 2)

            w_up_k = w_up[0].rearrange("(k p) (s n) -> p k s n", p=P, s=2)
            with sp.Fori(0, UPS) as j:
                for kh in range(2):
                    sp.wait_ge(S["lo_ready"], j * 2 + (U_UP + kh - 1))
                    for s in range(2):
                        sp.dma_start(w_raw[:, (U_UP + kh) % 2, :].rearrange("p (k s n) -> p k s n", k=4, s=2)[:, :, s, :],
                                     w_up_k[:, 4 * kh:4 * kh + 4, s, bass.ds(j * 256, 256)]
                                     ).then_inc(S[f"raw_loaded{(U_UP + kh) % 2}"], 16)
            with sp.Fori(0, FT // 2 - 1, 2) as j:
                for i in range(2):
                    sp.wait_ge(S["lo_ready"], j + (U_DOWN + i - 1))
                    for k in range(2):
                        sp.dma_start(w_raw[:, (U_DOWN + i) % 2, 1024 * k:1024 * k + 1024],
                                     w_down[0][bass.ds(j * 256 + (256 * i + P * k), P), :]
                                     ).then_inc(S[f"raw_loaded{(U_DOWN + i) % 2}"], 16)
            sp.wait_ge(S["lo_ready"], UNITS - 2)
            for k in range(2):
                sp.dma_start(w_raw[:, (UNITS - 1) % 2, 1024 * k:1024 * k + 1024],
                             w_down[0, (FT - 2 + k) * P:(FT - 1 + k) * P, :]
                             ).then_inc(S[f"raw_loaded{(UNITS - 1) % 2}"], 16)
            for n in range(4):
                sp.wait_ge(S["sum_ready"], 2 * n + 2)
                sp.dma_start(out[0].rearrange("(a p) n -> p a n", p=P)[:, :, 256 * n:256 * n + 256],
                             out_tok[:, :, 256 * n:256 * n + 256]).then_inc(S["stored"], 16)
            sp.wait_ge(S["stored"], 64)

        def raw_count(n):
            total = 0
            for i in range(n % 2, n + 1, 2):
                total += 2 if i >= U_UP else 1
            return 16 * total

        @block.gpsimd
        def _(pool):
            G = nc.gpsimd
            chain = [0]

            def link(ins):
                chain[0] += 1
                ins.then_inc(S["pool_chain"], 1)
                pool.wait_ge(S["pool_chain"], chain[0])

            def lo(slot, width=UNIT):
                nc.gpsimd.tensor_tensor(w_lo[:, slot, 0:width], w_raw[:, slot, 0:width],
                                        w_hi[:, slot, 0:width].bitcast(F32), ALU.subtract).then_inc(S["lo_ready"], 1)

            link(nc.gpsimd.memset(ident[:], 0.0))
            nc.gpsimd.affine_select(out=ident[:], in_=ident[:], compare_op=ALU.not_equal, fill=1.0, base=0,
                                    pattern=[[-1, P]], channel_multiplier=1).then_inc(S["ident_ready"], 1)
            nc.gpsimd.memset(ones[:], 1.0).then_inc(S["ones_ready"], 1)
            nc.gpsimd.memset(s5_mem[:, 0:2048], 0.0).then_inc(S["zero_ready"], 1)
            link(nc.gpsimd.memset(bias[0], 0.0))
            link(nc.gpsimd.affine_select(out=bias[0], in_=bias[0], compare_op=ALU.is_ge, fill=MASK, base=0,
                                         pattern=[[-1, P]], channel_multiplier=1))

            pool.wait_ge(S["silu_ready"], 1)
            pool.wait_ge(S["ada_first_loaded1"], 16)
            acc, w = ada_first_acc[:, 1], ada_first[:, 1]
            link(G.tensor_tensor(w, w, silu_c.unsqueeze(2).broadcast_to([P, KD, 512]), ALU.mult))
            link(G.tensor_tensor(w[:, 0:4], w[:, 0:4], w[:, 4:8], ALU.add))
            link(G.tensor_tensor(w[:, 0:2], w[:, 0:2], w[:, 2:4], ALU.add))
            G.tensor_tensor(acc, w[:, 0], w[:, 1], ALU.add).then_inc(S["ada_acc_pool"], 1)

            def future(t):
                pool.wait_ge(S["relu_used"], HEADS * t)
                diag = score[t][:, t * P:(t + 1) * P]
                nc.gpsimd.affine_select(out=diag, in_=diag, compare_op=ALU.is_ge, fill=FUTURE, base=0,
                                        pattern=[[-1, P]], channel_multiplier=1).then_inc(S["future_set"], 1)

            def weigh_lags(half):
                gs = slice(GH * half, GH * (half + 1))
                w = lag_w[half]
                t1 = up32[:].rearrange("p a n -> p (a n)").rearrange("p (g l h) -> p g l h", g=GH, l=CHUNK)
                spread = lambda v: v.rearrange("p l g -> p g l").unsqueeze(3).broadcast_to([P, GH, CHUNK, CH])
                cr, ci = (s5_c[:, i, gs].unsqueeze(2).broadcast_to([P, GH, CHUNK, CH]) for i in range(2))
                pr, pi, ni = (spread(v[:, :, gs]) for v in (power[:, 0, 1:, :], power[:, 1, 1:, :], power_neg))
                o_r, o_i = w[:, 0, :, 1:, :], w[:, 1, :, 1:, :]
                G.tensor_copy(w[:, 0, :, 0, :], s5_c[:, 0, gs])
                G.tensor_copy(w[:, 1, :, 0, :], s5_c[:, 1, gs])
                G.tensor_tensor(o_r, cr, pr, ALU.mult)
                link(G.tensor_tensor(t1, ci, pi, ALU.mult))
                link(G.tensor_tensor(o_r, o_r, t1, ALU.add))
                G.tensor_tensor(o_i, cr, ni, ALU.mult)
                link(G.tensor_tensor(t1, ci, pr, ALU.mult))
                G.tensor_tensor(o_i, o_i, t1, ALU.add).then_inc(S["lag_w_ready"], 1)
                pool.wait_ge(S["lag_w_ready"], half + 1)

            def turn_step(n):
                w1, w2, w3, w4, q1, q2 = (s5_p[:, i] for i in (20, 21, 22, 23, 4, 5))
                if n == 1:
                    pool.wait_ge(S["s5_params"], 1)
                    pool.wait_ge(S["ada_used"], 2)
                    G.memset(turn[:, 0, :, 0:1], 1.0)
                    G.memset(turn[:, 1, :, 0:1], 0.0)
                    G.tensor_copy(w3, s5_p[:, 17])
                    link(G.tensor_copy(w4, s5_p[:, 18]))
                t1, t2 = (up32[:, i, 0:GP * n].rearrange("p (g c) -> p g c", g=GP) for i in range(2))
                a_r, a_i = turn[:, 0, :, 0:n], turn[:, 1, :, 0:n]
                o_r, o_i = turn[:, 0, :, n:2 * n], turn[:, 1, :, n:2 * n]
                f_r, f_i = (v.unsqueeze(2).broadcast_to([P, GP, n]) for v in (w3, w4))
                G.tensor_tensor(o_r, a_r, f_r, ALU.mult)
                G.tensor_tensor(t1, a_i, f_i, ALU.mult)
                G.tensor_tensor(o_i, a_r, f_i, ALU.mult)
                G.tensor_tensor(t2, a_i, f_r, ALU.mult)
                G.tensor_tensor(w1, w3, w3, ALU.mult)
                G.tensor_tensor(w2, w4, w4, ALU.mult)
                link(G.tensor_tensor(q1, w3, w4, ALU.mult))
                G.tensor_tensor(o_r, o_r, t1, ALU.subtract)
                ins = G.tensor_tensor(o_i, o_i, t2, ALU.add)
                if 2 * n == NCH:
                    ins.then_inc(S["turn_ready"], 1)
                    return
                G.tensor_tensor(w3, w1, w2, ALU.subtract)
                link(G.tensor_tensor(w4, q1, q1, ALU.add))

            def sum_squares(m):
                pool.wait_ge(S["ss_h_ready"], m + 1)
                if m == 1:
                    link(G.tensor_tensor(h_sq_sum, h_sq[:, 0], h_sq[:, 1], ALU.add))
                elif m > 1:
                    ins = G.tensor_tensor(h_sq_sum, h_sq_sum, h_sq[:, m], ALU.add)
                    if m < KD - 3:
                        link(ins)
                    else:
                        ins.then_inc(S["sq_summed"], 1)

            for n in range(U_UP + 2):
                pool.wait_ge(S["hi_ready"], n + 1)
                lo(n % 2, KD * TAIL if n == U_TAIL else UNIT)
                if U_OUT + 2 <= n < U_UP + 1:
                    sum_squares(2 * (n - U_OUT - 2))
                    sum_squares(2 * (n - U_OUT - 2) + 1)
                if n == U_Q:
                    for t in range(1, TT):
                        future(t)
                for i in {U_U + 1: (1, 2), U_K: (4,), U_K + 1: (8, 16, 32)}.get(n, ()):
                    turn_step(i)
                if n == U_OUT:
                    pool.wait_ge(S["turned_ready"], 13)
                    for half in range(2):
                        weigh_lags(half)
                    pool.wait_ge(S["lags_stored"], 32)
                    pool.wait_ge(S["vt_ready"], 1)
                    source_of_v(G, link, 1, up32[:].rearrange("p a n -> p (a n)"))
            with pool.Fori(2, 2 * UPS + 10, 2) as j:
                for i in range(2):
                    pool.wait_ge(S["hi_ready"], j + (U_UP + i + 1))
                    lo((U_UP + i) % 2)
            pool.wait_ge(S["hi_ready"], UNITS)
            lo((UNITS - 1) % 2)

        @block.scalar
        def _(act):
            chain = [0]

            def link(ins):
                chain[0] += 1
                ins.then_inc(S["act_chain"], 1)
                act.wait_ge(S["act_chain"], chain[0])

            def hi(n, width=UNIT):
                act.wait_ge(S[f"raw_loaded{n % 2}"], raw_count(n))
                if n >= 2:
                    act.wait_ge(S["weights_used"], n - 1)
                nc.scalar.activation(w_hi[:, n % 2, 0:width], w_raw[:, n % 2, 0:width], ACT.Copy
                                     ).then_inc(S["hi_ready"], 1)

            act.wait_ge(S["c_loaded"], 16)
            nc.scalar.activation(c_col[:, 2, :], c_col[:, 0, :], ACT.Tanh, scale=0.5).then_inc(S["tanh_c"], 1)
            act.wait_ge(S["x_loaded"], 16 * TT)
            for t in range(TT):
                if t >= 2:
                    act.wait_ge(S["ss_x_ready"], t - 1)
                nc.scalar.activation(square_at[t % 2], xh[:, t, :], ACT.Square,
                                     accum_out=ss_x[:, t:t + 1]).then_inc(S["ss_x_ready"], 1)
            act.wait_ge(S["angle_ready"], 1)
            nc.scalar.activation(rope[:, 1], rope[:, 3], ACT.Sin).then_inc(S["sin_ready"], 1)
            nc.scalar.activation(rope[:, 0], rope[:, 2], ACT.Sin).then_inc(S["sin_ready"], 1)
            act.wait_ge(S["rstd_x_ready"], 1)
            for t in range(TT):
                nc.scalar.activation(xh[:, t, :], xh[:, t, :], ACT.Copy, scale=rstd_x[:, t:t + 1]
                                     ).then_inc(S["xn_ready"], 1)
            hi(U_TAIL, KD * TAIL)
            hi(U_QI)
            act.wait_ge(S["mod1_ready"], 1)
            for k in range(KD):
                act.wait_ge(S["x_t_ready"], k + 1)
                if k >= 2:
                    act.wait_ge(S["act_in_ready"], k - 1)
                nc.scalar.activation(up32[:, k % 2, :], bank[k % 4][:], ACT.Identity, scale=scale1[:, k:k + 1],
                                     bias=shift1[:, k:k + 1]).then_inc(S["x_t_read"], 1)

            def results(nth, n_last, dst, width=512, before=None):
                for t in range(TT):
                    if t < TT - 1:
                        act.wait_ge(S["proj_ready"], 3 * nth + t + 1)
                    else:
                        act.wait_ge(S["weights_used"], n_last + 1)
                    if before is not None:
                        before(t)
                    nc.scalar.activation(dst[:, t, 0:width], bank[t][:, 0:width], ACT.Copy).then_inc(S["proj_read"], 1)

            turned = [0]

            def turned_read(dst):
                for t in range(TT):
                    act.wait_ge(S["turned_ready"], turned[0] + 1)
                    nc.scalar.activation(dst[:, :, t * P:(t + 1) * P],
                                         bank[4 + turned[0] % 2][:].rearrange("p (g t) -> p g t", g=4), ACT.Copy
                                         ).then_inc(S["turned_read"], 1)
                    turned[0] += 1

            def squares(which):
                if which == 0:
                    act.wait_ge(S["turn_ready"], 1)
                for t in range(TT):
                    n = 4 * which + t
                    act.wait_ge(S["proj_read"], 4 * (2 + which) + t + 1)
                    if n >= 2:
                        act.wait_ge(S["sq_used"], n - 1)
                    nc.scalar.activation(up32[:, n % 2, :], pre[:, t, :], ACT.Square).then_inc(S["ss_qk_ready"], 1)

            act.wait_ge(S["weights_used"], U_TAIL + 1)
            nc.scalar.activation(tail_t, bank[6][0:TAIL, :], ACT.Copy).then_inc(S["tail_read"], 1)
            hi(U_QI + 1)
            hi(U_U)
            act.wait_ge(S["tail_t"], 1)
            nc.scalar.activation(ki_w, bank[5][:, 0:TT * TAIL].rearrange("p (t n) -> p t n", t=TT), ACT.Copy
                                 ).then_inc(S["tail_t_read"], 1)
            act.wait_ge(S["s5_angle"], 1)
            nc.scalar.activation(s5_p[:, 8:10], s5_p[:, 6:8], ACT.Sin).then_inc(S["s5_sin"], 1)
            results(0, U_QI + 1, pre)
            hi(U_U + 1)
            hi(U_K)
            results(1, U_U + 1, v_tok)
            hi(U_K + 1)
            act.wait_ge(S["c_t"], 1)
            for r in range(2):
                for q in range(2):
                    hp = slice(64 * q, 64 * q + 64)
                    nc.scalar.activation(s5_c[hp, r],
                                         bank[5 + r][hp, :].rearrange("p (g q h) -> p g q h", g=GP, q=2)[:, :, q, :],
                                         ACT.Copy, scale=(1.0, -1.0)[r]).then_inc(S["c_t_read"], 1)
            act.wait_ge(S["turned_ready"], 1)
            nc.scalar.activation(ki_hi[:], bank[4][:], ACT.Copy).then_inc(S["index_hi_ready"], 1)
            for t in range(TT):
                act.wait_ge(S["turned_ready"], t + 2)
                nc.scalar.activation(qi_hi[:, :, t * P:(t + 1) * P],
                                     bank[4 + (t + 1) % 2][:].rearrange("p (g t) -> p g t", g=4), ACT.Copy
                                     ).then_inc(S["index_hi_ready"], 1)
            turned[0] = 5
            hi(U_Q)
            results(2, U_K + 1, pre, before=lambda t: act.wait_ge(S["rot_ready"], 1 + t + 1))
            for i in range((TT - 1) * HEADS):
                t = 1 + i // HEADS
                act.wait_ge(S["score_mm"], i + 1)
                if i >= 2:
                    act.wait_ge(S["relu_used"], i - 1)
                nc.scalar.activation(relu[:, i % 2, 0:KEYS[t]], bank[6 + i % 2][:, 0:KEYS[t]], ACT.Relu
                                     ).then_inc(S["relu_ready"], 1)
            hi(U_Q + 1)
            squares(0)
            hi(U_V)
            results(3, U_Q + 1, pre, before=lambda t: act.wait_ge(S["rot_ready"], 5 + t + 1))
            hi(U_V + 1)
            squares(1)
            turned_read(k_t)
            hi(U_GLU)
            results(4, U_V + 1, v_tok, before=lambda t: act.wait_ge(S["u_stored"], 16 * TT))
            turned_read(q_t)
            hi(U_OUT)

            act.wait_ge(S["u_loaded"], 16)
            for i in range(2):
                gs = slice(NG * i, NG * (i + 1))
                nc.scalar.activation(
                    group_in[:, gs, :].rearrange("c g (i h) -> c g i h", i=CHUNK),
                    chunk_in.rearrange("c i (g h) -> c g i h", g=GROUPS)[:, gs], ACT.Copy).then_inc(S["u_grouped"], 1)

            def s5(stage, half, part):
                if stage == "x":
                    for k in (2 * half, 2 * half + 1):
                        act.wait_ge(S["x_turned"], k + 1)
                        if k == 0:
                            act.wait_ge(S["y_stored"], 16)
                        nc.scalar.activation(h_t[:, k, :], bank[6 + k % 2][:], ACT.Copy).then_inc(S["x_turned_read"], 1)
                    return
                for b in range(2):
                    i = 2 * part + b
                    src = bank[6 + b]
                    if stage == "V":
                        act.wait_ge(S["v_t"], 4 * half + i + 1)
                        if i == 0:
                            act.wait_ge(S["zeros_stored"], 32)
                            if half:
                                act.wait_ge(S["y_mm"], 2)
                        nc.scalar.activation(s5_v[half][:, 2 * i:2 * i + 2],
                                             src[:].rearrange("p (g r n) -> p g r n", g=2, r=2), ACT.Copy
                                             ).then_inc(S["v_ready"], 1)
                    elif stage == "u":
                        act.wait_ge(S["u_t"], 2 * half + i + 1)
                        nc.scalar.activation(s5_u[:, 8 * i:8 * i + 8], src[:].rearrange("p (g n) -> p g n", g=8),
                                             ACT.Copy).then_inc(S["u_t_read"], 1)
                    elif stage == "lags":
                        act.wait_ge(S["lag_mm"], 2 * half + i + 1)
                        nc.scalar.activation(lags[half][:, 4 * i:4 * i + 4],
                                             src[0:2 * CH, :].rearrange("p (g l h) -> p g l h", g=4, l=CHUNK),
                                             ACT.Copy).then_inc(S["lags_ready"], 1)
                    elif stage == "y":
                        act.wait_ge(S["y_mm"], 2 * half + i + 1)
                        g = GH * half + 4 * i
                        for q in range(2):
                            ins = nc.scalar.activation(
                                chunk_in.rearrange("c i (g q h) -> c q g i h", q=2, h=CH)[:, q, g:g + 4],
                                src[NCH * q:NCH * (q + 1), :].rearrange("c (g i h) -> c g i h", g=4, i=CHUNK), ACT.Copy)
                        ins.then_inc(S["y_read"], 1)

            def turned_probs(i):
                t = i // HEADS
                act.wait_ge(S["prob_turned"], i + 1)
                if i >= 2:
                    act.wait_ge(S["pv_done"], i - 1)
                nc.scalar.activation(prob_t[:, i % 2, 0:KEYS[t]], bank[2 + i % 2][:, 0:KEYS[t]], ACT.Copy
                                     ).then_inc(S["prob_t_ready"], 1)

            for i in range(ATT_UNITS):
                t = i // HEADS
                act.wait_ge(S["logit_ready"], i + 1)
                if i >= 2:
                    act.wait_ge(S["prob_turned"], i - 1)
                nc.scalar.activation(prob[:, i % 2, 0:KEYS[t]], logit[:, i % LOGITS, 0:KEYS[t]], ACT.Exp, scale=-1.0,
                                     bias=neg_max[:, i:i + 1], accum_out=psum_p[:, i:i + 1]
                                     ).then_inc(S["prob_ready"], 1)
                if i >= 1:
                    turned_probs(i - 1)
                if i in S5_AT:
                    s5(*S5_AT[i])
            turned_probs(ATT_UNITS - 1)

            act.wait_ge(S["y_loaded"], 16)
            for t in range(TT):
                nc.scalar.activation(y_ssm[:, t, :], y_ssm[:, t, :], ACT.Gelu_apprx_tanh).then_inc(S["gelu_ready"], 1)
            for k in range(4):
                act.wait_ge(S["g_t"], k + 1)
                if k >= 2:
                    act.wait_ge(S["glu_in"], k - 1)
                nc.scalar.activation(up32[:, k % 2, :], bank[k][:], ACT.Copy).then_inc(S["g_t_read"], 1)
            for t in range(TT):
                act.wait_ge(S["y_attn_ready"], t + 1)
                if t >= 1:
                    act.wait_ge(S["ss_y_ready"], t)
                nc.scalar.activation(square_to[t % 2], y_attn[:, t, :], ACT.Square,
                                     accum_out=ss_y[:, TT + t:TT + t + 1]).then_inc(S["ss_y_ready"], 1)
            for t in range(TT):
                if t < TT - 1:
                    act.wait_ge(S["glu_mm"], t + 1)
                else:
                    act.wait_ge(S["weights_used"], U_GLU + 1)
                if t >= 2:
                    act.wait_ge(S["glu_read"], t - 1)
                if t == 0:
                    act.wait_ge(S["glu_in"], 4)
                nc.scalar.activation(up32[:, t % 2, :], bank[4 + t][:], ACT.Tanh, scale=0.5).then_inc(S["tanh_z"], 1)
            hi(U_OUT + 1)
            for t in range(TT):
                act.wait_ge(S["glu_read"], t + 1)
                nc.scalar.activation(square_to[t % 2], y_ssm[:, t, :], ACT.Square,
                                     accum_out=ss_y[:, t:t + 1]).then_inc(S["ss_y_ready"], 1)
                if t >= 1:
                    act.wait_ge(S["ss_y_ready"], TT + t)
            for k in MIX_ORDER:
                n = MIX_ORDER.index(k)
                act.wait_ge(S["mix_t"], n + 1)
                if n >= 2:
                    act.wait_ge(S["mix_in"], n - 1)
                nc.scalar.activation(up32[:, n % 2, :], bank[n % 4][:], ACT.Copy,
                                     scale=vec_cols[:, C_NSSM + k:C_NSSM + k + 1]).then_inc(S["mix_t_read"], 1)
            for n in range(4):
                hi(U_OUT + 2 + n)
                for m in (2 * n, 2 * n + 1):
                    act.wait_ge(S["h_ready"], m + 1)
                    nc.scalar.activation(h_sq[:, m], h_t[:, m], ACT.Square).then_inc(S["ss_h_ready"], 1)
            for k in range(KD):
                act.wait_ge(S["hn_ready"], k + 1)
                nc.scalar.activation(act_hi[:, k, :], up32[:, k % 2, :], ACT.Identity, bias=shift2[:, k:k + 1]
                                     ).then_inc(S["hn_hi_ready"], 1)
            act.wait_ge(S["mlp_in"], KD)

            def hi_ahead(j, kh):
                act.wait_ge(S[f"raw_loaded{kh}"], j * 32 + (raw_count(U_UP + kh) + 32))
                act.wait_ge(S["weights_used"], j * 2 + (U_UP + kh + 1))
                nc.scalar.activation(w_hi[:, kh, :], w_raw[:, kh, :], ACT.Copy).then_inc(S["hi_ready"], 1)

            with act.Fori(0, UPS) as j:
                hi_ahead(j, 0)
                for q in range(4):
                    f = (0, 1, FT, FT + 1)[q]
                    if q < 3:
                        act.wait_ge(S["up_mm"], j * 3 + (q + 1))
                    else:
                        act.wait_ge(S["weights_used"], j * 2 + (U_UP + 2))
                    nc.scalar.activation(conv[:, q, :], bank[q][:], ACT.Identity,
                                         scale=vec_cols[:, bass.ds(j * 2 + (C_W2 + f), 1)],
                                         bias=vec_cols[:, bass.ds(j * 2 + (C_CB + f), 1)]
                                         ).then_inc(S["tap_ready"], 1)
                hi_ahead(j, 1)
                for q in range(2):
                    act.wait_ge(S["conv_ready"], j * 4 + (q + 1))
                    nc.scalar.activation(conv[:, q, :], conv[:, q, :], ACT.Gelu_apprx_tanh
                                         ).then_inc(S["gelu_up"], 1)
                for q in range(2):
                    act.wait_ge(S["ff32_ready"], j * 2 + (q + 1))
                    nc.scalar.activation(ff_hi[:, bass.ds(j * 2 + q, 1), :].rearrange("p a t -> p (a t)"),
                                         up32[:, q, :], ACT.Copy).then_inc(S["ff_hi_ready"], 1)
            for n in range(U_DOWN + 2, UNITS):
                hi(n)
            for n in range(KD):
                act.wait_ge(S["down_t"], n + 1)
                nc.scalar.activation(out_tok[:, :, n * P:(n + 1) * P], bank[n][:].rearrange("p (t d) -> p t d", t=TT),
                                     ACT.Copy).then_inc(S["sum_ready"], 1)

        @block.vector
        def _(dve):
            V = nc.vector
            count = {}

            def link(ins, s="dve_chain"):
                count[s] = count.get(s, 0) + 1
                ins.then_inc(S[s], 1)
                dve.wait_ge(S[s], count[s])

            def marked(ins):
                signal(ins, "dve_chain")
                return count["dve_chain"]

            def signal(ins, s):
                count[s] = count.get(s, 0) + 1
                ins.then_inc(S[s], 1)

            def rsqrt(y, v, t, s="dve_chain"):
                link(V.tensor_scalar(y.bitcast(I32), v.bitcast(I32), 1, None, ALU.logical_shift_right))
                link(V.tensor_scalar(y.bitcast(I32), y.bitcast(I32), -1.0, RSQRT_GUESS, ALU.mult, ALU.add))
                for n in range(3):
                    link(V.scalar_tensor_tensor(t, y, 1.0, y, ALU.mult, ALU.mult))
                    link(V.scalar_tensor_tensor(t, t, -0.5, v, ALU.mult, ALU.mult))
                    link(V.scalar_tensor_tensor(y, t, 1.5, y, ALU.add, ALU.mult), s if n == 2 else "dve_chain")

            def reduce_angle(r, k):
                link(V.tensor_scalar(k, r, 1 / (2 * math.pi), MAGIC, ALU.mult, ALU.add))
                link(V.tensor_scalar(k, k, -MAGIC, None, ALU.add))
                for part in TWO_PI:
                    link(V.scalar_tensor_tensor(r, k, -part, r, ALU.mult, ALU.add))
                pi = float(np.nextafter(np.float32(math.pi), np.float32(0)))
                link(V.tensor_scalar(r, r, pi, -pi, ALU.min, ALU.max))

            def cos_angle(out, r, s):
                link(V.scalar_tensor_tensor(out, r, -1.0, r, ALU.mult, ALU.min))
                link(V.tensor_scalar(out, out, math.pi / 2, None, ALU.add), s)

            def exp(y, x, k, k1, r):
                link(V.tensor_scalar(r, x, -174.0, 178.0, ALU.max, ALU.min))
                link(V.tensor_scalar(k, r, 1 / math.log(2.0), MAGIC, ALU.mult, ALU.add))
                link(V.tensor_scalar(k, k, -MAGIC, None, ALU.add))
                for part in LN2:
                    link(V.scalar_tensor_tensor(r, k, -part, r, ALU.mult, ALU.add))
                link(V.tensor_scalar(y, r, 1 / 5040, 1 / 720, ALU.mult, ALU.add))
                for i in (5, 4, 3, 2, 1, 0):
                    link(V.tensor_tensor(y, y, r, ALU.mult))
                    link(V.tensor_scalar(y, y, 1 / math.factorial(i), None, ALU.add))
                link(V.tensor_scalar(k1, k, 0.5, MAGIC, ALU.mult, ALU.add))
                link(V.tensor_scalar(k1, k1, -MAGIC, None, ALU.add))
                link(V.tensor_tensor(k, k, k1, ALU.subtract))
                for e in (k1, k):
                    link(V.tensor_scalar(r.bitcast(I32), e, 127.0, 8388608.0, ALU.add, ALU.mult))
                    link(V.tensor_tensor(y, y, r, ALU.mult))

            dve.wait_ge(S["rows_loaded"], 16 * 11)
            V.tensor_copy(vec_rows[32:32 + GP, 3, :].rearrange("g (q p) -> g q p", q=2),
                          dt_rows[32:32 + GP, :].unsqueeze(2).broadcast_to([GP, 2, 64])).then_inc(S["dt_spread"], 1)
            dve.wait_ge(S["tanh_c"], 1)
            link(V.scalar_tensor_tensor(silu_c, c_col[:, 2, :], 1.0, c_col[:, 0, :], ALU.add, ALU.mult))
            link(V.tensor_scalar(silu_c, silu_c, 0.5, None, ALU.mult), "silu_ready")
            dve.wait_ge(S["pos_loaded"], 16)
            dve.wait_ge(S["bc_loaded"], 48)
            link(V.tensor_copy(pos_f, pos_i))
            ang = rope[:, 3]
            for i in range(2):
                link(V.tensor_tensor(ang[:, :, HALF * i:HALF * (i + 1)], pos_f.unsqueeze(2).broadcast_to([P, TT, HALF]),
                                     inv_bc.unsqueeze(1).broadcast_to([P, TT, HALF]), ALU.mult))
            reduce_angle(ang, rope[:, 4])
            cos_angle(rope[:, 2], ang, "angle_ready")

            dve.wait_ge(S["ss_x_ready"], TT)
            link(V.tensor_scalar(ss_x, ss_x, 1 / D_MODEL, EPS, ALU.mult, ALU.add))
            rsqrt(rstd_x, ss_x, work[:, 0:4], "rstd_x_ready")

            dve.wait_ge(S["vec_t"], 1)
            link(V.tensor_copy(vec_cols[:], bank[4][:, 0:296]))
            dve.wait_ge(S["sin_ready"], 2)
            link(V.tensor_scalar(rope[:, 1, :, 0:HALF], rope[:, 1, :, 0:HALF], -1.0, None, ALU.mult))
            for i, g in ((2, gq_bc), (4, gk_bc)):
                link(V.tensor_tensor(rope[:, i], rope[:, 0], g.unsqueeze(1).broadcast_to([P, TT, HD]), ALU.mult))
                for a in range(2):
                    link(V.tensor_tensor(rope[:, i + 1, :, HALF * a:HALF * (a + 1)], rope[:, 1, :, HALF * a:HALF * (a + 1)],
                                         g[:, HALF * (1 - a):HALF * (2 - a)].unsqueeze(1).broadcast_to([P, TT, HALF]),
                                         ALU.mult))

            def ada(dst, src, s):
                link(V.tensor_scalar(dst, src[:, 0, :], silu_c[:, 0:1], None, ALU.mult))
                for k in range(1, KD):
                    ins = V.scalar_tensor_tensor(dst, src[:, k, :], silu_c[:, k:k + 1], dst, ALU.mult, ALU.add)
                    link(ins, s if k == KD - 1 else "dve_chain")

            def later_ada(first, last):
                for n in range(first, last):
                    dve.wait_ge(S[f"ada_next_loaded{n % 2}"], 16 * (n // 2 + 1))
                    if n < 2:
                        ada(ada_next_acc[:, n], ada_next[n], "ada_used")
                    elif n < 6:
                        ada(ada_late_acc[n - 2], ada_late[n % 2], "ada_used")
                    else:
                        ada(gate2_acc[n - 6], gate2_w[n - 6], "ada_used")

            for i in range(4):
                if i != 1:
                    dve.wait_ge(S[f"ada_first_loaded{i}"], 16)
                    ada(ada_first_acc[:, i], ada_first[:, i], "ada_acc_ready")
            dve.wait_ge(S["mod_ready"], 1)
            link(V.tensor_tensor(shift1, bank[5][:, 0:KD], vec_cols[:, C_BADA:C_BADA + KD], ALU.add))
            link(V.tensor_tensor(scale1, bank[5][:, KD:2 * KD], vec_cols[:, C_BADA + KD:C_BADA + 2 * KD], ALU.add))
            link(V.scalar_tensor_tensor(scale1, scale1, 1.0, vec_cols[:, C_NMIX:C_NMIX + KD], ALU.add, ALU.mult),
                 "mod1_ready")

            def split(k, s, ready, nth=None):
                n = k if nth is None else nth
                dve.wait_ge(S[s], n + 1)
                link(V.tensor_copy(act_hi[:, k, :], up32[:, n % 2, :]))
                signal(V.tensor_tensor(act_lo[:, k, :], up32[:, n % 2, :], act_hi[:, k, :].bitcast(F32), ALU.subtract),
                       ready)

            dve.wait_ge(S["zeros_stored"], 32)
            for k in range(KD):
                split(k, "x_t_read", "act_in_ready")

            later_ada(0, 1)
            lr, li, ldt = (vec_cols[:, a:a + GP] for a in (C_ARE, C_AIM, C_LDT))
            dt_, mag, th, cth, kk, k1, tc, ts, snt, cst = (s5_p[:, i] for i in range(10))
            ang_s, ang_c = s5_p[:, 6], s5_p[:, 7]
            sin_t, cos_t = s5_p[:, 8], s5_p[:, 9]
            lb_r, lb_i, cf_r, cf_i, den, n1, n2, ur, ui, r8, w1, w2, w3, w4 = (s5_p[:, i] for i in range(10, 24))
            exp(dt_, ldt, kk, k1, w1)
            link(V.tensor_tensor(w2, lr, dt_, ALU.mult))
            exp(mag, w2, kk, k1, w1)
            link(V.tensor_tensor(ang_s, li, dt_, ALU.mult))
            reduce_angle(ang_s, kk)
            cos_angle(ang_c, ang_s, "s5_angle")
            later_ada(1, 2)
            dve.wait_ge(S["s5_sin"], 1)
            link(V.tensor_tensor(lb_r, mag, cos_t, ALU.mult))
            link(V.tensor_tensor(lb_i, mag, sin_t, ALU.mult))
            link(V.tensor_tensor(den, lr, lr, ALU.mult))
            link(V.tensor_tensor(w1, li, li, ALU.mult))
            link(V.tensor_tensor(den, den, w1, ALU.add))
            link(V.reciprocal(den, den))
            link(V.tensor_scalar(n1, lb_r, -1.0, None, ALU.add))
            link(V.tensor_tensor(cf_r, n1, lr, ALU.mult))
            link(V.tensor_tensor(w1, lb_i, li, ALU.mult))
            link(V.tensor_tensor(cf_r, cf_r, w1, ALU.add))
            link(V.tensor_tensor(cf_r, cf_r, den, ALU.mult))
            link(V.tensor_tensor(cf_i, lb_i, lr, ALU.mult))
            link(V.tensor_tensor(w1, n1, li, ALU.mult))
            link(V.tensor_tensor(cf_i, cf_i, w1, ALU.subtract))
            link(V.tensor_tensor(cf_i, cf_i, den, ALU.mult))

            def cmul(o_r, o_i, a_r, a_i, b_r, b_i, t1, t2, s="dve_chain"):
                V.tensor_tensor(o_r, a_r, b_r, ALU.mult)
                V.tensor_tensor(t1, a_i, b_i, ALU.mult)
                V.tensor_tensor(o_i, a_r, b_i, ALU.mult)
                link(V.tensor_tensor(t2, a_i, b_r, ALU.mult))
                V.tensor_tensor(o_r, o_r, t1, ALU.subtract)
                link(V.tensor_tensor(o_i, o_i, t2, ALU.add), s)

            link(V.memset(power[:, 0, 0, :], 1.0))
            link(V.memset(power[:, 1, 0, :], 0.0))
            link(V.tensor_copy(power[:, 0, 1, :], lb_r))
            link(V.tensor_copy(power[:, 1, 1, :], lb_i))
            for n in range(2, CHUNK + 1):
                a, b = n // 2, n - n // 2
                cmul(power[:, 0, n, :], power[:, 1, n, :], power[:, 0, a, :], power[:, 1, a, :], power[:, 0, b, :],
                     power[:, 1, b, :], w1, w2)
            cmul(ur, ui, cos_t, sin_t, cos_t, sin_t, w1, w2)
            cmul(w3, w4, ur, ui, ur, ui, w1, w2)
            cmul(ur, ui, w3, w4, w3, w4, w1, w2)
            link(V.tensor_tensor(r8, mag, mag, ALU.mult))
            link(V.tensor_tensor(r8, r8, r8, ALU.mult))
            link(V.tensor_tensor(r8, r8, r8, ALU.mult))
            V.tensor_scalar(power_neg, power[:, 1, 1:, :], -1.0, None, ALU.mult)
            for j in range(CHUNK - 1):
                V.tensor_copy(power_back[:, :, j, :], power[:, :, CHUNK - 1 - j, :])
            link(V.tensor_copy(power_back[:, :, CHUNK - 1, :], power[:, :, 0, :]), "s5_params")

            def rotate(src, dst, tab, t, heads, s):
                cos, sin = rope[:, tab, t, :], rope[:, tab + 1, t, :]
                sh = src.rearrange("p (h d) -> p h d", h=heads)
                dh = dst.rearrange("p (h d) -> p h d", h=heads)
                th = tmp[:, 0:heads * HD].rearrange("p (h d) -> p h d", h=heads)
                V.tensor_tensor(dh, sh, cos.unsqueeze(1).broadcast_to([P, heads, HD]), ALU.mult)
                for a in range(2):
                    o = slice(HALF * a, HALF * (a + 1))
                    w = slice(HALF * (1 - a), HALF * (2 - a))
                    ins = V.tensor_tensor(th[:, :, o], sh[:, :, w],
                                          sin[:, o].unsqueeze(1).broadcast_to([P, heads, HALF]), ALU.mult)
                link(ins)
                link(V.tensor_tensor(dst, dst, tmp[:, 0:heads * HD], ALU.add), s)

            dve.wait_ge(S["tail_t_read"], 1)
            link(V.tensor_scalar(wi[:], ki_w[:, :, HD:TAIL], WI_SCALE, None, ALU.mult))
            for t in range(TT):
                rotate(ki_w[:, t, 0:HD], rot[:, 0, P * t:P * t + HD], 0, t, 1, "dve_chain")
            signal(V.tensor_copy(rot[:, 0, :].rearrange("p (t a d) -> p t a d", t=TT, a=2)[:, :, 1, :],
                                 rot[:, 0, :].rearrange("p (t a d) -> p t a d", t=TT, a=2)[:, :, 0, :]), "rot_ready")
            for t in range(TT):
                dve.wait_ge(S["proj_read"], t + 1)
                if t == 0:
                    dve.wait_ge(S["turned_ready"], 1)
                rotate(pre[:, t, :], rot[:, t, :], 0, t, HEADS, "rot_ready")
            dve.wait_ge(S["index_hi_ready"], 1)
            signal(V.tensor_tensor(ki_lo[:], bank[4][:], ki_hi[:].bitcast(F32), ALU.subtract), "turned_read")
            for t in range(TT):
                ts = slice(t * P, (t + 1) * P)
                dve.wait_ge(S["index_hi_ready"], t + 2)
                signal(V.tensor_tensor(qi_lo[:, :, ts], bank[4 + (t + 1) % 2][:].rearrange("p (g t) -> p g t", g=4),
                                       qi_hi[:, :, ts].bitcast(F32), ALU.subtract), "turned_read")
            dve.wait_ge(S["ada_sum_ready"], 2)
            link(V.tensor_tensor(gate1, bank[7][:, 0:KD], vec_cols[:, C_BADA + 2 * KD:C_BADA + 3 * KD], ALU.add),
                 "ada_sums_read")

            def scores(t):
                for h in range(HEADS):
                    i = (t - 1) * HEADS + h
                    dve.wait_ge(S["relu_ready"], i + 1)
                    if h == 0:
                        link(V.tensor_scalar(score[t], relu[:, i % 2, 0:KEYS[t]], wi[:, t, h:h + 1], None, ALU.mult),
                             "relu_used")
                    else:
                        link(V.scalar_tensor_tensor(score[t], relu[:, i % 2, 0:KEYS[t]], wi[:, t, h:h + 1], score[t],
                                                    ALU.mult, ALU.add), "relu_used")

            def top_k(tiles, first=0, last=TOPK // 8):
                dve.wait_ge(S["future_set"], tiles[-1])
                for _ in range(first, last):
                    after = [marked(V.max(top8[t % 2], score[t])) for t in tiles]
                    for n, t in enumerate(tiles):
                        dve.wait_ge(S["dve_chain"], after[n])
                        after[n] = marked(V.match_replace(score[t], top8[t % 2], score[t], TAKEN))
                    if len(tiles) == 1:
                        dve.wait_ge(S["dve_chain"], after[0])
                    else:
                        dve.wait_ge(S["dve_chain"], after[-1])
                if last == TOPK // 8:
                    for t in tiles:
                        link(V.tensor_scalar(bias[t], score[t], TAKEN, MASK, ALU.not_equal, ALU.mult))

            def head_sums(which):
                for t in range(TT):
                    n = 4 * which + t
                    dve.wait_ge(S["ss_qk_ready"], n + 1)
                    link(V.tensor_reduce(ss_qk[:, 32 * which + 8 * t:32 * which + 8 * t + 8],
                                         up32[:, n % 2, :].rearrange("p (h d) -> p h d", h=HEADS), AX, ALU.add), "sq_used")
                w = slice(32 * which, 32 * which + 32)
                link(V.tensor_scalar(ss_qk[:, w], ss_qk[:, w], 1 / HD, EPS, ALU.mult, ALU.add))
                rsqrt(rstd_qk[:, w], ss_qk[:, w], work[:, 0:32])

            def norm_rotate(which, t):
                dve.wait_ge(S["turned_ready"], 1 + 4 + (4 if which else 0))
                rotate(pre[:, t, :], rot[:, t, :], 2 if which else 4, t, HEADS, "rot_ready" if which else "dve_chain")
                if not which:
                    rs = rstd_qk[:, 8 * t:8 * t + 8].unsqueeze(2).broadcast_to([P, HEADS, HD])
                    r3 = rot[:, t, :].rearrange("p (h d) -> p h d", h=HEADS)
                    link(V.tensor_tensor(r3, r3, rs, ALU.mult), "rot_ready")

            for t in range(1, TT):
                scores(t)
            head_sums(0)
            for t in range(TT):
                norm_rotate(0, t)
            top_k((1,))
            head_sums(1)
            for t in range(TT):
                norm_rotate(1, t)
            link(V.tensor_scalar(q_scale, rstd_qk[:, 32:64], -ATT_SCALE, None, ALU.mult))

            def logits(i):
                t = i // HEADS
                dve.wait_ge(S["logit_mm"], i + 1)
                if i >= LOGITS:
                    dve.wait_ge(S["prob_ready"], i - LOGITS + 1)
                signal(V.tensor_tensor_reduce(out=logit[:, i % LOGITS, 0:KEYS[t]], in0=bank[i % 2][:, 0:KEYS[t]], in1=bias[t],
                                              scale=q_scale[:, i:i + 1], scalar=3.0e38, op0=ALU.add, op1=ALU.min,
                                              accum_out=neg_max[:, i:i + 1]), "logit_ready")

            def heads_out(t):
                dve.wait_ge(S["pv_done"], HEADS * (t + 1))
                w = slice(HEADS * t, HEADS * (t + 1))
                link(V.reciprocal(rinv[:, w], psum_p[:, w]))
                signal(V.tensor_tensor(y_attn[:, t, :].rearrange("p (h d) -> p h d", h=HEADS),
                                       bank[4 + t % 2][:].rearrange("p (h d) -> p h d", h=HEADS),
                                       rinv[:, w].unsqueeze(2).broadcast_to([P, HEADS, HD]), ALU.mult), "y_attn_ready")

            def by_channel(v, n=GP):
                return v.unsqueeze(2).broadcast_to([P, n, CH])
            dve.wait_ge(S["s5_loaded"], 32)
            t1, t2 = (cut(a, GP, CH) for a in (22952, 23208))
            cmul(s5_bb[:, 0], s5_bb[:, 1], s5_b[:, 0], s5_b[:, 1], by_channel(cf_r), by_channel(cf_i), t1, t2)

            dve.wait_ge(S["d_loaded"], 32)
            dve.wait_ge(S["ident_ready"], 1)
            mask = work[0:2 * CH, 0:CH]
            link(V.tensor_tensor(mask, ident[0:2 * CH, 0:CH], ident[0:2 * CH, CH:2 * CH], ALU.add))
            link(V.tensor_tensor(d_eye, d_eye, mask.unsqueeze(1).broadcast_to([2 * CH, GP, CH]), ALU.mult))
            link(V.memset(bb_diag, 0.0))
            for q in range(2):
                hp = slice(64 * q, 64 * q + 64)
                ins = V.tensor_copy(bb_diag[hp, :, :, CH * q:CH * q + CH], s5_bb[hp])
            signal(ins, "bb_ready")

            def add_d(half):
                for i in range(2):
                    dve.wait_ge(S["lags_ready"], 2 * half + i + 1)
                    g = 4 * i
                    signal(V.tensor_tensor(lags[half][:, g:g + 4, 0, :], lags[half][:, g:g + 4, 0, :],
                                           d_eye[:, GH * half + g:GH * half + g + 4, :], ALU.add), "lag_d_added")

            def scan(half, part):
                gs = slice(GH * half, GH * (half + 1))
                flat = lambda v: v.rearrange("p g c -> p (g c)")
                er, ei = flat(turn[:, 0, gs]), flat(turn[:, 1, gs])
                zr, zi = s5_z
                t1, t2 = s5_t[:, 0, :], s5_t[:, 1, :]
                if part == 0:
                    dve.wait_ge(S["turn_ready"], 1)
                    dve.wait_ge(S["state_mm"], half + 1)
                    sr, si = bank[6][:], bank[7][:]
                    V.tensor_tensor(zr, sr, er, ALU.mult)
                    V.tensor_tensor(t1, si, ei, ALU.mult)
                    V.tensor_tensor(zi, si, er, ALU.mult)
                    link(V.tensor_tensor(t2, sr, ei, ALU.mult), "state_read")
                    V.tensor_tensor(zr, zr, t1, ALU.add)
                    link(V.tensor_tensor(zi, zi, t2, ALU.subtract))
                    return
                if part == 1:
                    link(V.tensor_copy(scan_r, r8[:, gs].unsqueeze(2).broadcast_to([P, GH, NCH])))
                    link(V.memset(scan_r[:, :, 0:1], 0.0))
                    fr = flat(scan_r)
                    V.tensor_tensor_scan(t1, fr, zr, 0.0, ALU.mult, ALU.add)
                    link(V.tensor_tensor_scan(t2, fr, zi, 0.0, ALU.mult, ALU.add))
                    return
                a, b = (v.rearrange("p (g c) -> p g c", g=GH)[:, :, 0:NCH - 1] for v in (t1, t2))
                e1, e2 = turn[:, 0, gs, 0:NCH - 1], turn[:, 1, gs, 0:NCH - 1]
                z1, z2 = (v.rearrange("p (g c) -> p g c", g=GH)[:, :, 0:NCH - 1] for v in (zr, zi))
                V.tensor_tensor(z1, b, e2, ALU.mult)
                link(V.tensor_tensor(z2, b, e1, ALU.mult))
                link(V.tensor_tensor(b, a, e2, ALU.mult))
                link(V.tensor_tensor(a, a, e1, ALU.mult))
                for q in range(2):
                    hp = slice(64 * q, 64 * q + 64)
                    V.tensor_tensor(s5_x[hp, 0, :, q, 1:NCH], a[hp], z1[hp], ALU.subtract)
                    ins = V.tensor_tensor(s5_x[hp, 1, :, q, 1:NCH], b[hp], z2[hp], ALU.add)
                link(ins, "s5_state")

            for i in range(ATT_UNITS + 1):
                if i < ATT_UNITS:
                    logits(i)
                if i >= 1:
                    if i % HEADS == 0 and i // HEADS >= 2:
                        heads_out(i // HEADS - 2)
                if i == 1:
                    dve.wait_ge(S["weights_used"], U_V + 2)
                    source_of_v(V, link, 0, s5_mem[:, 7168:8192])
                    link(V.memset(s5_mem[:, 5120:7168], 0.0))
                if i < TOPK // 8:
                    top_k((2, 3), i, i + 1)
                for back in (1, 2, 3):
                    stage, half, part = S5_AT.get(i - back, ("none", 0, 0))
                    if stage == "lags" and back == 1:
                        add_d(half)
                    elif stage == "states":
                        scan(half, back - 1)
            heads_out(TT - 1)

            for k in range(4):
                dve.wait_ge(S["g_t_read"], k + 1)
                link(V.tensor_copy(act_hi[:, k, :], up32[:, k % 2, :]))
                signal(V.tensor_tensor(act_lo[:, k, :], up32[:, k % 2, :], act_hi[:, k, :].bitcast(F32), ALU.subtract),
                       "glu_in")
            def norm_y(w, y, scale):
                ws = slice(4 * w, 4 * w + 4)
                link(V.tensor_scalar(ss_y[:, ws], ss_y[:, ws], scale * scale / 512, EPS, ALU.mult, ALU.add))
                rsqrt(rstd_y[:, ws], ss_y[:, ws], work[:, 0:4])
                if scale != 1:
                    link(V.tensor_scalar(rstd_y[:, ws], rstd_y[:, ws], scale, None, ALU.mult))
                for t in range(TT):
                    signal(V.tensor_scalar(y[:, t, :], y[:, t, :], rstd_y[:, 4 * w + t:4 * w + t + 1], None, ALU.mult),
                           "yn_ready")

            dve.wait_ge(S["ss_y_ready"], TT)
            norm_y(1, y_attn, 1)
            later_ada(2, 3)
            for t in range(TT):
                if t == 2:
                    later_ada(3, 4)
                dve.wait_ge(S["tanh_z"], t + 1)
                signal(V.scalar_tensor_tensor(y_ssm[:, t, :], up32[:, t % 2, :], 1.0, y_ssm[:, t, :], ALU.add, ALU.mult),
                       "glu_read")
            dve.wait_ge(S["ss_y_ready"], 2 * TT)
            norm_y(0, y_ssm, 0.5)
            dve.wait_ge(S["weights_used"], U_GLU + 1)
            for n, k in enumerate(MIX_ORDER):
                split(k, "mix_t_read", "mix_in", n)
            later_ada(4, 6)
            for m in range(KD):
                if m % 2 == 0:
                    dve.wait_ge(S["out_mm"], m // 2 + 1)
                else:
                    dve.wait_ge(S["weights_used"], U_OUT + m // 2 + 1)
                signal(V.scalar_tensor_tensor(h_t[:, m], bank[(m + 4) % 8][:], gate1[:, m:m + 1], h_t[:, m],
                                              ALU.mult, ALU.add), "h_ready")
                if m == 5:
                    dve.wait_ge(S["ada_sum_ready"], 3)
                    sums = bank[5][:, 0:2 * KD].rearrange("p (v k) -> p v k", v=2)
                    b = vec_cols[:, C_BADA + 3 * KD:C_BADA + 5 * KD].rearrange("p (v k) -> p v k", v=2)
                    link(V.tensor_tensor(mod_cols[:, 3:5, :], sums, b, ALU.add))
                    link(V.scalar_tensor_tensor(scale2, scale2, 1.0, vec_cols[:, C_NFFN:C_NFFN + KD], ALU.add, ALU.mult))
            dve.wait_ge(S["ss_h_mm"], 1)
            link(V.tensor_scalar(ss_h, bank[4][:, 0:TT], 1 / D_MODEL, EPS, ALU.mult, ALU.add))
            rsqrt(rstd_h, ss_h, work[:, 64:68])
            for t in range(TT):
                ins = V.tensor_scalar(rstd_diag[:, t], ident[:], rstd_h[:, t:t + 1], None, ALU.mult)
            signal(ins, "rstd_diag_ready")
            dve.wait_ge(S["rstd_spread"], 1)
            for k in range(KD):
                if k == 0:
                    signal(V.scalar_tensor_tensor(up32[:, 0], h_t[:, 0], scale2[:, 0:1], bank[6][:], ALU.mult, ALU.mult),
                           "hn_ready")
                if k + 1 < KD:
                    if k >= 1:
                        dve.wait_ge(S["mlp_in"], k)
                    signal(V.scalar_tensor_tensor(up32[:, (k + 1) % 2], h_t[:, k + 1], scale2[:, k + 1:k + 2], bank[6][:],
                                                  ALU.mult, ALU.mult), "hn_ready")
                dve.wait_ge(S["hn_hi_ready"], k + 1)
                signal(V.scalar_tensor_tensor(act_lo[:, k, :], up32[:, k % 2], shift2[:, k:k + 1],
                                              act_hi[:, k, :].bitcast(F32), ALU.add, ALU.subtract), "mlp_in")

            later_ada(6, 8)

            with dve.Fori(0, UPS) as j:
                for q in range(4):
                    f = (0, 1, FT, FT + 1)[q]
                    dve.wait_ge(S["tap_ready"], j * 4 + (q + 1))
                    V.scalar_tensor_tensor(conv[:, q, 1:], bank[q][:, 0:SEQ - 1],
                                           vec_cols[:, bass.ds(j * 2 + (C_W1 + f), 1)], conv[:, q, 1:],
                                           ALU.mult, ALU.add).then_inc(S["conv_read"], 1)
                    dve.wait_ge(S["conv_read"], j * 4 + (q + 1))
                    V.scalar_tensor_tensor(conv[:, q, 2:], bank[q][:, 0:SEQ - 2],
                                           vec_cols[:, bass.ds(j * 2 + (C_W0 + f), 1)], conv[:, q, 2:],
                                           ALU.mult, ALU.add).then_inc(S["conv_ready"], 1)
                for q in range(2):
                    dve.wait_ge(S["gelu_up"], j * 2 + (q + 1))
                    dve.wait_ge(S["conv_ready"], j * 4 + 4)
                    V.tensor_tensor(up32[:, q, :], conv[:, q, :], conv[:, 2 + q, :], ALU.mult
                                    ).then_inc(S["ff32_ready"], 1)
                for q in range(2):
                    dve.wait_ge(S["ff_hi_ready"], j * 2 + (q + 1))
                    V.tensor_tensor(ff_lo[:, bass.ds(j * 2 + q, 1), :].rearrange("p a t -> p (a t)"), up32[:, q, :],
                                    ff_hi[:, bass.ds(j * 2 + q, 1), :].rearrange("p a t -> p (a t)").bitcast(F32),
                                    ALU.subtract).then_inc(S["ff_lo_ready"], 1)
            dve.wait_ge(S["ada_sum_ready"], 4)
            link(V.tensor_tensor(gate2, bank[7][:, 0:KD], vec_cols[:, C_BADA + 5 * KD:C_BADA + 6 * KD], ALU.add),
                 "gate2_ready")
            for n in range(KD):
                dve.wait_ge(S["down_mm"], n + 1)
                signal(V.scalar_tensor_tensor(h_t[:, n], bank[n][:], gate2[:, n:n + 1], h_t[:, n], ALU.mult, ALU.add),
                       "down_scaled")

        @block.tensor
        def _(pe):
            T = nc.tensor

            def mm3(dst, lhs_hi, lhs_lo, rhs_hi, rhs_lo, start, stop):
                T.matmul(dst, lhs_hi, rhs_hi, start=start, stop=False)
                T.matmul(dst, lhs_hi, rhs_lo, start=False, stop=False)
                return T.matmul(dst, lhs_lo, rhs_hi, start=False, stop=stop)

            def flip(dst, src, n=P, at=0):
                return T.matmul(dst, src, ident[at:at + n, at:at + n], is_transpose=True, start=True, stop=True)

            def over_partitions(dst, acc):
                for i in range(4):
                    ins = T.matmul(dst[:, i:i + 1], acc[:, i * P:(i + 1) * P], ones[:, 0:1], start=True, stop=True)
                return ins

            pe.wait_ge(S["ident_ready"], 1)
            pe.wait_ge(S["rows_loaded"], 16 * 11)
            pe.wait_ge(S["dt_spread"], 1)
            at = 0
            for i, n in enumerate((72, 88, 88, 48)):
                ins = flip(bank[4][:, at:at + n], vec_rows[0:n, i, :], n)
                at += n
            ins.then_inc(S["vec_t"], 1)
            pe.wait_ge(S["xn_ready"], TT)
            for k in range(KD):
                if k >= 4:
                    pe.wait_ge(S["x_t_read"], k - 3)
                for t in range(TT):
                    ins = flip(bank[k % 4][:, t * P:(t + 1) * P], xh[:, t, k * P:(k + 1) * P])
                ins.then_inc(S["x_t_ready"], 1)
                if k == 3:
                    pe.wait_ge(S["ones_ready"], 1)
                    for i in range(4):
                        if i == 1:
                            pe.wait_ge(S["ada_acc_pool"], 1)
                        else:
                            pe.wait_ge(S["ada_acc_ready"], max(i, 1))
                        ins = over_partitions(bank[5][:, 4 * i:4 * i + 4], ada_first_acc[:, i])
                    ins.then_inc(S["mod_ready"], 1)

            def tail():
                n = U_TAIL
                pe.wait_ge(S["lo_ready"], n + 1)
                pe.wait_ge(S["x_t_read"], KD)
                wh, wl = unit_view(w_hi, n, KD, TAIL), unit_view(w_lo, n, KD, TAIL)
                for k in range(KD):
                    pe.wait_ge(S["act_in_ready"], k + 1)
                    ins = mm3(bank[6][0:TAIL, :], wh[:, k, :], wl[:, k, :], act_hi[:, k, :], act_lo[:, k, :],
                              k == 0, k == KD - 1)
                ins.then_inc(S["weights_used"], 1)

            def turn_tail():
                pe.wait_ge(S["tail_read"], 1)
                pe.wait_ge(S["mod1_ready"], 1)
                for t in range(TT):
                    ins = flip(bank[5][:, t * TAIL:(t + 1) * TAIL], tail_t[:, t * P:(t + 1) * P], TAIL)
                ins.then_inc(S["tail_t"], 1)

            def later_ada(n):
                pe.wait_ge(S["ada_used"], n + 1)
                over_partitions(bank[7][:, 4 * n:4 * n + 4], ada_next_acc[:, n]).then_inc(S["ada_sum_ready"], 1)

            def project(n0, nth, banks=0, out_sem="proj_ready", free=None, between={}):
                for kh in range(2):
                    n = n0 + kh
                    pe.wait_ge(S["lo_ready"], n + 1)
                    wh, wl = unit_view(w_hi, n, 4, 512), unit_view(w_lo, n, 4, 512)
                    for t in range(TT):
                        ts = slice(t * P, (t + 1) * P)
                        if kh == 0 and free is not None:
                            pe.wait_ge(S[free], 4 * (nth - 1) + t + 1)
                        for i in range(4):
                            k = 4 * kh + i
                            ins = mm3(bank[banks + t][:], act_hi[:, k, ts], act_lo[:, k, ts], wh[:, i, :], wl[:, i, :],
                                      k == 0, k == KD - 1)
                        if t == TT - 1:
                            ins.then_inc(S["weights_used"], 1)
                        elif kh == 1:
                            ins.then_inc(S[out_sem], 1)
                        if (kh, t) in between:
                            between[kh, t]()

            turned = [0]

            def turn_head(t, rot_before):
                pe.wait_ge(S["rot_ready"], rot_before + t + 1)
                pe.wait_ge(S["turned_read"], max(turned[0] - 1, 1))
                for g in range(4):
                    ins = flip(bank[4 + turned[0] % 2][:, g * P:(g + 1) * P], rot[:, t, g * P:(g + 1) * P])
                ins.then_inc(S["turned_ready"], 1)
                turned[0] += 1

            def turn_heads(rot_before):
                for t in range(TT):
                    turn_head(t, rot_before)

            tail()
            project(U_QI, 0, between={(0, 0): turn_tail, (0, 3): lambda: later_ada(0), (1, 3): lambda: later_ada(1)})
            project(U_U, 1, free="proj_read")

            def turn_keys():
                pe.wait_ge(S["rot_ready"], 1)
                pe.wait_ge(S["mod1_ready"], 1)
                for t in range(TT):
                    ins = flip(bank[4][:, t * P:(t + 1) * P], rot[:, 0, t * P:(t + 1) * P])
                ins.then_inc(S["turned_ready"], 1)
                turned[0] = 1

            def turn_c():
                pe.wait_ge(S["c_rows_loaded"], 64)
                pe.wait_ge(S["tail_t_read"], 1)
                for r in range(2):
                    for a in range(4):
                        ins = flip(bank[5 + r][:, P * a:P * (a + 1)], c_rows[:, r, a].rearrange("p q n -> p (q n)"))
                ins.then_inc(S["c_t"], 1)

            def turn_first_queries():
                pe.wait_ge(S["c_t_read"], 4)
                turn_head(0, 1)

            project(U_K, 2, free="proj_read", between={
                (0, 0): turn_keys, (0, 1): turn_c, (0, 3): turn_first_queries, (1, 0): lambda: turn_head(1, 1),
                (1, 1): lambda: turn_head(2, 1), (1, 2): lambda: turn_head(3, 1)})
            pe.wait_ge(S["turned_read"], 5)
            pe.wait_ge(S["ada_sums_read"], 1)
            for i in range((TT - 1) * HEADS):
                t, h = 1 + i // HEADS, i % HEADS
                if i >= 2:
                    pe.wait_ge(S["relu_ready"], i - 1)
                hp = slice(64 * (h % 2), 64 * (h % 2) + 64)
                ts, ks = slice(t * P, (t + 1) * P), slice(0, KEYS[t])
                mm3(bank[6 + i % 2][:, ks], qi_hi[hp, h // 2, ts], qi_lo[hp, h // 2, ts], ki_hi[hp, ks], ki_lo[hp, ks],
                    True, True).then_inc(S["score_mm"], 1)

            project(U_Q, 3, free="proj_read")
            project(U_V, 4, free="proj_read", between={
                (0, 2): lambda: turn_head(0, 5), (0, 3): lambda: turn_head(1, 5), (1, 0): lambda: turn_head(2, 5),
                (1, 1): lambda: turn_head(3, 5)})
            turn_heads(9)
            pe.wait_ge(S["proj_read"], 20)
            pe.wait_ge(S["turned_read"], 13)

            def logits(i):
                t, h = i // HEADS, i % HEADS
                hp = slice(64 * (h % 2), 64 * (h % 2) + 64)
                if i >= 2:
                    pe.wait_ge(S["logit_ready"], i - 1)
                T.matmul(bank[i % 2][:, 0:KEYS[t]], q_t[hp, h // 2, t * P:(t + 1) * P], k_t[hp, h // 2, 0:KEYS[t]],
                         start=True, stop=True).then_inc(S["logit_mm"], 1)

            def turn_probs(i):
                t = i // HEADS
                pe.wait_ge(S["prob_ready"], i + 1)
                if i >= 2:
                    pe.wait_ge(S["prob_t_ready"], i - 1)
                for s in range(t + 1):
                    ins = flip(bank[2 + i % 2][:, s * P:(s + 1) * P], prob[:, i % 2, s * P:(s + 1) * P])
                ins.then_inc(S["prob_turned"], 1)

            def values(i):
                t, h = i // HEADS, i % HEADS
                pe.wait_ge(S["prob_t_ready"], i + 1)
                if h == 0 and t >= 2:
                    pe.wait_ge(S["y_attn_ready"], t - 1)
                for s in range(t + 1):
                    ins = T.matmul(bank[4 + t % 2][:, h * HD:(h + 1) * HD], prob_t[:, i % 2, s * P:(s + 1) * P],
                                   v_tok[:, s, h * HD:(h + 1) * HD], start=(s == 0), stop=(s == t))
                ins.then_inc(S["pv_done"], 1)

            def s5(stage, half, part):
                b0 = 4 * half
                if stage == "x":
                    pe.wait_ge(S["x_again"], 16 * TT)
                    if half:
                        pe.wait_ge(S["x_turned_read"], 2 * half)
                    else:
                        pe.wait_ge(S["y_read"], 4)
                    for k in (2 * half, 2 * half + 1):
                        for t in range(TT):
                            ins = flip(bank[6 + k % 2][:, t * P:(t + 1) * P], x_tok[:, t, k * P:(k + 1) * P])
                        ins.then_inc(S["x_turned"], 1)
                    return
                if stage == "V":
                    if part:
                        pe.wait_ge(S["v_ready"], b0 + 2)
                    else:
                        pe.wait_ge(S["vt_ready"], half + 1)
                        if half:
                            pe.wait_ge(S["y_read"], 2)
                    for g in range(4 * part, 4 * part + 4):
                        for r in range(2):
                            ins = flip(bank[6 + g % 4 // 2][:, ((g % 2) * 2 + r) * P:((g % 2) * 2 + r + 1) * P],
                                       s5_vt[half][:, r, g].rearrange("p j h -> p (j h)"))
                        if g % 2:
                            ins.then_inc(S["v_t"], 1)
                elif stage == "u":
                    pe.wait_ge(S["u_grouped"], 2)
                    pe.wait_ge(S["v_ready"], b0 + 4)
                    for g in range(NG):
                        ins = flip(bank[6 + g // 8][:, (g % 8) * NCH:(g % 8 + 1) * NCH], group_in[:, NG * half + g, :],
                                   NCH, NCH)
                        if g % 8 == 7:
                            ins.then_inc(S["u_t"], 1)
                elif stage == "states":
                    pe.wait_ge(S["u_t_read"], 2 * half + 2)
                    for g in range(NG):
                        hp = slice(64 * (g % 2), 64 * (g % 2) + 64)
                        for r in range(2):
                            ins = T.matmul(bank[6 + r][hp, (g // 2) * NCH:(g // 2 + 1) * NCH],
                                           s5_v[half][:, g // 2, r, hp], s5_u[:, g, :], start=True, stop=True)
                    ins.then_inc(S["state_mm"], 1)
                elif stage == "lags":
                    pe.wait_ge(S["lag_w_ready"], half + 1)
                    pe.wait_ge(S["bb_ready"], 1)
                    pe.wait_ge(S["state_read"], half + 1)
                    for g in range(GH):
                        for r in range(2):
                            ins = T.matmul(bank[6 + g // 4][0:2 * CH, (g % 4) * P:(g % 4 + 1) * P],
                                           bb_diag[:, r, GH * half + g, :],
                                           lag_w[half][:, r, g, 0:CHUNK, :].rearrange("p l h -> p (l h)"),
                                           start=(r == 0), stop=(r == 1))
                        if g % 4 == 3:
                            ins.then_inc(S["lag_mm"], 1)
                else:
                    pe.wait_ge(S["lags_ready"], 2 * half + 2)
                    pe.wait_ge(S["m_loaded"], 16 * CHUNK * (half + 1))
                    pe.wait_ge(S["s5_state"], half + 1)
                    for g in range(GH):
                        o = bank[6 + g // 4][:, (g % 4) * P:(g % 4 + 1) * P]
                        for q in range(2):
                            T.matmul(o[NCH * q:NCH * (q + 1)], s5_u[:, 2 * g + q, :], s5_m[half][:, 2 * g + q, :],
                                     start=True, stop=False)
                        for r in range(2):
                            ins = T.matmul(o, s5_x[:, r, g].rearrange("p q c -> p (q c)"),
                                           lag_w[half][:, r, g, 1:, :].rearrange("p l h -> p (l h)"),
                                           start=False, stop=(r == 1))
                        if g % 4 == 3:
                            ins.then_inc(S["y_mm"], 1)

            for i in range(ATT_UNITS + 2):
                if i < ATT_UNITS:
                    logits(i)
                if 1 <= i <= ATT_UNITS:
                    turn_probs(i - 1)
                if i >= 2:
                    values(i - 2)
                if i in S5_AT:
                    s5(*S5_AT[i])
            pe.wait_ge(S["prob_t_ready"], ATT_UNITS)
            pe.wait_ge(S["y_attn_ready"], TT)

            pe.wait_ge(S["gelu_ready"], TT)
            for k in range(4):
                for t in range(TT):
                    ins = flip(bank[k][:, t * P:(t + 1) * P], y_ssm[:, t, k * P:(k + 1) * P])
                ins.then_inc(S["g_t"], 1)
            pe.wait_ge(S["lo_ready"], U_GLU + 1)
            pe.wait_ge(S["glu_in"], 4)
            pe.wait_ge(S["x_turned_read"], KD)
            pe.wait_ge(S["b_rows_loaded"], 16)
            wh, wl = unit_view(w_hi, U_GLU, 4, 512), unit_view(w_lo, U_GLU, 4, 512)
            for t in range(TT):
                ts = slice(t * P, (t + 1) * P)
                T.matmul(bank[4 + t][:], ones[0:1, :], b_glu_row, start=True, stop=False)
                for k in range(4):
                    ins = mm3(bank[4 + t][:], act_hi[:, k, ts], act_lo[:, k, ts], wh[:, k, :], wl[:, k, :],
                              False, k == 3)
                ins.then_inc(S["glu_mm" if t < TT - 1 else "weights_used"], 1)

            for n, k in enumerate(MIX_ORDER):
                pe.wait_ge(S["yn_ready"], 4 * (n // 4) + 4)
                if n >= 4:
                    pe.wait_ge(S["mix_t_read"], n - 3)
                y = y_ssm if k < 4 else y_attn
                for t in range(TT):
                    ins = flip(bank[n % 4][:, t * P:(t + 1) * P], y[:, t, (k % 4) * P:(k % 4 + 1) * P])
                ins.then_inc(S["mix_t"], 1)
            pe.wait_ge(S["tanh_z"], TT)
            for m in range(KD):
                if m % 2 == 0:
                    n = U_OUT + m // 2
                    pe.wait_ge(S["lo_ready"], n + 1)
                    wh, wl = unit_view(w_hi, n, KD, 256), unit_view(w_lo, n, KD, 256)
                ms = slice((m % 2) * P, (m % 2 + 1) * P)
                for i, k in enumerate(MIX_ORDER):
                    if m == 0:
                        pe.wait_ge(S["mix_in"], i + 1)
                    ins = mm3(bank[(m + 4) % 8][:], wh[:, k, ms], wl[:, k, ms], act_hi[:, k, :], act_lo[:, k, :],
                              i == 0, i == KD - 1)
                ins.then_inc(S["weights_used" if m % 2 else "out_mm"], 1)
                if m == 5:
                    pe.wait_ge(S["ada_used"], 6)
                    pe.wait_ge(S["h_ready"], 2)
                    for i in range(4):
                        ins = over_partitions(bank[5][:, 4 * i:4 * i + 4], ada_late_acc[i])
                    ins.then_inc(S["ada_sum_ready"], 1)
            pe.wait_ge(S["h_ready"], 1)
            pe.wait_ge(S["sq_summed"], 1)
            pe.wait_ge(S["ss_h_ready"], KD)
            for t in range(TT):
                ts = slice(t * P, (t + 1) * P)
                for i, q in enumerate((h_sq_sum, h_sq[:, KD - 2], h_sq[:, KD - 1])):
                    ins = T.matmul(bank[4][:, t:t + 1], q[:, ts], ones[:, 0:1], start=(i == 0), stop=(i == 2))
            ins.then_inc(S["ss_h_mm"], 1)
            pe.wait_ge(S["rstd_diag_ready"], 1)
            for t in range(TT):
                ins = T.matmul(bank[6][:, t * P:(t + 1) * P], ones[:], rstd_diag[:, t], start=True, stop=True)
            ins.then_inc(S["rstd_spread"], 1)

            def up(j, first):
                for kh in range(2):
                    pe.wait_ge(S["lo_ready"], j * 2 + (U_UP + kh + 1))
                    wh, wl = unit_view(w_hi, U_UP + kh, 4, 512), unit_view(w_lo, U_UP + kh, 4, 512)
                    def product(q, i):
                        k = 4 * kh + i
                        qs = slice(q * P, (q + 1) * P)
                        return mm3(bank[q][:], wh[:, i, qs], wl[:, i, qs], act_hi[:, k, :], act_lo[:, k, :],
                                   k == 0, k == KD - 1)

                    if first:
                        for i in range(4 - kh):
                            pe.wait_ge(S["mlp_in"], 4 * kh + i + 1)
                            for q in range(4):
                                ins = product(q, i)
                        if kh == 0:
                            ins.then_inc(S["weights_used"], 1)
                            continue
                        pe.wait_ge(S["mlp_in"], KD)
                    for q in range(4):
                        if kh == 0:
                            pe.wait_ge(S["conv_ready"], j * 4 + (q - 3))
                        for i in (3,) if first else range(4):
                            ins = product(q, i)
                        if q == 3:
                            ins.then_inc(S["weights_used"], 1)
                        elif kh == 1:
                            ins.then_inc(S["up_mm"], 1)

            up(0, True)
            pe.wait_ge(S["ada_used"], 8)
            for i in range(2):
                ins = over_partitions(bank[7][:, 4 * i:4 * i + 4], gate2_acc[i])
            ins.then_inc(S["ada_sum_ready"], 1)
            with pe.Fori(1, UPS) as j:
                up(j, False)

            def down(slot, k0, first, last, dyn):
                wh = w_hi[:, slot, :].rearrange("p (k n) -> p k n", k=2)
                wl = w_lo[:, slot, :].rearrange("p (k n) -> p k n", k=2)
                for i in range(2):
                    if dyn:
                        fh = ff_hi[:, bass.ds(k0 + i, 1), :].rearrange("p a t -> p (a t)")
                        fl = ff_lo[:, bass.ds(k0 + i, 1), :].rearrange("p a t -> p (a t)")
                    else:
                        fh, fl = ff_hi[:, k0 + i, :], ff_lo[:, k0 + i, :]
                    for n in (4, 5, 6, 0, 1, 2, 3, 7) if first else range(KD):
                        if first and i == 0 and n == 7:
                            pe.wait_ge(S["gate2_ready"], 1)
                        if first and i == 0 and n == 0:
                            pe.wait_ge(S["conv_ready"], 4 * UPS)
                        ns = slice(n * P, (n + 1) * P)
                        ins = mm3(bank[n][:], wh[:, i, ns], wl[:, i, ns], fh, fl, first and i == 0, last and i == 1)
                        if last and i == 1:
                            ins.then_inc(S["down_mm"], 1)
                if not last:
                    ins.then_inc(S["weights_used"], 1)

            pe.wait_ge(S["ff_lo_ready"], 2)
            pe.wait_ge(S["lo_ready"], U_DOWN + 1)
            down(U_DOWN % 2, 0, True, False, False)
            pe.wait_ge(S["ff_lo_ready"], FT)
            with pe.Fori(0, FT // 2 - 3, 2) as j:
                for i in range(2):
                    pe.wait_ge(S["lo_ready"], j + (U_DOWN + 2 + i))
                    down((U_DOWN + 1 + i) % 2, j * 2 + (2 + 2 * i), False, False, True)
            pe.wait_ge(S["lo_ready"], UNITS - 1)
            down((UNITS - 2) % 2, FT - 4, False, False, False)
            pe.wait_ge(S["lo_ready"], UNITS)
            down((UNITS - 1) % 2, FT - 2, False, True, False)
            for n in range(KD):
                pe.wait_ge(S["down_scaled"], n + 1)
                for t in range(TT):
                    ins = flip(bank[n][:, t * P:(t + 1) * P], h_t[:, n, t * P:(t + 1) * P])
                ins.then_inc(S["down_t"], 1)


INPUTS = ["x", "c", "positions", "w_ada", "b_ada", "norm_mix", "w_in", "ssm_log_dt", "ssm_a_re", "ssm_a_im",
          "ssm_b_re", "ssm_b_im", "ssm_c_re", "ssm_c_im", "ssm_d", "ssm_w_glu", "ssm_b_glu", "q_norm", "k_norm",
          "out_norm_ssm", "out_norm_attn", "w_out", "norm_ffn", "w_up", "conv_w", "conv_b", "w_down"]


def kernel(**inputs):
    import concourse.bacc as bacc
    from concourse.bass_utils import run_bass_kernel_spmd

    nc = bacc.Bacc("TRN2", target_bir_lowering=False, num_devices=1)
    arrays, args = {}, []
    given = [(n, inputs[n]) for n in INPUTS]
    given.append(("inv_freq", (10000.0 ** (-np.arange(0, HD, 2, dtype=np.float64) / HD)).astype(np.float32)[None]))
    for name, a in given:
        a = np.ascontiguousarray(a)
        arrays[f"in_{name}"] = a
        args.append(nc.dram_tensor(f"in_{name}", a.shape, mybir.dt.from_np(a.dtype), kind="ExternalInput").ap())
    out = nc.dram_tensor("out", (1, SEQ, D_MODEL), F32, kind="ExternalOutput").ap()
    layer(nc, *args, out)
    result = run_bass_kernel_spmd(nc, [arrays], core_ids=[0])
    return result.results[0]["out"]
```
